# Optimizing a Trainium2 kernel written in Bass

```python
import jax, jax.numpy as jnp
from jax import lax
import numpy as np

D_MODEL = 2048
BATCH = 1
SEQ = 512
DEPTH = 1

N_META = 16
RMS_EPS = 1e-6
HEAD_DIM = 128
ATT_Q_HEADS = 8
ATT_KV_HEADS = 2
ATT_GROUP = ATT_Q_HEADS // ATT_KV_HEADS
WINDOW = 128
ATT_BLOCK = 128
ROPE_THETA = 500000.0
ROPE_DIM = HEAD_DIM // 4
HGRN_HEADS = 8
HGRN_DK = 128
HGRN_DV = 128
HGRN_CHUNK = 64
ATT_WIDTH = ATT_Q_HEADS * HEAD_DIM
HGRN_WIDTH = HGRN_HEADS * HGRN_DV
MIX_WIDTH = ATT_WIDTH + HGRN_WIDTH
Q_COLS = ATT_Q_HEADS * HEAD_DIM
KV_COLS = ATT_KV_HEADS * HEAD_DIM
HK = HGRN_HEADS * HGRN_DK
HV = HGRN_HEADS * HGRN_DV
IN_SPLITS = [Q_COLS, KV_COLS, KV_COLS, HK, HK, HV, HV]
IN_COLS = sum(IN_SPLITS)
PEER_HEADS = 8
PEER_NKEYS = 128
PEER_N = PEER_NKEYS * PEER_NKEYS
PEER_DKEY = 256
PEER_DHALF = PEER_DKEY // 2
PEER_TOPK = 16
PEER_TOKEN_BLOCK = 128

kernel_name = "hymba_swa_sink_hgrn2_peer_block"

def rms_norm(x, g):
    xf = x.astype(jnp.float32)
    y = xf * lax.rsqrt(jnp.mean(xf * xf, axis=-1, keepdims=True) + RMS_EPS)
    return (y * g.astype(jnp.float32)).astype(x.dtype)

def partial_rope(x, pos):
    half = ROPE_DIM // 2
    inv = ROPE_THETA ** (-jnp.arange(0, ROPE_DIM, 2, dtype=jnp.float32) / ROPE_DIM)
    ang = pos.astype(jnp.float32)[:, None] * inv[None, :]
    cos = jnp.cos(ang)[None, :, None, :]
    sin = jnp.sin(ang)[None, :, None, :]
    xr = x[..., :ROPE_DIM].astype(jnp.float32)
    x1, x2 = xr[..., :half], xr[..., half:]
    rot = jnp.concatenate([x1 * cos - x2 * sin, x2 * cos + x1 * sin], axis=-1)
    return jnp.concatenate([rot.astype(x.dtype), x[..., ROPE_DIM:]], axis=-1)

def sliding_window_sink_attention(q, k, v, sinks):
    B, L = q.shape[0], q.shape[1]
    pad = ATT_BLOCK - N_META
    Lp = L + pad
    nb = Lp // ATT_BLOCK
    padw = ((0, 0), (pad, 0), (0, 0), (0, 0))
    qb = jnp.pad(q, padw).reshape(B, nb, ATT_BLOCK, ATT_KV_HEADS, ATT_GROUP, HEAD_DIM)
    kb = jnp.pad(k, padw).reshape(B, nb, ATT_BLOCK, ATT_KV_HEADS, HEAD_DIM)
    vb = jnp.pad(v, padw).reshape(B, nb, ATT_BLOCK, ATT_KV_HEADS, HEAD_DIM)

    def with_meta_and_band(t, tb):
        prev = jnp.concatenate([jnp.zeros_like(tb[:, :1]), tb[:, :-1]], axis=1)
        meta = jnp.broadcast_to(t[:, None, :N_META], (B, nb, N_META, ATT_KV_HEADS, HEAD_DIM))
        return jnp.concatenate([meta, prev, tb], axis=2)

    keys = with_meta_and_band(k, kb)
    vals = with_meta_and_band(v, vb)
    qpos = (jnp.arange(Lp) - pad).reshape(nb, ATT_BLOCK)
    kpos = jnp.concatenate([qpos - ATT_BLOCK, qpos], axis=-1)
    rel = qpos[:, :, None] - kpos[:, None, :]
    band_mask = (rel >= 0) & (rel < WINDOW) & (kpos[:, None, :] >= N_META)
    meta_mask = jnp.arange(N_META)[None, None, :] <= qpos[:, :, None]
    mask = jnp.concatenate([meta_mask, band_mask], axis=-1)

    scale = HEAD_DIM ** -0.5
    scores = jnp.einsum('bnqhgd,bnkhd->bhgnqk', qb, keys).astype(jnp.float32) * scale
    scores = jnp.where(mask, scores, -jnp.inf)
    sink = jnp.broadcast_to(sinks.astype(jnp.float32).reshape(1, ATT_KV_HEADS, ATT_GROUP, 1, 1, 1),
                            scores.shape[:-1] + (1,))
    probs = jax.nn.softmax(jnp.concatenate([scores, sink], axis=-1), axis=-1)[..., :-1]
    out = jnp.einsum('bhgnqk,bnkhd->bnqhgd', probs.astype(v.dtype), vals)
    return out.reshape(B, Lp, ATT_WIDTH)[:, pad:]

def _hgrn2_chunk_step(state, inp):
    q, lf, kk, v = inp
    C = q.shape[2]
    b = jnp.cumsum(lf, axis=2)
    causal = jnp.tril(jnp.ones((C, C), dtype=bool))
    diff = b[:, :, :, None, :] - b[:, :, None, :, :]
    decay = jnp.exp(jnp.where(causal[None, None, :, :, None], diff, -jnp.inf))
    scores = jnp.einsum('bhtsk,bhsk->bhts', q[:, :, :, None, :] * decay, kk)
    o = (jnp.einsum('bhts,bhsv->bhtv', scores, v)
         + jnp.einsum('bhtk,bhkv->bhtv', q * jnp.exp(b), state))
    b_last = b[:, :, -1:, :]
    new_state = (jnp.exp(b_last[:, :, 0, :])[..., None] * state
                 + jnp.einsum('bhsk,bhsv->bhkv', kk * jnp.exp(b_last - b), v))
    return new_state, o

def hgrn2_mixer(hq, hf, hi, hg, lb, norm_g):
    B, L = hq.shape[0], hq.shape[1]
    out_dtype = hi.dtype
    lbf = lb.astype(jnp.float32)
    z = hf.astype(jnp.float32)
    logf = jnp.log(lbf + (1.0 - lbf) * jax.nn.sigmoid(z))
    kgate = (1.0 - lbf) * jax.nn.sigmoid(-z)
    q = jax.nn.silu(hq.astype(jnp.float32))
    v = hi.astype(jnp.float32)
    pad = HGRN_CHUNK - N_META
    Lp = L + pad
    nc = Lp // HGRN_CHUNK

    def chunks(t, d):
        t = jnp.pad(t, ((0, 0), (pad, 0), (0, 0)))
        return t.reshape(B, nc, HGRN_CHUNK, HGRN_HEADS, d).transpose(1, 0, 3, 2, 4)

    xs = (chunks(q, HGRN_DK), chunks(logf, HGRN_DK), chunks(kgate, HGRN_DK), chunks(v, HGRN_DV))
    s0 = jnp.zeros((B, HGRN_HEADS, HGRN_DK, HGRN_DV), jnp.float32)
    _, o = lax.scan(_hgrn2_chunk_step, s0, xs)
    o = o.transpose(1, 0, 3, 2, 4).reshape(B, Lp, HGRN_HEADS, HGRN_DV)[:, pad:]
    o = rms_norm(o, norm_g.reshape(HGRN_HEADS, HGRN_DV)).reshape(B, L, HV)
    return (o * jax.nn.silu(hg.astype(jnp.float32))).astype(out_dtype)

def peer_ffn(x, w_q, sub_keys, u, v):
    B, S, D = x.shape
    T = B * S
    xt = x.reshape(T, D)
    q = (xt @ w_q).reshape(T, PEER_HEADS, 2, PEER_DHALF)
    s = jnp.einsum('thcd,hcnd->thcn', q, sub_keys).astype(jnp.float32)
    s1v, s1i = lax.top_k(s[:, :, 0], PEER_TOPK)
    s2v, s2i = lax.top_k(s[:, :, 1], PEER_TOPK)
    cand = (s1v[..., :, None] + s2v[..., None, :]).reshape(T, PEER_HEADS, PEER_TOPK * PEER_TOPK)
    cidx = (s1i[..., :, None] * PEER_NKEYS + s2i[..., None, :]).reshape(T, PEER_HEADS, PEER_TOPK * PEER_TOPK)
    top_s, top_pos = lax.top_k(cand, PEER_TOPK)
    eidx = jnp.take_along_axis(cidx, top_pos, axis=-1)
    gates = jax.nn.softmax(top_s, axis=-1)
    nblk = T // PEER_TOKEN_BLOCK
    xb = xt.reshape(nblk, PEER_TOKEN_BLOCK, D)
    eb = eidx.reshape(nblk, PEER_TOKEN_BLOCK, PEER_HEADS * PEER_TOPK)
    gb = gates.reshape(nblk, PEER_TOKEN_BLOCK, PEER_HEADS * PEER_TOPK)

    def block(args):
        xs, es, gs = args
        a = jnp.einsum('td,ted->te', xs, u[es])
        hact = (jax.nn.gelu(a.astype(jnp.float32)) * gs).astype(xs.dtype)
        return jnp.einsum('te,ted->td', hact, v[es])

    out = lax.map(block, (xb, eb, gb))
    return out.reshape(B, S, D)

def setup_inputs(seed: int = 0) -> dict:
    key = jax.random.key(seed)
    ks = jax.random.split(key, 16)
    f32 = jnp.float32

    def nrm(k, shape, scale):
        return jax.random.normal(k, shape, f32) * scale

    return {
        "x": nrm(ks[0], (BATCH, SEQ, D_MODEL), 1.0),
        "meta_tokens": nrm(ks[1], (N_META, D_MODEL), 1.0),
        "hgrn_lb_logits": nrm(ks[2], (DEPTH + 1, HK), 0.5),
        "ln_mix_g": 1.0 + nrm(ks[3], (DEPTH, D_MODEL), 0.02),
        "w_in": nrm(ks[4], (DEPTH, D_MODEL, IN_COLS), D_MODEL ** -0.5),
        "q_norm_g": 1.0 + nrm(ks[5], (DEPTH, HEAD_DIM), 0.02),
        "k_norm_g": 1.0 + nrm(ks[6], (DEPTH, HEAD_DIM), 0.02),
        "attn_sinks": nrm(ks[7], (DEPTH, ATT_Q_HEADS), 0.5),
        "hgrn_norm_g": 1.0 + nrm(ks[8], (DEPTH, HV), 0.02),
        "w_out": nrm(ks[9], (DEPTH, MIX_WIDTH, D_MODEL), MIX_WIDTH ** -0.5),
        "ln_ffn_g": 1.0 + nrm(ks[10], (DEPTH, D_MODEL), 0.02),
        "peer_w_q": nrm(ks[11], (DEPTH, D_MODEL, PEER_HEADS * PEER_DKEY), D_MODEL ** -0.5),
        "peer_sub_keys": nrm(ks[12], (DEPTH, PEER_HEADS, 2, PEER_NKEYS, PEER_DHALF), PEER_DHALF ** -0.5),
        "peer_u": nrm(ks[13], (DEPTH, PEER_N, D_MODEL), D_MODEL ** -0.5),
        "peer_v": nrm(ks[14], (DEPTH, PEER_N, D_MODEL), 0.25),
    }

def reference(x, meta_tokens, hgrn_lb_logits, ln_mix_g, w_in, q_norm_g, k_norm_g, attn_sinks,
              hgrn_norm_g, w_out, ln_ffn_g, peer_w_q, peer_sub_keys, peer_u, peer_v):
    B, S, D = x.shape
    meta = jnp.broadcast_to(meta_tokens[None].astype(x.dtype), (B, N_META, D))
    h = jnp.concatenate([meta, x], axis=1)
    L = S + N_META
    pos = jnp.arange(L)
    lbs = jnp.cumsum(jax.nn.softmax(hgrn_lb_logits.astype(jnp.float32), axis=0), axis=0)
    split_at = list(np.cumsum(IN_SPLITS)[:-1])
    for l in range(DEPTH):
        hn = rms_norm(h, ln_mix_g[l])
        proj = hn @ w_in[l]
        aq, ak, av, hq, hf, hi, hg = jnp.split(proj, split_at, axis=-1)
        aq = partial_rope(rms_norm(aq.reshape(B, L, ATT_Q_HEADS, HEAD_DIM), q_norm_g[l]), pos)
        ak = partial_rope(rms_norm(ak.reshape(B, L, ATT_KV_HEADS, HEAD_DIM), k_norm_g[l]), pos)
        av = av.reshape(B, L, ATT_KV_HEADS, HEAD_DIM)
        att = sliding_window_sink_attention(aq, ak, av, attn_sinks[l])
        rec = hgrn2_mixer(hq, hf, hi, hg, lbs[l], hgrn_norm_g[l])
        h = h + jnp.concatenate([att, rec], axis=-1) @ w_out[l]
        if l == DEPTH - 1:
            h = h[:, N_META:]
        h = h + peer_ffn(rms_norm(h, ln_ffn_g[l]), peer_w_q[l], peer_sub_keys[l], peer_u[l], peer_v[l])
    return h


_drawn_inputs = setup_inputs


def setup_inputs(seed=0):
    import zlib

    import numpy as np

    out = dict(_drawn_inputs(seed))
    spreads = {}
    factors = {'ln_mix_g': 3.263,
     'q_norm_g': 8.0,
     'k_norm_g': 8.0,
     'attn_sinks': 8.0,
     'hgrn_norm_g': 13.053,
     'ln_ffn_g': 26.136}
    for name, (base, spread) in spreads.items():
        noise = np.random.default_rng([zlib.crc32(name.encode()), seed]).standard_normal(out[name].shape)
        drawn = base * np.exp(spread * noise) if base else spread * noise
        out[name] = __import__('jax').numpy.asarray(drawn.astype(out[name].dtype))
    for name, factor in factors.items():
        out[name] = (out[name] * factor).astype(out[name].dtype)
    return out
```

```python
from contextlib import ExitStack

import numpy as np

import concourse.bass as bass
from concourse import mybir

ALU = mybir.AluOpType
ACT = mybir.ActivationFunctionType
AX = mybir.AxisListType
F32 = mybir.dt.float32
F32R = mybir.dt.float32r
U32 = mybir.dt.uint32

P = 128
D = 2048
DC = D // P
T = 512
TB = T // P
M = 16
L = M + T
HD = 128
QH, KVH = 8, 2
GROUP = QH // KVH
RH = 8
ROPE = 32
HALF = ROPE // 2
EPS = 1e-6
SCALE = HD ** -0.5
BAND = 2 * P
KEYS = M + BAND
NEG = -1e30
LEVELS = 7
PH, NK, TOPK = 8, 128, 16
PC = 512
KB = 1024
BASE = 16512


class Count:

    def __init__(self, eng, sem):
        self.eng, self.sem, self.n, self.reg, self.per = eng, sem, 0, None, 0

    def up(self, ins):
        ins.then_inc(self.sem, 1)
        self.n += 1

    def link(self, ins):
        self.up(ins)
        self.wait()

    def wait(self):
        self.eng.wait_ge(self.sem, self.n if self.reg is None else self.reg * self.per + self.n)

    def enter(self, reg, per):
        self.reg, self.per, self.start = reg, per, self.n

    def leave(self, trips):
        assert self.n - self.start == self.per, (self.n - self.start, self.per)
        self.n = self.start + trips * self.per
        self.reg = None


class Place:

    def __init__(self, nc):
        self.nc = nc

    def __call__(self, name, shape, dtype, kb):
        off = BASE + int(round(kb * KB))
        assert off % 4 == 0
        return self.nc.alloc_sbuf_tensor_at(name, shape, dtype, offset=off)


def inverse_root(dve, link, out, square, root, spare):
    link(dve.reciprocal(out, root))
    link(dve.tensor_tensor(spare, out, out, ALU.mult))
    link(dve.tensor_tensor(spare, spare, square, ALU.mult))
    link(dve.tensor_scalar(spare, spare, -0.5, 1.5, ALU.mult, ALU.add))
    link(dve.tensor_tensor(out, out, spare, ALU.mult))




def norm_rows(nc, tag, tiles, gain, xT, ident, place, kb, extra_sync=None):
    n = len(tiles)
    with ExitStack() as ctx:
        def sem(name):
            return ctx.enter_context(nc.semaphore(f"{tag}_{name}"))

        loaded, summed, meaned, rooted = sem("loaded"), sem("summed"), sem("meaned"), sem("rooted")
        scaled, turned, emptied, chain = sem("scaled"), sem("turned"), sem("emptied"), sem("chain")
        scaled_rows = place(f"{tag}_scaled_rows", [P, 2, D], F32, kb)
        squares = place(f"{tag}_squares", [P, D], F32, kb + 16)
        stat = place(f"{tag}_stat", [P, 4, 8], F32, kb + 24)
        banks = [ctx.enter_context(nc.psum_tensor(f"{tag}_bank{b}", [P, 4, P], F32)) for b in range(4)]
        block = ctx.enter_context(nc.Block())
        groups = DC // 4

        @block.sync
        def _(sp):
            for rows, m, col, src in tiles:
                if src is not None:
                    sp.dma_start(rows, src).then_inc(loaded, 16)
            if extra_sync:
                extra_sync(sp)

        @block.scalar
        def _(act):
            act.wait_ge(chain, 1)
            for i, (rows, m, col, src) in enumerate(tiles):
                if src is not None:
                    act.wait_ge(loaded, 16 * n)
                if i:
                    act.wait_ge(summed, i)
                act.activation(squares[0:m, :], rows, ACT.Square,
                               accum_out=stat[0:m, 0, i:i + 1]).then_inc(summed, 1)
            act.wait_ge(meaned, 1)
            act.activation(stat[:, 2, 0:n], stat[:, 1, 0:n], ACT.Sqrt).then_inc(rooted, 1)

        def empty(dve, i):
            rows, m, col, src = tiles[i]
            for g in range(groups):
                k = i * groups + g
                dve.wait_ge(turned, k + 1)
                dve.tensor_tensor(xT[:, 4 * g:4 * g + 4, col:col + m], banks[k % 4][:, :, 0:m],
                                  gain[:, 4 * g:4 * g + 4].unsqueeze(2).to_broadcast([P, 4, m]),
                                  ALU.mult).then_inc(emptied, 1)

        @block.vector
        def _(dve):
            link = Count(dve, chain).link
            link(dve.memset(stat[:, 0, :], 1.0))
            dve.wait_ge(summed, n)
            dve.tensor_scalar(stat[:, 1, 0:n], stat[:, 0, 0:n], 1.0 / D, EPS,
                              ALU.mult, ALU.add).then_inc(meaned, 1)
            dve.wait_ge(rooted, 1)
            inverse_root(dve, link, stat[:, 3, 0:n], stat[:, 1, 0:n], stat[:, 2, 0:n], stat[:, 0, 0:n])
            for i, (rows, m, col, src) in enumerate(tiles):
                if i >= 2:
                    dve.wait_ge(turned, groups * (i - 1))
                dve.tensor_scalar(scaled_rows[0:m, i % 2, :], rows, stat[0:m, 3, i:i + 1], None,
                                  ALU.mult).then_inc(scaled, 1)
                if i == 0:
                    continue
                empty(dve, i - 1)
            empty(dve, n - 1)

        @block.tensor
        def _(pe):
            for i, (rows, m, col, src) in enumerate(tiles):
                pe.wait_ge(scaled, i + 1)
                for g in range(groups):
                    k = i * groups + g
                    if k >= 4:
                        pe.wait_ge(emptied, k - 3)
                    for j in range(4):
                        c = 4 * g + j
                        last = pe.transpose(banks[k % 4][:, j, 0:m],
                                            scaled_rows[0:m, i % 2, c * P:(c + 1) * P],
                                            ident[0:m, 0:m])
                    last.then_inc(turned, 1)



META_PIECES, PLAIN_PIECES, TURNED_PIECES = 3, 4, 4
NAT_PIECES = META_PIECES + PLAIN_PIECES
PIECES = NAT_PIECES + TURNED_PIECES
ORDER = [2, 7, 8, 0, 1, 9, 10, 3, 4, 5, 6]
KV_PIECE, HI_PIECE, Q_PIECE, HG_PIECE = 0, 1, 3, 5


def load_piece(sp, p, w_in, w, loaded):
    sp.dma_start(w[:, p % 2], w_in[p]).then_inc(loaded[p % 2], 16)


def project(nc, w_in, w, w_loaded, hnT, nat, nat_meta, turned):
    with ExitStack() as ctx:
        def sem(name):
            return ctx.enter_context(nc.semaphore(f"proj_{name}"))

        bank_free, unit_done = sem("bank_free"), sem("unit_done")
        meta_free, meta_done = sem("meta_free"), sem("meta_done")
        turned_free = sem("turned_free")
        banks = [ctx.enter_context(nc.psum_tensor(f"proj_bank{b}", [P, PC], F32)) for b in range(4)]
        meta_bank = [ctx.enter_context(nc.psum_tensor(f"proj_meta{b}", [P, 4, P], F32))
                     for b in range(2)]
        block = ctx.enter_context(nc.Block())

        @block.sync
        def _(sp):
            for p in range(2, PIECES):
                sp.wait_ge(unit_done, 4 * (p - 1))
                load_piece(sp, p, w_in, w, w_loaded)

        @block.tensor
        def _(pe):
            def natural(j, slot, turn, with_meta):
                pe.wait_ge(w_loaded[slot], 16 * (turn + 1))
                if with_meta:
                    pe.wait_ge(meta_free, j + 1)
                    for c in range(DC):
                        last = pe.matmul(meta_bank[0][0:M, :, :], hnT[:, c, 0:M],
                                         w[:, slot, c, :], start=(c == 0), stop=(c == DC - 1))
                    last.then_inc(meta_done, 1)
                for tb in range(TB):
                    pe.wait_ge(bank_free, 4 * j + tb + 1)
                    for c in range(DC):
                        last = pe.matmul(banks[tb][:, :], hnT[:, c, M + tb * P:M + (tb + 1) * P],
                                         w[:, slot, c, :], start=(c == 0), stop=(c == DC - 1))
                    last.then_inc(unit_done, 1)

            for j in range(META_PIECES):
                natural(j, j % 2, j // 2, True)
            with pe.Fori(0, PLAIN_PIECES // 2) as i:
                for s in range(2):
                    first = META_PIECES + s
                    natural(2 * i + first, first % 2, i + first // 2, False)
            pe.wait_ge(meta_free, META_PIECES + 1)
            with pe.Fori(0, TURNED_PIECES // 2) as i:
                for s in range(2):
                    j = i * 2 + (NAT_PIECES + s)
                    slot = (NAT_PIECES + s) % 2
                    pe.wait_ge(w_loaded[slot], 16 * (i + ((NAT_PIECES + s) // 2 + 1)))
                    pe.wait_ge(turned_free, i * 2 + (s + 1))
                    for cb in range(4):
                        cols = slice(cb * P, (cb + 1) * P)
                        for c in range(DC):
                            last = pe.matmul(meta_bank[s][:, cb, 0:M], w[:, slot, c, cols],
                                             hnT[:, c, 0:M], start=(c == 0), stop=(c == DC - 1))
                        if cb == 3:
                            last.then_inc(meta_done, 1)
                        pe.wait_ge(bank_free, 4 * j + cb + 1)
                        for c in range(DC):
                            last = pe.matmul(banks[cb][:, :], w[:, slot, c, cols],
                                             hnT[:, c, M:L], start=(c == 0), stop=(c == DC - 1))
                        last.then_inc(unit_done, 1)

        @block.vector
        def _(dve):
            dve.sem_inc(bank_free, 4)
            with dve.Fori(0, NAT_PIECES) as j:
                for tb in range(TB):
                    dve.wait_ge(unit_done, 4 * j + tb + 1)
                    dve.tensor_copy(nat[:, j, tb, :], banks[tb][:, :]).then_inc(bank_free, 1)
            with dve.Fori(0, TURNED_PIECES) as i:
                for cb in range(4):
                    dve.wait_ge(unit_done, 4 * i + (4 * NAT_PIECES + cb + 1))
                    dve.tensor_copy(turned[:, 4 * i + cb, M:L], banks[cb][:, :])\
                        .then_inc(bank_free, 1)

        @block.scalar
        def _(act):
            act.sem_inc(meta_free, 1)
            act.sem_inc(turned_free, 2)
            with act.Fori(0, META_PIECES) as j:
                act.wait_ge(meta_done, j + 1)
                act.copy(nat_meta[:, j, :], meta_bank[0][0:M, :, :].rearrange("m a b -> m (a b)"))\
                    .then_inc(meta_free, 1)
            with act.Fori(0, TURNED_PIECES // 2) as i:
                for s in range(2):
                    act.wait_ge(meta_done, i * 2 + (META_PIECES + s + 1))
                    act.copy(turned[:, pl(8 * i + 4 * s, 4), 0:M], meta_bank[s][:, :, 0:M])\
                        .then_inc(turned_free, 1)


def pl(start, count):
    return bass.ds(start, count)




def attend(nc, place, kb, nat, nat_meta, mix, cst):
    units = GROUP * TB
    qk = GROUP + 1
    with ExitStack() as ctx:
        def sem(name):
            return ctx.enter_context(nc.semaphore(f"att_{name}"))

        def bank(name, shape):
            return ctx.enter_context(nc.psum_tensor(f"att_{name}", shape, F32))

        rows = place("att_rows", [P, TB, qk, HD], F32, kb)
        squares = place("att_squares", [P, TB, qk, HD], F32, kb + 10)
        qT = place("att_qT", [P, GROUP, T], F32, kb + 20)
        kT = place("att_kT", [P, L], F32, kb + 28)
        logits = place("att_logits", [P, 2, KEYS], F32, kb + 31)
        probs = place("att_probs", [P, 2, KEYS], F32, kb + 34)
        probsT = place("att_probsT", [P, 2, 2, P], F32, kb + 37)
        probsT_meta = place("att_probsT_meta", [M, 2, P], F32, kb + 39)
        rows_meta = place("att_rows_meta", [M, 2, HD], F32, kb + 40)
        rot = place("att_rot", [P, 2, TB, qk, HALF], F32, kb + 41)
        stat = place("att_stat", [P, 4, TB * qk + 1], F32, kb + 44)
        soft = place("att_soft", [P, 6, units], F32, kb + 44.5)
        sink = place("att_sink", [P, GROUP], F32, kb + 45)
        top, neg_top, den, sink_exp, inv = (soft[:, k, :] for k in range(5))

        squared, meaned, rooted, rows_ready = (sem("squared"), sem("meaned"), sem("rooted"),
                                               sem("rows_ready"))
        chain, turned, turned_out, key_out = sem("chain"), sem("turned"), sem("turned_out"), sem("key_out")
        scores_done, scores_free, soft_ready = sem("scores_done"), sem("scores_free"), sem("soft_ready")
        exp_done, probs_turned, probs_out = sem("exp_done"), sem("probs_turned"), sem("probs_out")
        out_done, out_free = sem("out_done"), sem("out_free")
        prep_bank = [bank(f"prep{b}", [P, TB, P]) for b in range(2)]
        s_bank = [bank(f"s{b}", [P, PC]) for b in range(2)]
        t_bank = [bank(f"t{b}", [P, 3, P]) for b in range(2)]
        o_bank = [bank(f"o{b}", [P, HD]) for b in range(2)]
        block = ctx.enter_context(nc.Block())

        def heads(u):
            return u // TB, u % TB

        @block.scalar
        def _(act):
            with act.Fori(0, KVH) as g:
                act.wait_ge(rows_ready, g)
                act.activation(squares[:, :, 0:GROUP, :],
                               nat[:, Q_PIECE + g, :, :].rearrange("p t (h d) -> p t h d", d=HD),
                               ACT.Square).then_inc(squared, 1)
                act.activation(squares[:, :, GROUP, :], nat[:, KV_PIECE, :, pl(g * HD, HD)],
                               ACT.Square).then_inc(squared, 1)
                act.activation(rows_meta[:, 1, :], nat_meta[:, KV_PIECE, pl(g * HD, HD)],
                               ACT.Square).then_inc(squared, 1)
                act.wait_ge(meaned, g + 1)
                act.activation(stat[:, 2, :], stat[:, 1, :], ACT.Sqrt).then_inc(rooted, 1)
                for k in range(qk):
                    act.wait_ge(turned, g * qk + k + 1)
                    if k == 0:
                        act.wait_ge(out_done, g * units)
                    if k < GROUP:
                        act.copy(qT[:, k, :], prep_bank[k % 2][:, :, :].rearrange("p t d -> p (t d)"))\
                            .then_inc(turned_out, 1)
                    else:
                        act.copy(kT[:, M:L], prep_bank[k % 2][:, :, :].rearrange("p t d -> p (t d)"))\
                            .then_inc(turned_out, 1)
                for s in range(units + 1):
                    if s < units:
                        act.wait_ge(soft_ready, g * units + s + 1)
                        if s >= 2:
                            act.wait_ge(probs_turned, g * units + s - 1)
                        h, n = heads(s)
                        keys = KEYS if n else M + P
                        act.activation(probs[:, s % 2, 0:keys], logits[:, s % 2, 0:keys], ACT.Exp,
                                       bias=neg_top[:, s:s + 1], accum_out=den[:, s:s + 1])\
                            .then_inc(exp_done, 1)
                        act.activation(sink_exp[:, s:s + 1], sink[:, h:h + 1], ACT.Exp,
                                       bias=neg_top[:, s:s + 1]).then_inc(exp_done, 1)
                    if s:
                        u = s - 1
                        act.wait_ge(probs_turned, g * units + u + 1)
                        if u >= 2:
                            act.wait_ge(out_done, g * units + u - 1)
                        act.copy(probsT_meta[:, u % 2, :], t_bank[u % 2][0:M, 2, :])
                        lo = 0 if u % TB else 1
                        act.copy(probsT[:, u % 2, lo:2, :], t_bank[u % 2][:, lo:2, :])\
                            .then_inc(probs_out, 1)

        @block.vector
        def _(dve):
            count = Count(dve, chain)
            link = count.link
            dve.sem_inc(scores_free, 2)
            dve.sem_inc(out_free, 2)
            link(dve.memset(stat[:, 0, :], 1.0))
            with dve.Fori(0, KVH) as g:
                count.enter(g, PREP_LINKS + 3 * units)
                dve.wait_ge(squared, 3 * g + 3)
                link(dve.tensor_reduce(stat[:, 0, 0:TB * qk],
                                       squares[:, :, :, :].rearrange("p t h d -> p (t h) d"),
                                       AX.X, ALU.add))
                link(dve.tensor_reduce(stat[0:M, 0, TB * qk:], rows_meta[:, 1, :], AX.X, ALU.add))
                dve.tensor_scalar(stat[:, 1, :], stat[:, 0, :], 1.0 / HD, EPS,
                                  ALU.mult, ALU.add).then_inc(meaned, 1)
                dve.wait_ge(rooted, g + 1)
                inverse_root(dve, link, stat[:, 3, :], stat[:, 1, :], stat[:, 2, :], stat[:, 0, :])
                link(dve.tensor_copy(sink[:, :], cst["sinks"][:, pl(g * GROUP, GROUP)]))
                rstd = stat[:, 3, 0:TB * qk].rearrange("p (t h) -> p t h", h=qk)
                for tb in range(TB):
                    dve.tensor_tensor(
                        rows[:, tb, 0:GROUP, :],
                        nat[:, Q_PIECE + g, tb, :].rearrange("p (h d) -> p h d", d=HD),
                        rstd[:, tb, 0:GROUP].unsqueeze(2).to_broadcast([P, GROUP, HD]), ALU.mult)
                link(dve.tensor_tensor(
                    rows[:, :, GROUP, :], nat[:, KV_PIECE, :, pl(g * HD, HD)],
                    rstd[:, :, GROUP:qk].to_broadcast([P, TB, HD]), ALU.mult))
                link(dve.tensor_tensor(
                    rows[:, :, :, :], rows[:, :, :, :],
                    cst["qk_gain"][:, :, :].unsqueeze(1).to_broadcast([P, TB, qk, HD]), ALU.mult))
                link(dve.scalar_tensor_tensor(
                    rows_meta[:, 0, :], nat_meta[:, KV_PIECE, pl(g * HD, HD)],
                    stat[0:M, 3, TB * qk:], cst["qk_gain"][0:M, GROUP, :], ALU.mult, ALU.mult))
                rotate(dve, link, rows[:, :, :, 0:HALF], rows[:, :, :, HALF:ROPE],
                       rot[:, 0], rot[:, 1],
                       cst["cos"][:, :, :].unsqueeze(2).to_broadcast([P, TB, qk, HALF]),
                       cst["sin"][:, :, :].unsqueeze(2).to_broadcast([P, TB, qk, HALF]))
                rotate(dve, link, rows_meta[:, 0, 0:HALF], rows_meta[:, 0, HALF:ROPE],
                       rot[0:M, 0, 0, 0, :], rot[0:M, 1, 0, 0, :],
                       cst["meta_cos"][:, :], cst["meta_sin"][:, :])
                dve.sem_inc(rows_ready, 1)
                dve.wait_ge(turned, g * qk + qk)
                dve.wait_ge(out_done, g * units)
                dve.tensor_copy(kT[:, 0:M], t_bank[0][:, 0, 0:M]).then_inc(key_out, 1)
                for s in range(units + 2):
                    if s < units:
                        h, n = heads(s)
                        keys = KEYS if n else M + P
                        mask = cst["mask"][:, 0:KEYS] if n else cst["mask_first"][:, :]
                        dve.wait_ge(scores_done, g * units + s + 1)
                        if s >= 2:
                            dve.wait_ge(exp_done, 2 * units * g + 2 * (s - 1))
                        dve.scalar_tensor_tensor(logits[:, s % 2, 0:keys], s_bank[s % 2][:, 0:keys],
                                                 SCALE, mask, ALU.mult, ALU.add)\
                            .then_inc(scores_free, 1)
                        dve.wait_ge(scores_free, g * units + s + 3)
                        link(dve.tensor_reduce(top[:, s:s + 1], logits[:, s % 2, 0:keys],
                                               AX.X, ALU.max))
                        dve.tensor_scalar(neg_top[:, s:s + 1], top[:, s:s + 1], sink[:, h:h + 1],
                                          -1.0, ALU.max, ALU.mult).then_inc(soft_ready, 1)
                    if 1 <= s <= units:
                        u = s - 1
                        dve.wait_ge(exp_done, 2 * units * g + 2 * (u + 1))
                        link(dve.tensor_tensor(inv[:, u:u + 1], den[:, u:u + 1],
                                               sink_exp[:, u:u + 1], ALU.add))
                        link(dve.reciprocal(inv[:, u:u + 1], inv[:, u:u + 1]))
                    if s >= 2:
                        u = s - 2
                        h, n = heads(u)
                        dve.wait_ge(out_done, g * units + u + 1)
                        dve.tensor_scalar(mix[:, n, pl(g * (GROUP * HD) + h * HD, HD)],
                                          o_bank[u % 2][:, :], inv[:, u:u + 1], None, ALU.mult)\
                            .then_inc(out_free, 1)
                count.leave(KVH)

        @block.tensor
        def _(pe):
            ident = cst["ident"]
            with pe.Fori(0, KVH) as g:
                pe.wait_ge(rows_ready, g + 1)
                for k in range(qk):
                    if k >= 2:
                        pe.wait_ge(turned_out, g * qk + k - 1)
                    for tb in range(TB):
                        last = pe.transpose(prep_bank[k % 2][:, tb, :], rows[:, tb, k, :],
                                            ident[:, :])
                    if k == GROUP:
                        last = pe.transpose(t_bank[0][:, 0, 0:M], rows_meta[:, 0, :],
                                            ident[0:M, 0:M])
                    last.then_inc(turned, 1)
                pe.wait_ge(turned_out, (g + 1) * qk)
                pe.wait_ge(key_out, g + 1)
                for s in range(units + 2):
                    if s < units:
                        h, n = heads(s)
                        pe.wait_ge(scores_free, g * units + s + 1)
                        q = qT[:, h, n * P:(n + 1) * P]
                        if n < 2:
                            keys = M + (n + 1) * P
                            last = pe.matmul(s_bank[s % 2][:, 0:keys], q, kT[:, 0:keys],
                                             start=True, stop=True)
                        else:
                            pe.matmul(s_bank[s % 2][:, 0:M], q, kT[:, 0:M], start=True, stop=True)
                            last = pe.matmul(s_bank[s % 2][:, M:KEYS], q,
                                             kT[:, M + (n - 1) * P:M + (n + 1) * P],
                                             start=True, stop=True)
                        last.then_inc(scores_done, 1)
                    if 1 <= s <= units:
                        u = s - 1
                        pe.wait_ge(exp_done, 2 * units * g + 2 * u + 1)
                        if u >= 2:
                            pe.wait_ge(probs_out, g * units + u - 1)
                        pe.transpose(t_bank[u % 2][0:M, 2, :], probs[:, u % 2, 0:M], ident[:, :])
                        if u % TB:
                            pe.transpose(t_bank[u % 2][:, 0, :], probs[:, u % 2, M:M + P], ident[:, :])
                            own = probs[:, u % 2, M + P:KEYS]
                        else:
                            own = probs[:, u % 2, M:M + P]
                        pe.transpose(t_bank[u % 2][:, 1, :], own, ident[:, :])\
                            .then_inc(probs_turned, 1)
                    if s >= 2:
                        u = s - 2
                        h, n = heads(u)
                        b = u % 2
                        pe.wait_ge(probs_out, g * units + u + 1)
                        pe.wait_ge(out_free, g * units + u + 1)
                        value = pl(g * HD + KVH * HD, HD)
                        pe.matmul(o_bank[b][:, :], probsT[:, b, 1, :],
                                  nat[:, KV_PIECE, n, value], start=True, stop=False)
                        if n:
                            pe.matmul(o_bank[b][:, :], probsT[:, b, 0, :],
                                      nat[:, KV_PIECE, n - 1, value], start=False, stop=False)
                        pe.matmul(o_bank[b][:, :], probsT_meta[:, b, :],
                                  nat_meta[:, KV_PIECE, value], start=False, stop=True)\
                            .then_inc(out_done, 1)


PREP_LINKS = 2 + 5 + 1 + 3 + 2 * 3


def rotate(dve, link, x1, x2, a, b, cos, sin):
    dve.tensor_tensor(a, x1, sin, ALU.mult)
    link(dve.tensor_tensor(b, x2, sin, ALU.mult))
    dve.tensor_tensor(x1, x1, cos, ALU.mult)
    link(dve.tensor_tensor(x2, x2, cos, ALU.mult))
    dve.tensor_tensor(x1, x1, b, ALU.subtract)
    link(dve.tensor_tensor(x2, x2, a, ALU.add))




def recur(nc, place, kb, nat, nat_meta, turned, mix, cst):
    grams = LEVELS + 1
    with ExitStack() as ctx:
        def sem(name):
            return ctx.enter_context(nc.semaphore(f"rec_{name}"))

        def bank(name, shape):
            return ctx.enter_context(nc.psum_tensor(f"rec_{name}", shape, F32))

        keys = place("rec_keys", [P, RH, L], F32, kb)
        logs = place("rec_logs", [P, RH, L], F32, kb + 16.5)
        gaps = place("rec_gaps", [P, 2, T], F32, kb + 33)
        decays = place("rec_decays", [P, 2, T], F32, kb + 37)
        halves = place("rec_halves", [P, 2, T], F32, kb + 41)
        scores = place("rec_scores", [P, TB, P], F32, kb + 45)
        q_in = place("rec_q_in", [P, T], F32, kb + 47)
        k_out = place("rec_k_out", [P, L], F32, kb + 49)
        gap_out = place("rec_gap_out", [P, L], F32, kb + 51.5)
        k_now = place("rec_k_now", [P, T], F32, kb + 54)
        grown = place("rec_grown", [P, T], F32, kb + 56)
        k_outT = place("rec_k_outT", [P, TB, HD], F32, kb + 58)
        state = place("rec_state", [P, TB, HD], F32, kb + 60)
        lb = place("rec_lb", [P, 2, RH], F32, kb + 62)
        diff = place("rec_diff", [P, RH], F32, kb + 62.25)
        stat = place("rec_stat", [P, 4, TB * RH], F32, kb + 62.5)
        query, gate = turned[:, 0:RH, :], turned[:, RH:2 * RH, :]

        apart, bounded = sem("apart"), sem("bounded")
        opened, logged, bounds, summed = sem("opened"), sem("logged"), sem("bounds"), sem("summed")
        gap_ready, decay_ready, half_ready = sem("gap_ready"), sem("decay_ready"), sem("half_ready")
        gram_done, gram_out, copied = sem("gram_done"), sem("gram_out"), sem("k_now_copied")
        out_gap, edge_ready = sem("out_gap"), sem("edge_ready")
        in_out_ready, k_turned, k_turned_out = sem("in_out"), sem("k_turned"), sem("k_turned_out")
        update_done, state_ready = sem("update_done"), sem("state_ready")
        out_done, out_copied, mix_ready = sem("out_done"), sem("out_copied"), sem("mix_ready")
        squared, meaned, rooted, silu = sem("squared"), sem("meaned"), sem("rooted"), sem("silu")
        waited = sem("waited")
        g_bank = [bank(f"g{b}", [P, TB, P]) for b in range(2)]
        k_bank, u_bank = bank("k", [P, TB, P]), bank("u", [P, TB, HD])
        o_bank = bank("o", [P, TB, HD])
        block = ctx.enter_context(nc.Block())

        def value(h, c):
            return nat[:, h // 4 + HI_PIECE, c, pl((h % 4) * HD, HD)]

        @block.gpsimd
        def _(pool):
            pool.wait_ge(logged, 1)
            with pool.Fori(0, RH) as h:
                pool.wait_ge(gram_done, grams * h)
                pool.tensor_copy(k_now[:, :], keys[:, h, M:L]).then_inc(copied, 1)

        @block.scalar
        def _(act):
            act.wait_ge(apart, 1)
            act.activation(lb[:, 0, :], diff[:, :], ACT.Sigmoid)
            act.activation(lb[:, 1, :], diff[:, :], ACT.Sigmoid, scale=-1.0).then_inc(bounded, 1)
            act.activation(logs[:, :, :], query, ACT.Sigmoid).then_inc(opened, 1)
            act.activation(keys[:, :, :], gate, ACT.Sigmoid, scale=-1.0).then_inc(opened, 1)
            act.wait_ge(opened, 2)
            act.activation(gate, gate, ACT.Sigmoid).then_inc(opened, 1)
            act.wait_ge(bounds, 1)
            act.activation(gate, gate, ACT.Ln).then_inc(logged, 1)
            act.wait_ge(summed, 1)
            with act.Fori(0, RH) as h:
                act.wait_ge(in_out_ready, 2 * h)
                act.activation(grown[:, :], logs[:, h, M:L], ACT.Exp).then_inc(edge_ready, 1)
                act.wait_ge(out_gap, h + 1)
                act.wait_ge(edge_ready, 2 * h + 1)
                act.wait_ge(k_turned, h)
                act.activation(k_out[:, :], gap_out[:, :], ACT.Exp).then_inc(edge_ready, 1)
                for l in range(LEVELS):
                    b = l % 2
                    act.wait_ge(gap_ready, LEVELS * h + l + 1)
                    if l >= 2:
                        act.wait_ge(half_ready, LEVELS * h + l - 1)
                    act.activation(decays[:, b, :], gaps[:, b, :], ACT.Exp)\
                        .then_inc(decay_ready, 1)
                    if l == 1:
                        act.wait_ge(k_turned, h + 1)
                        act.copy(k_outT[:, 0:TB - 1, :], k_bank[:, 0:TB - 1, :])
                        act.copy(k_outT[0:M, TB - 1, :], k_bank[0:M, TB - 1, :])\
                            .then_inc(k_turned_out, 1)
                act.wait_ge(out_done, h + 1)
                act.copy(mix[:, :, pl(h * HD + QH * HD, HD)], o_bank[:, :, :]).then_inc(out_copied, 1)
            act.wait_ge(out_copied, RH)
            act.activation(logs_as_squares(logs), mix[:, :, QH * HD:], ACT.Square).then_inc(squared, 1)
            act.activation(keys_as_gates(keys), hg_view(nat), ACT.Sigmoid).then_inc(silu, 1)
            act.wait_ge(meaned, 1)
            act.activation(stat[:, 2, :], stat[:, 1, :], ACT.Sqrt).then_inc(rooted, 1)

        @block.tensor
        def _(pe):
            ident = cst["ident"]
            with pe.Fori(0, RH) as h:
                pe.wait_ge(copied, h + 1)
                pe.wait_ge(gram_out, grams * h)
                for c in range(TB):
                    last = pe.matmul(g_bank[0][:, c, :], k_now[:, c * P:(c + 1) * P],
                                     query[:, h, pl(M + c * P, P)], start=True, stop=True)
                last.then_inc(gram_done, 1)
                pe.wait_ge(in_out_ready, 2 * h + 2)
                for c in range(TB - 1):
                    pe.transpose(k_bank[:, c, :], k_out[:, M + c * P:M + (c + 1) * P], ident[:, :])
                pe.transpose(k_bank[0:M, TB - 1, :], k_out[:, 0:M], ident[:, :])\
                    .then_inc(k_turned, 1)
                for l in range(LEVELS):
                    b = (l + 1) % 2
                    pe.wait_ge(half_ready, LEVELS * h + l + 1)
                    if l:
                        pe.wait_ge(gram_out, grams * h + l)
                    tile = halves[:, l % 2, :]
                    for c in range(TB):
                        part = tile[:, c * P:(c + 1) * P]
                        last = pe.matmul(g_bank[b][:, c, :], part, part, start=True, stop=True)
                    last.then_inc(gram_done, 1)
                    if l == 2:
                        pe.wait_ge(k_turned_out, h + 1)
                        for c in range(TB - 1):
                            pe.matmul(u_bank[:, c, :], k_outT[:, c, :], value(h, c),
                                      start=True, stop=True)
                        pe.matmul(u_bank[:, TB - 1, :], k_outT[0:M, TB - 1, :],
                                  nat_meta[:, h // 4 + HI_PIECE, pl((h % 4) * HD, HD)],
                                  start=True, stop=True).then_inc(update_done, 1)
                pe.wait_ge(gram_out, grams * (h + 1))
                pe.wait_ge(state_ready, TB * (h + 1))
                pe.wait_ge(out_copied, h)
                for c in range(TB):
                    pe.matmul(o_bank[:, c, :], scores[:, c, :], value(h, c), start=True, stop=False)
                    last = pe.matmul(o_bank[:, c, :], q_in[:, c * P:(c + 1) * P], state[:, c, :],
                                     start=False, stop=True)
                last.then_inc(out_done, 1)

        @block.vector
        def _(dve):
            dve.tensor_tensor(diff[:, :], cst["lb_logits"][:, 0, :], cst["lb_logits"][:, 1, :],
                              ALU.subtract).then_inc(apart, 1)
            dve.wait_ge(opened, 1)
            dve.tensor_tensor(query, query, logs[:, :, :], ALU.mult)
            dve.wait_ge(bounded, 1)
            dve.wait_ge(opened, 3)
            for h in range(RH):
                dve.tensor_scalar(keys[:, h, :], keys[:, h, :], lb[:, 1, h:h + 1], None, ALU.mult)
                last = dve.tensor_scalar(gate[:, h, :], gate[:, h, :], lb[:, 1, h:h + 1],
                                         lb[:, 0, h:h + 1], ALU.mult, ALU.add)
            last.then_inc(bounds, 1)
            dve.wait_ge(logged, 1)
            for h in range(RH):
                last = dve.tensor_tensor_scan(logs[:, h, :], cst["keep"][:, :], gate[:, h, :], 0.0,
                                              ALU.mult, ALU.add)
            last.then_inc(summed, 1)
            dve.wait_ge(summed, 1)
            with dve.Fori(0, RH) as h:
                b_real = logs[:, h, M:L]
                by_chunk = b_real.rearrange("p (c t) -> p c t", t=P)
                dve.wait_ge(edge_ready, 2 * h)
                dve.tensor_tensor(gap_out[:, M:L].rearrange("p (c t) -> p c t", t=P),
                                  by_chunk[:, :, P - 1:P].to_broadcast([P, TB, P]), by_chunk,
                                  ALU.subtract)
                dve.tensor_tensor(gap_out[:, 0:M], logs[:, h, M - 1:M].to_broadcast([P, M]),
                                  logs[:, h, 0:M], ALU.subtract).then_inc(out_gap, 1)

                def split(ap, l):
                    return ap.rearrange("p (n s m) -> p n s m", s=2, m=P >> (l + 1))

                def gap(l):
                    m = P >> (l + 1)
                    b, d = split(b_real, l), split(gaps[:, l % 2, :], l)
                    edge = b[:, :, 0, m - 1:m].to_broadcast([P, T // (2 * m), m])
                    if l >= 2:
                        dve.wait_ge(decay_ready, LEVELS * h + l - 1)
                    dve.tensor_tensor(d[:, :, 0, :], edge, b[:, :, 0, :], ALU.subtract)
                    dve.tensor_tensor(d[:, :, 1, :], b[:, :, 1, :], edge, ALU.subtract)\
                        .then_inc(gap_ready, 1)

                def half(l):
                    w, e = split(halves[:, l % 2, :], l), split(decays[:, l % 2, :], l)
                    dve.wait_ge(decay_ready, LEVELS * h + l + 1)
                    if l >= 2:
                        dve.wait_ge(gram_done, grams * h + l)
                    dve.tensor_tensor(w[:, :, 0, :], e[:, :, 0, :],
                                      split(keys[:, h, M:L], l)[:, :, 0, :], ALU.mult)
                    dve.tensor_tensor(w[:, :, 1, :], e[:, :, 1, :],
                                      split(query[:, h, M:L], l)[:, :, 1, :], ALU.mult)\
                        .then_inc(half_ready, 1)

                def pick(l):
                    dve.wait_ge(gram_done, grams * h + l + 2)
                    dve.wait_ge(gram_out, grams * h + l + 1)
                    dve.sem_inc(waited, 1)
                    dve.copy_predicated(
                        scores[:, :, :],
                        cst["level_mask"][:, l, :].bitcast(U32).unsqueeze(1).to_broadcast([P, TB, P]),
                        g_bank[(l + 1) % 2][:, :, :]).then_inc(gram_out, 1)

                gap(0)
                gap(1)
                dve.wait_ge(edge_ready, 2 * h + 1)
                dve.wait_ge(out_done, h)
                dve.tensor_tensor(q_in[:, :], grown[:, :], query[:, h, M:L], ALU.mult)\
                    .then_inc(in_out_ready, 1)
                dve.wait_ge(edge_ready, 2 * h + 2)
                dve.tensor_tensor(k_out[:, :], k_out[:, :], keys[:, h, :], ALU.mult)\
                    .then_inc(in_out_ready, 1)
                dve.wait_ge(gram_done, grams * h + 1)
                dve.tensor_tensor(scores[:, :, :], g_bank[0][:, :, :],
                                  cst["ident"][:, :].unsqueeze(1).to_broadcast([P, TB, P]),
                                  ALU.mult).then_inc(gram_out, 1)
                for l in range(LEVELS):
                    half(l)
                    if l + 2 < LEVELS:
                        gap(l + 2)
                    if l:
                        pick(l - 1)
                    if l == 4:
                        dve.wait_ge(update_done, h + 1)
                        dve.tensor_copy(state[:, 0, :], u_bank[:, TB - 1, :])\
                            .then_inc(state_ready, 1)
                        for c in range(TB - 1):
                            dve.wait_ge(state_ready, TB * h + c + 1)
                            dve.scalar_tensor_tensor(state[:, c + 1, :], state[:, c, :],
                                                     grown[:, (c + 1) * P - 1:(c + 1) * P],
                                                     u_bank[:, c, :], ALU.mult, ALU.add)\
                                .then_inc(state_ready, 1)
                pick(LEVELS - 1)
            outs = mix[:, :, QH * HD:].rearrange("p t (h d) -> p t h d", d=HD)
            gates = hg_view(nat)
            squares = logs_as_squares(logs)
            dve.wait_ge(squared, 1)
            dve.tensor_reduce(stat[:, 0, :], squares.rearrange("p t (h d) -> p (t h) d", d=HD),
                              AX.X, ALU.add).then_inc(squared, 1)
            dve.wait_ge(squared, 2)
            dve.tensor_scalar(stat[:, 1, :], stat[:, 0, :], 1.0 / HD, EPS, ALU.mult, ALU.add)\
                .then_inc(meaned, 1)
            dve.wait_ge(rooted, 1)
            tail = Count(dve, mix_ready)
            inverse_root(dve, tail.link, stat[:, 3, :], stat[:, 1, :], stat[:, 2, :], stat[:, 0, :])
            dve.wait_ge(silu, 1)
            dve.tensor_tensor(gates, gates, keys_as_gates(keys), ALU.mult)
            tail.link(dve.tensor_tensor(outs, outs, stat[:, 3, :].rearrange("p (t h) -> p t h", h=RH)
                                        .unsqueeze(3).to_broadcast([P, TB, RH, HD]), ALU.mult))
            rows = mix[:, :, QH * HD:]
            tail.link(dve.tensor_tensor(rows, rows, cst["hgrn_gain"][:, :].unsqueeze(1)
                                        .to_broadcast([P, TB, RH * HD]), ALU.mult))
            dve.tensor_tensor(rows.rearrange("p t (j c) -> p j t c", c=PC),
                              rows.rearrange("p t (j c) -> p j t c", c=PC), gates, ALU.mult)


def logs_as_squares(logs):
    return logs[:, :, :].rearrange("p h t -> p (h t)")[:, 0:TB * RH * HD]\
        .rearrange("p (t c) -> p t c", t=TB)


def hg_view(nat):
    return nat[:, HG_PIECE:HG_PIECE + 2, :, :]


def keys_as_gates(keys):
    return keys[:, :, :].rearrange("p h t -> p (h t)")[:, 0:TB * RH * HD]\
        .rearrange("p (j t c) -> p j t c", j=2, t=TB)



OUT_PIECES = D // PC


def mix_out(nc, place, w_out, w, mix, mixT, h, x, cst):
    with ExitStack() as ctx:
        def sem(name):
            return ctx.enter_context(nc.semaphore(f"out_{name}"))

        loaded = [sem("loaded0"), sem("loaded1")]
        turned, act_out, dve_out = sem("turned"), sem("act_out"), sem("dve_out")
        x_loaded, unit_done, added = sem("x_loaded"), sem("unit_done"), sem("added")
        t_bank = [ctx.enter_context(nc.psum_tensor(f"out_t{b}", [P, TB, P], F32)) for b in range(4)]
        banks = [ctx.enter_context(nc.psum_tensor(f"out_bank{b}", [P, PC], F32)) for b in range(4)]
        block = ctx.enter_context(nc.Block())

        @block.sync
        def _(sp):
            load_piece(sp, 0, w_out, w, loaded)
            load_piece(sp, 1, w_out, w, loaded)
            sp.wait_ge(turned, DC)
            sp.dma_start(h[:, :, :], x.rearrange("(b p) d -> p b d", p=P)).then_inc(x_loaded, 16)
            for p in range(2, OUT_PIECES):
                sp.wait_ge(unit_done, TB * (p - 1))
                load_piece(sp, p, w_out, w, loaded)

        @block.tensor
        def _(pe):
            for c in range(DC):
                if c >= 4:
                    pe.wait_ge(act_out if c % 2 == 0 else dve_out, c // 2 - 1)
                for tb in range(TB):
                    last = pe.transpose(t_bank[c % 4][:, tb, :], mix[:, tb, c * P:(c + 1) * P],
                                        cst["ident"][:, :])
                last.then_inc(turned, 1)
            pe.wait_ge(act_out, DC // 2)
            pe.wait_ge(dve_out, DC // 2)
            with pe.Fori(0, OUT_PIECES // 2) as i:
                for s in range(2):
                    pe.wait_ge(loaded[s], 16 * (i + 1))
                    for tb in range(TB):
                        pe.wait_ge(added, i * (2 * TB) + (TB * s + tb + 1))
                        for c in range(DC):
                            last = pe.matmul(banks[tb][:, :], mixT[:, c, tb * P:(tb + 1) * P],
                                             w[:, s, c, :], start=(c == 0), stop=(c == DC - 1))
                        last.then_inc(unit_done, 1)

        @block.scalar
        def _(act):
            for c in range(0, DC, 2):
                act.wait_ge(turned, c + 1)
                act.copy(mixT[:, c, :], t_bank[c % 4][:, :, :].rearrange("p b t -> p (b t)"))\
                    .then_inc(act_out, 1)

        @block.vector
        def _(dve):
            dve.sem_inc(added, TB)
            for c in range(1, DC, 2):
                dve.wait_ge(turned, c + 1)
                dve.tensor_copy(mixT[:, c, :], t_bank[c % 4][:, :, :].rearrange("p b t -> p (b t)"))\
                    .then_inc(dve_out, 1)
            dve.wait_ge(x_loaded, 16)
            with dve.Fori(0, OUT_PIECES) as p:
                for tb in range(TB):
                    dve.wait_ge(unit_done, p * TB + tb + 1)
                    cols = h[:, tb, pl(p * PC, PC)]
                    dve.tensor_tensor(cols, cols, banks[tb][:, :], ALU.add).then_inc(added, 1)



HC = 2 * PH
WQ = 2 * P


def route(nc, place, kb, w_q, xT, picks, cst):
    with ExitStack() as ctx:
        def sem(name):
            return ctx.enter_context(nc.semaphore(f"route_{name}"))

        w = place("route_w", [P, 2, DC, WQ], F32, kb)
        qT = place("route_qT", [P, 2, T], F32, kb + 32)
        sc = place("route_scores", [P, 2, TB, NK], F32, kb + 36)
        rest = place("route_rest", [P, 2, TB, NK], F32, kb + 40)
        cand = place("route_cand", [P, TB, TOPK * TOPK], F32, kb + 44)
        cand_rest = place("route_cand_rest", [P, TB, TOPK * TOPK], F32, kb + 48)
        hot = place("route_hot", [P, TB, TOPK, TOPK], F32, kb + 52)
        val = place("route_val", [P, 2, TB, TOPK], F32, kb + 56)
        idx = place("route_idx", [P, 2, TB, TOPK], U32, kb + 56.5)
        idx_f = place("route_idx_f", [P, 2, TB, TOPK], F32, kb + 57)
        best = place("route_best", [P, TB, TOPK], F32, kb + 57.5)
        pos = place("route_pos", [P, 3, TB, TOPK], U32, kb + 58)
        pos_f = place("route_pos_f", [P, 2, TB, TOPK], F32, kb + 59)
        gate = place("route_gate", [P, 2, TB, TOPK], F32, kb + 59.5)
        total = place("route_total", [P, 2, TB], F32, kb + 60)

        loaded = [sem("loaded0"), sem("loaded1")]
        q_done, q_out, s_done, s_out = sem("q_done"), sem("q_out"), sem("s_done"), sem("s_out")
        chain, shifted, exp_done = sem("chain"), sem("shifted"), sem("exp_done")
        waited = sem("waited")
        q_bank = [ctx.enter_context(nc.psum_tensor(f"route_q{c}", [P, T], F32)) for c in range(2)]
        s_bank = [ctx.enter_context(nc.psum_tensor(f"route_s{c}", [P, TB, NK], F32)) for c in range(2)]
        block = ctx.enter_context(nc.Block())

        @block.sync
        def _(sp):
            for i in range(2):
                sp.dma_start(w[:, i], w_q[i]).then_inc(loaded[i], 16)
            with sp.Fori(1, PH // 2) as i:
                for s in range(2):
                    sp.wait_ge(q_done, i * 4 + (2 * s - 2))
                    sp.dma_start(w[:, s], w_q[i * 2 + s]).then_inc(loaded[s], 16)

        @block.tensor
        def _(pe):
            with pe.Fori(0, PH // 2) as i:
                for s in range(2):
                    pe.wait_ge(loaded[s], 16 * (i + 1))
                    for c in range(2):
                        pe.wait_ge(q_out, i * 4 + 2 * s)
                        for k in range(DC):
                            last = pe.matmul(q_bank[c][:, :], w[:, s, k, c * P:(c + 1) * P],
                                             xT[:, k, :], start=(k == 0), stop=(k == DC - 1))
                        last.then_inc(q_done, 1)
                    for c in range(2):
                        pe.wait_ge(q_out, i * 4 + (2 * s + c + 1))
                        pe.wait_ge(s_out, i * 4 + 2 * s)
                        for tb in range(TB):
                            last = pe.matmul(s_bank[c][:, tb, :], qT[:, c, tb * P:(tb + 1) * P],
                                             cst["sub_keys"][:, i * 4 + (2 * s + c), :],
                                             start=True, stop=True)
                        last.then_inc(s_done, 1)

        @block.scalar
        def _(act):
            with act.Fori(0, PH) as h:
                act.wait_ge(s_done, 2 * h)
                for c in range(2):
                    act.wait_ge(q_done, 2 * h + c + 1)
                    act.copy(qT[:, c, :], q_bank[c][:, :]).then_inc(q_out, 1)
                act.wait_ge(shifted, h)
                for c in range(2):
                    act.wait_ge(s_done, 2 * h + c + 1)
                    act.copy(sc[:, c], s_bank[c][:, :, :]).then_inc(s_out, 1)
                act.wait_ge(shifted, h + 1)
                act.activation(gate[:, 1], gate[:, 0], ACT.Exp).then_inc(exp_done, 1)

        @block.vector
        def _(dve):
            count = Count(dve, chain)
            link = count.link

            def take_wait():
                dve.sem_inc(waited, 1)

            def top16(rows, rests, values, places):
                take_wait()
                for part in range(2):
                    cols = slice(8 * part, 8 * part + 8)
                    src = rows if part == 0 else rests
                    for r, v in zip(src, values):
                        last = dve.max(out=v[:, cols], in_=r)
                    link(last)
                    take_wait()
                    for r, v, p in zip(src, values, places):
                        last = dve.max_index(out=p[:, cols], in_max=v[:, cols], in_values=r)
                    if part == 0:
                        for r, t, v in zip(rows, rests, values):
                            last = dve.match_replace(out=t, in_to_replace=v[:, cols],
                                                     in_values=r, imm_value=-3.0e38)
                    link(last)
                    take_wait()

            with dve.Fori(0, PH) as h:
                count.enter(h, 4 + 1 + 1 + 4 + 1 + 1 + 1 + 6 + 3)
                dve.wait_ge(s_out, 2 * h + 2)
                both = [(c, tb) for c in range(2) for tb in range(TB)]
                top16([sc[:, c, tb, :] for c, tb in both], [rest[:, c, tb, :] for c, tb in both],
                      [val[:, c, tb, :] for c, tb in both], [idx[:, c, tb, :] for c, tb in both])
                link(dve.tensor_copy(idx_f[:, :, :, :], idx[:, :, :, :]))
                link(dve.tensor_tensor(
                    cand[:, :, :].rearrange("p b (i j) -> p b i j", j=TOPK),
                    val[:, 0].unsqueeze(3).to_broadcast([P, TB, TOPK, TOPK]),
                    val[:, 1].unsqueeze(2).to_broadcast([P, TB, TOPK, TOPK]), ALU.add))
                tiles = range(TB)
                top16([cand[:, b, :] for b in tiles], [cand_rest[:, b, :] for b in tiles],
                      [best[:, b, :] for b in tiles], [pos[:, 0, b, :] for b in tiles])
                dve.tensor_tensor(gate[:, 0], best[:, :, :],
                                  best[:, :, 0:1].to_broadcast([P, TB, TOPK]), ALU.subtract)\
                    .then_inc(shifted, 1)
                link(dve.tensor_scalar(pos[:, 1], pos[:, 0], 4, None, ALU.logical_shift_right))
                link(dve.tensor_scalar(pos[:, 2], pos[:, 0], TOPK - 1, None, ALU.bitwise_and))
                link(dve.tensor_copy(pos_f[:, :, :, :], pos[:, 1:3]))
                for c in range(2):
                    link(dve.tensor_tensor(
                        hot[:, :, :, :].rearrange("p b n r -> p (b n) r"),
                        pos_f[:, c].rearrange("p b n -> p (b n)").unsqueeze(2)
                        .to_broadcast([P, TB * TOPK, TOPK]),
                        cst["iota"][:, 0:TOPK].unsqueeze(1).to_broadcast([P, TB * TOPK, TOPK]),
                        ALU.is_equal))
                    link(dve.tensor_tensor(
                        hot[:, :, :, :], hot[:, :, :, :],
                        idx_f[:, c].unsqueeze(2).to_broadcast([P, TB, TOPK, TOPK]), ALU.mult))
                    link(dve.tensor_reduce(picks[c][:, :, pl(h * TOPK, TOPK)], hot[:, :, :, :],
                                           AX.X, ALU.add))
                dve.wait_ge(exp_done, h + 1)
                link(dve.tensor_reduce(total[:, 0], gate[:, 1], AX.X, ALU.add))
                link(dve.reciprocal(total[:, 1], total[:, 0]))
                link(dve.tensor_tensor(picks[2][:, :, pl(h * TOPK, TOPK)], gate[:, 1],
                                       total[:, 1].unsqueeze(2).to_broadcast([P, TB, TOPK]),
                                       ALU.mult))
                count.leave(PH)



STEP = 8


def gate_table(nc, place, kb, kb_hot, picks, picksT, table, cst):
    passes = P // STEP
    half = STEP // 2
    with ExitStack() as ctx:
        def sem(name):
            return ctx.enter_context(nc.semaphore(f"table_{name}"))

        stage = place("table_stage", [P, 2, NK, P], F32, kb)
        first = place("table_first", [P, 2, half, NK], F32, kb_hot)
        second = place("table_second", [P, 2, half, NK], F32, kb_hot + 4)
        turned, turned_out = sem("turned"), sem("turned_out")
        hot_ready, banks_done, banks_out = sem("hot_ready"), sem("banks_done"), sem("banks_out")
        stored = [sem("stored0"), sem("stored1")]
        t_bank = [ctx.enter_context(nc.psum_tensor(f"table_t{b}", [P, TB, P], F32)) for b in range(3)]
        banks = [ctx.enter_context(nc.psum_tensor(f"table_b{b}", [P, half, NK], F32)) for b in range(2)]
        block = ctx.enter_context(nc.Block())

        @block.sync
        def _(sp):
            for tb in range(TB):
                sp.wait_ge(banks_out, 2 * passes * (tb + 1) + 2)
                sp.dma_start(table[:, :, tb * P:(tb + 1) * P].rearrange("i j t -> j i t"),
                             stage[:, tb % 2]).then_inc(stored[tb % 2], 16)
            for s in stored:
                sp.wait_ge(s, 16 * TB // 2)

        @block.tensor
        def _(pe):
            pe.sem_inc(banks_done, 2)
            for k in range(3):
                for tb in range(TB):
                    last = pe.transpose(t_bank[k][:, tb, :], picks[k][:, tb, :], cst["ident"][:, :])
                last.then_inc(turned, 1)
            for tb in range(TB):
                with pe.Fori(0, passes) as i:
                    for s in range(2):
                        n = i * 2 + (2 * passes * tb + s)
                        pe.wait_ge(hot_ready, n + 1)
                        pe.wait_ge(banks_out, n + 1)
                        for j in range(half):
                            last = pe.matmul(banks[s][:, j, :], second[:, s, j, :],
                                             first[:, s, j, :], start=True, stop=True)
                        last.then_inc(banks_done, 1)

        @block.vector
        def _(dve):
            for k in range(3):
                dve.wait_ge(turned, k + 1)
                dve.tensor_copy(picksT[k][:, :], t_bank[k][:, :, :].rearrange("p b t -> p (b t)"))\
                    .then_inc(turned_out, 1)
            dve.wait_ge(turned_out, 3)
            for tb in range(TB):
                with dve.Fori(0, passes) as i:
                    for s in range(2):
                        n = i * 2 + (2 * passes * tb + s)
                        dve.wait_ge(banks_done, n + 1)
                        for j in range(half):
                            t = i * STEP + (tb * P + s * half + j)
                            dve.tensor_scalar(first[:, s, j, :], cst["iota"][:, :],
                                              picksT[0][:, pl(t, 1)], None, ALU.is_equal)
                            last = dve.tensor_scalar(second[:, s, j, :], cst["iota"][:, :],
                                                     picksT[1][:, pl(t, 1)], picksT[2][:, pl(t, 1)],
                                                     ALU.is_equal, ALU.mult)
                        last.then_inc(hot_ready, 1)

        @block.scalar
        def _(act):
            act.sem_inc(banks_out, 2)
            for tb in range(TB):
                if tb >= 2:
                    act.wait_ge(stored[tb % 2], 16 * (tb // 2))
                with act.Fori(0, passes) as i:
                    for s in range(2):
                        n = i * 2 + (2 * passes * tb + s)
                        act.wait_ge(banks_done, n + 3)
                        act.copy(stage[:, tb % 2, :, pl(i * STEP + s * half, half)],
                                 banks[s][:, :, :].rearrange("p t i -> p i t"))\
                            .then_inc(banks_out, 1)



GROUPS = NK // 2
HALF_D = D // 2


def experts(nc, place, h, xT, u, v, table, out):
    with ExitStack() as ctx:
        def sem(name):
            return ctx.enter_context(nc.semaphore(f"exp_{name}"))

        uh = place("exp_uh", [P, 2, DC, P], F32R, 32)
        ul = place("exp_ul", [P, 2, DC, P], F32R, 48)
        xh = place("exp_xh", [P, DC, T], F32R, 64)
        xl = place("exp_xl", [P, DC, T], F32R, 96)
        vh = place("exp_vh", [P, 2, D], F32R, 128)
        vl = place("exp_vl", [P, 2, D], F32R, 144)
        ah = place("exp_ah", [P, 2, 2, T], F32R, 160)
        al = place("exp_al", [P, 2, 2, T], F32R, 168)
        raw = place("exp_raw", [P, 4, HALF_D], F32, 176)
        gates = place("exp_gates", [P, 2, T], F32, 192)
        act_f = place("exp_act", [P, 2, T], F32, 196)

        x_high, x_split = sem("x_high"), sem("x_split")
        loaded = [sem(f"loaded{n}") for n in range(4)]
        gates_in = [sem(f"gates_in{b}") for b in range(2)]
        high, low = sem("high"), sem("low")
        a_done, gelu_done, weighted, a_high, a_split = (sem("a_done"), sem("gelu_done"),
                                                        sem("weighted"), sem("a_high"), sem("a_split"))
        o_done, o_out, stored = sem("o_done"), sem("o_out"), sem("stored")
        a_bank = [ctx.enter_context(nc.psum_tensor(f"exp_a{b}", [P, T], F32)) for b in range(2)]
        o_bank = [ctx.enter_context(nc.psum_tensor(f"exp_o{b}", [P, PC], F32)) for b in range(D // PC)]
        block = ctx.enter_context(nc.Block())
        units = TB * (D // PC)

        def wait(eng, s, value):
            if not isinstance(value, int) or value > 0:
                eng.wait_ge(s, value)

        def run(eng, phase):
            last = GROUPS - 1
            phase("u", 0, 0, 0, ("u", 1))
            with eng.Fori(0, GROUPS // 2 - 1) as i:
                phase("u", i * 2 + 1, 1, i * 4 + 1, ("v", i * 2))
                phase("v", i * 2, 0, i * 4 + 2, ("u", i * 2 + 2))
                phase("u", i * 2 + 2, 0, i * 4 + 3, ("v", i * 2 + 1))
                phase("v", i * 2 + 1, 1, i * 4 + 4, ("u", i * 2 + 3))
            phase("u", last, 1, 2 * last - 1, ("v", last - 1))
            phase("v", last - 1, 0, 2 * last, ("v", last))
            phase("v", last, 1, 2 * last + 1, None)

        @block.sync
        def _(sp):
            def u_phase(g, parity, k):
                for n in range(4):
                    b, half = n // 2, n % 2
                    wait(sp, low, 4 * (k - 1) + (n + 1))
                    sp.dma_start(raw[:, n, :], u[g * 2 + b, :, half * HALF_D:(half + 1) * HALF_D])\
                        .then_inc(loaded[n], 16)
                for b in range(2):
                    wait(sp, weighted, 2 * g + (b - 1))
                    sp.dma_start(gates[:, b, :], table[g * 2 + b]).then_inc(gates_in[b], 16)

            def v_phase(g, parity, k):
                for n in range(4):
                    b, half = n // 2, n % 2
                    wait(sp, low, 4 * (k - 1) + (n + 1))
                    sp.dma_start(raw[:, n, :], v[g * 2 + b, :, half * HALF_D:(half + 1) * HALF_D])\
                        .then_inc(loaded[n], 16)

            run(sp, lambda kind, g, parity, k, after:
                (u_phase if kind == "u" else v_phase)(g, parity, k))
            sp.wait_ge(o_out, units * GROUPS + 4)
            sp.dma_start(out.rearrange("(b p) d -> p b d", p=P), h[:, :, :]).then_inc(stored, 16)
            sp.wait_ge(stored, 16)

        @block.tensor
        def _(pe):
            def u_phase(g, parity, k):
                for b in range(2):
                    wait(pe, gelu_done, g * 2 + (b - 1))
                    for c in range(DC):
                        if c % (DC // 2) == 0:
                            pe.wait_ge(low, 4 * k + (2 * b + c // (DC // 2) + 1))
                        pe.matmul(a_bank[b][:, :], uh[:, b, c, :], xh[:, c, :],
                                  start=(c == 0), stop=False)
                        pe.matmul(a_bank[b][:, :], uh[:, b, c, :], xl[:, c, :],
                                  start=False, stop=False)
                        last = pe.matmul(a_bank[b][:, :], ul[:, b, c, :], xh[:, c, :],
                                         start=False, stop=(c == DC - 1))
                    last.then_inc(a_done, 1)

            def v_phase(g, parity, k):
                pe.wait_ge(low, 4 * k + 4)
                pe.wait_ge(a_split, g * 2 + 2)
                for n in range(units):
                    tb, dc = n // 4, n % 4
                    tokens, cols = slice(tb * P, (tb + 1) * P), slice(dc * PC, (dc + 1) * PC)
                    pe.wait_ge(o_out, g * units + (n + 1))
                    for b in range(2):
                        pe.matmul(o_bank[dc][:, :], ah[:, parity, b, tokens], vh[:, b, cols],
                                  start=(b == 0), stop=False)
                        pe.matmul(o_bank[dc][:, :], ah[:, parity, b, tokens], vl[:, b, cols],
                                  start=False, stop=False)
                        last = pe.matmul(o_bank[dc][:, :], al[:, parity, b, tokens], vh[:, b, cols],
                                         start=False, stop=(b == 1))
                    last.then_inc(o_done, 1)

            pe.wait_ge(x_split, DC)
            run(pe, lambda kind, g, parity, k, after:
                (u_phase if kind == "u" else v_phase)(g, parity, k))

        @block.scalar
        def _(act):
            for c in range(DC):
                act.copy(xh[:, c, :], xT[:, c, :]).then_inc(x_high, 1)
            act.wait_ge(x_split, DC)

            def split_high(kind, g, k, n):
                if n == 0:
                    wait(act, a_done if kind == "u" else o_done, g * (2 if kind == "u" else units))
                act.wait_ge(loaded[n], 16 * (k + 1))
                act.copy(part(uh if kind == "u" else vh, kind, n), raw[:, n, :]).then_inc(high, 1)

            def phase(kind, g, parity, k, after):
                late = after is None or kind == after[0]
                if kind == "u":
                    for b in range(2):
                        if not late:
                            split_high(*after, k + 1, 2 * b)
                            split_high(*after, k + 1, 2 * b + 1)
                        act.wait_ge(a_done, g * 2 + (b + 1))
                        wait(act, a_split, g * 2 + (b - 1))
                        act.activation(act_f[:, b, :], a_bank[b][:, :], ACT.Gelu_apprx_tanh)\
                            .then_inc(gelu_done, 1)
                if (late or kind == "v") and after is not None:
                    for n in range(4):
                        split_high(*after, k + 1, n)

            for n in range(4):
                split_high("u", 0, 0, n)
            run(act, phase)

        @block.vector
        def _(dve):
            dve.sem_inc(o_out, 4)
            for c in range(DC):
                dve.wait_ge(x_high, c + 1)
                dve.tensor_tensor(xl[:, c, :], xT[:, c, :], xh[:, c, :].bitcast(F32), ALU.subtract)\
                    .then_inc(x_split, 1)
            dve.wait_ge(x_split, DC)

            def split_low(kind, g, k, n):
                dve.wait_ge(high, 4 * k + (n + 1))
                dve.tensor_tensor(part(ul if kind == "u" else vl, kind, n), raw[:, n, :],
                                  part(uh if kind == "u" else vh, kind, n).bitcast(F32), ALU.subtract)\
                    .then_inc(low, 1)

            def phase(kind, g, parity, k, after):
                late = after is None or kind == after[0]
                if kind == "u":
                    for b in range(2):
                        if not late:
                            split_low(*after, k + 1, 2 * b)
                            split_low(*after, k + 1, 2 * b + 1)
                        dve.wait_ge(gelu_done, g * 2 + (b + 1))
                        dve.wait_ge(gates_in[b], 16 * (g + 1))
                        dve.tensor_tensor(act_f[:, b, :], act_f[:, b, :], gates[:, b, :], ALU.mult)\
                            .then_inc(weighted, 1)
                        dve.wait_ge(weighted, g * 2 + (b + 1))
                        wait(dve, o_done, (g - 1) * units)
                        dve.tensor_copy(ah[:, parity, b, :], act_f[:, b, :]).then_inc(a_high, 1)
                        dve.wait_ge(a_high, g * 2 + (b + 1))
                        dve.tensor_tensor(al[:, parity, b, :], act_f[:, b, :],
                                          ah[:, parity, b, :].bitcast(F32), ALU.subtract)\
                            .then_inc(a_split, 1)
                else:
                    for n in range(units):
                        tb, dc = n // 4, n % 4
                        dve.wait_ge(o_done, g * units + (n + 1))
                        sums = h[:, tb, dc * PC:(dc + 1) * PC]
                        dve.tensor_tensor(sums, sums, o_bank[dc][:, :], ALU.add).then_inc(o_out, 1)
                        if n % 4 == 2 and not late:
                            split_low(*after, k + 1, n // 4)
                if late and after is not None:
                    for n in range(4):
                        split_low(*after, k + 1, n)

            for n in range(4):
                split_low("u", 0, 0, n)
            run(dve, phase)


def part(tile, kind, n):
    b, half = n // 2, n % 2
    if kind == "u":
        return tile[:, b, half * (DC // 2):(half + 1) * (DC // 2), :].rearrange("p c e -> p (c e)")
    return tile[:, b, half * HALF_D:(half + 1) * HALF_D]




def shape_constants():
    pos = np.arange(L, dtype=np.float32)
    inv = (np.float32(500000.0) ** (-np.arange(0, ROPE, 2, dtype=np.float32) / np.float32(ROPE)))
    ang = pos[:, None] * inv.astype(np.float32)[None, :]
    cos, sin = np.cos(ang).astype(np.float32), np.sin(ang).astype(np.float32)
    row = np.arange(P)[:, None]
    col = np.arange(P)[None, :]
    prev = np.where(col > row, 0.0, NEG)
    own = np.where(col <= row, 0.0, NEG)
    meta = np.zeros((P, M))
    return {
        "iota": np.broadcast_to(np.arange(P, dtype=np.float32), (P, P)),
        "ident": np.eye(P, dtype=np.float32),
        "cos": cos[M:].reshape(TB, P, HALF).transpose(1, 0, 2),
        "sin": sin[M:].reshape(TB, P, HALF).transpose(1, 0, 2),
        "meta_cos": cos[:M],
        "meta_sin": sin[:M],
        "mask": np.concatenate([meta, prev, own], 1).astype(np.float32),
        "keep": np.broadcast_to(((np.arange(L) % P != M) & (np.arange(L) > 0)).astype(np.float32), (P, L)),
        "level_mask": np.stack([(row // (P >> l) == col // (P >> l)) & (row % (P >> l) < (P >> (l + 1)))
                                & (col % (P >> l) >= (P >> (l + 1))) for l in range(LEVELS)],
                               1).astype(np.float32),
        "mask_first": np.concatenate([meta, own], 1).astype(np.float32),
    }



def build(nc, a, out):
    place = Place(nc)
    h = place("h", [P, TB, D], F32, 0)
    mix = place("mix", [P, TB, D], F32, 0)
    hnT = place("hnT", [P, DC, L], F32, 0)
    w = place("w", [P, 2, DC, PC], F32, 33)
    nat = place("nat", [P, NAT_PIECES, TB, PC], F32, 97)
    nat_meta = place("nat_meta", [M, META_PIECES, PC], F32, 153)
    turned = place("turned", [P, 2 * RH, L], F32, 159)
    mixT = place("mixT", [P, DC, T], F32, 97)
    x_rows = place("x_rows", [P, TB, D], F32, 97)
    meta_rows = place("meta_rows", [M, D], F32, 129)
    xT = place("xT", [P, DC, T], F32, 32)
    picks = [place(f"picks{k}", [P, TB, P], F32, 130 + 2 * k) for k in range(3)]
    picksT = [place(f"picksT{k}", [P, T], F32, 193 + 2 * k) for k in range(3)]
    sub_keys = place("sub_keys", [P, HC, NK], F32, 136)
    table = nc.dram_tensor("gate_table", [NK, NK, T], F32, kind="Internal").ap()

    cst, kb = {}, 192.0
    sources = []
    for name, shape, dtype in CONSTANTS:
        cst[name] = place(f"c_{name}", shape, dtype, kb)
        kb += -(-int(np.prod(shape[1:])) * mybir.dt.size(dtype) // 4) * 4 / KB
        src = a[name]
        sources.append((cst[name], src.partition_broadcast(P) if name in ROWS else src))
    assert kb < 207.8, kb
    cst["sub_keys"] = sub_keys

    w_loaded = [nc.alloc_semaphore("w_loaded0"), nc.alloc_semaphore("w_loaded1")]
    keys_loaded = nc.alloc_semaphore("sub_keys_loaded")

    with nc.semaphore("consts_loaded") as loaded, nc.Block() as block:
        @block.sync
        def _(sp):
            for dst, src in sources:
                sp.dma_start(dst[:], src).then_inc(loaded, 16)
            sp.wait_ge(loaded, 16 * len(sources))

    def first_pieces(sp):
        load_piece(sp, 0, a["w_in"], w, w_loaded)
        load_piece(sp, 1, a["w_in"], w, w_loaded)

    def load_keys(sp):
        sp.dma_start(sub_keys[:], a["sub_keys"]).then_inc(keys_loaded, 16)
        sp.wait_ge(keys_loaded, 16)

    rows = [(x_rows[:, tb, :], P, M + tb * P, a["x"][tb * P:(tb + 1) * P, :]) for tb in range(TB)]
    norm_rows(nc, "mixnorm", [(meta_rows[:, :], M, 0, a["meta"])] + rows, cst["ln_mix"], hnT,
              cst["ident"], place, 137, first_pieces)
    project(nc, a["w_in"], w, w_loaded, hnT, nat, nat_meta, turned)
    attend(nc, place, 33, nat, nat_meta, mix, cst)
    recur(nc, place, 33, nat, nat_meta, turned, mix, cst)
    mix_out(nc, place, a["w_out"], w, mix, mixT, h, a["x"], cst)
    norm_rows(nc, "ffnnorm", [(h[:, tb, :], P, tb * P, None) for tb in range(TB)], cst["ln_ffn"],
              xT, cst["ident"], place, 64, load_keys)
    route(nc, place, 64, a["w_q"], xT, picks, cst)
    gate_table(nc, place, 64, 199, picks, picksT, table, cst)
    experts(nc, place, h, xT, a["u"], a["v"], table, out)


CONSTANTS = [
    ("ident", [P, P], F32), ("iota", [P, P], F32), ("ln_mix", [P, DC], F32), ("ln_ffn", [P, DC], F32),
    ("cos", [P, TB, HALF], F32), ("sin", [P, TB, HALF], F32),
    ("meta_cos", [M, HALF], F32), ("meta_sin", [M, HALF], F32),
    ("mask", [P, KEYS], F32), ("mask_first", [P, M + P], F32), ("qk_gain", [P, GROUP + 1, HD], F32),
    ("sinks", [P, QH], F32), ("keep", [P, L], F32), ("level_mask", [P, LEVELS, P], F32),
    ("lb_logits", [P, 2, RH], F32), ("hgrn_gain", [P, RH * HD], F32),
]
ROWS = ("iota", "qk_gain", "sinks", "keep", "hgrn_gain")


def turn_rows(w, pieces, cols):
    return w.reshape(DC, P, pieces, cols).transpose(2, 1, 0, 3)


def kernel(**inputs):
    import concourse.bacc as bacc
    from concourse.bass_utils import run_bass_kernel_spmd

    i = {name: np.asarray(value) for name, value in inputs.items()}
    shapes = shape_constants()
    q_gain, k_gain = i["q_norm_g"][0], i["k_norm_g"][0]
    arrays = {
        **shapes,
        "iota": shapes["iota"][0],
        "keep": shapes["keep"][0],
        "x": i["x"][0],
        "meta": i["meta_tokens"],
        "ln_mix": i["ln_mix_g"][0].reshape(DC, P).T,
        "ln_ffn": i["ln_ffn_g"][0].reshape(DC, P).T,
        "qk_gain": np.stack([q_gain] * GROUP + [k_gain]),
        "sinks": i["attn_sinks"][0],
        "lb_logits": i["hgrn_lb_logits"].reshape(2, RH, P).transpose(2, 0, 1),
        "hgrn_gain": i["hgrn_norm_g"][0],
        "w_in": turn_rows(i["w_in"][0], PIECES, PC)[ORDER],
        "w_out": turn_rows(i["w_out"][0], OUT_PIECES, PC),
        "w_q": turn_rows(i["peer_w_q"][0], PH, WQ),
        "sub_keys": i["peer_sub_keys"][0].reshape(HC, NK, P).transpose(2, 0, 1),
        "u": i["peer_u"][0].reshape(NK, NK, DC, P).transpose(0, 3, 2, 1).reshape(NK, P, D),
        "v": i["peer_v"][0].reshape(NK, NK, D),
    }
    arrays = {f"in_{name}": np.ascontiguousarray(value) for name, value in arrays.items()}
    nc = bacc.Bacc("TRN2", target_bir_lowering=False, num_devices=1)
    aps = {name[3:]: nc.dram_tensor(name, value.shape, mybir.dt.from_np(value.dtype),
                                    kind="ExternalInput").ap() for name, value in arrays.items()}
    out = nc.dram_tensor("out_dram", [T, D], F32, kind="ExternalOutput").ap()
    build(nc, aps, out)
    result = run_bass_kernel_spmd(nc, [arrays], core_ids=[0])
    return result.results[0]["out_dram"].reshape(1, T, D)
```

```python
from contextlib import ExitStack

import numpy as np

import concourse.bass as bass
from concourse import mybir

ALU = mybir.AluOpType
ACT = mybir.ActivationFunctionType
AX = mybir.AxisListType
F32 = mybir.dt.float32
F32R = mybir.dt.float32r
U32 = mybir.dt.uint32
U8 = mybir.dt.uint8

P = 128
D = 2048
DC = D // P
T = 512
TB = T // P
M = 16
L = M + T
HD = 128
QH, KVH = 8, 2
GROUP = QH // KVH
RH = 8
ROPE = 32
HALF = ROPE // 2
EPS = 1e-6
SCALE = HD ** -0.5
BAND = 2 * P
KEYS = M + BAND
NEG = -1e30
LEVELS = 7
PH, NK, TOPK = 8, 128, 16
PC = 512
KB = 1024
BASE = 16512


class Count:

    def __init__(self, eng, sem):
        self.eng, self.sem, self.n, self.reg, self.per = eng, sem, 0, None, 0

    def up(self, ins):
        ins.then_inc(self.sem, 1)
        self.n += 1

    def link(self, ins):
        self.up(ins)
        self.wait()

    def wait(self):
        self.eng.wait_ge(self.sem, self.n if self.reg is None else self.reg * self.per + self.n)

    def enter(self, reg, per):
        self.reg, self.per, self.start = reg, per, self.n

    def leave(self, trips):
        assert self.n - self.start == self.per, (self.n - self.start, self.per)
        self.n = self.start + trips * self.per
        self.reg = None


class Place:

    def __init__(self, nc):
        self.nc = nc

    def __call__(self, name, shape, dtype, kb):
        off = BASE + int(round(kb * KB))
        assert off % 4 == 0
        return self.nc.alloc_sbuf_tensor_at(name, shape, dtype, offset=off)


def inverse_root(dve, link, out, square, root, spare):
    link(dve.reciprocal(out, root))
    link(dve.tensor_tensor(spare, out, out, ALU.mult))
    link(dve.tensor_tensor(spare, spare, square, ALU.mult))
    link(dve.tensor_scalar(spare, spare, -0.5, 1.5, ALU.mult, ALU.add))
    link(dve.tensor_tensor(out, out, spare, ALU.mult))




def norm_rows(nc, tag, tiles, gain, parts, ident, place, kb, first_loads=None, more_loads=None,
              consts=None, at_end=None):
    n = len(tiles)
    hi, lo = parts
    with ExitStack() as ctx:
        def sem(name):
            return ctx.enter_context(nc.semaphore(f"{tag}_{name}"))

        loaded, summed, meaned, rooted = ([sem(f"loaded{i}") for i in range(n)], sem("summed"),
                                          sem("meaned"), sem("rooted"))
        scaled, turned, emptied, chain = sem("scaled"), sem("turned"), sem("emptied"), sem("chain")
        high, low = sem("high"), sem("low")
        scaled_rows = place(f"{tag}_scaled_rows", [P, 2, D], F32, kb)
        squares = place(f"{tag}_squares", [P, D], F32, kb + 16)
        stat = place(f"{tag}_stat", [P, 4, 8], F32, kb + 24)
        whole = place(f"{tag}_whole", [P, 4, 4, P], F32, kb + 25)
        banks = [ctx.enter_context(nc.psum_tensor(f"{tag}_bank{b}", [P, 4, P], F32)) for b in range(4)]
        block = ctx.enter_context(nc.Block())
        groups = DC // 4

        @block.sync
        def _(sp):
            if first_loads:
                first_loads(sp)
            for i, (rows, m, col, src) in enumerate(tiles):
                if src is not None:
                    sp.dma_start(rows, src).then_inc(loaded[i], 16)
            if more_loads:
                more_loads(sp)

        @block.scalar
        def _(act):
            act.wait_ge(chain, 1)
            for i, (rows, m, col, src) in enumerate(tiles):
                if src is not None:
                    act.wait_ge(loaded[i], 16)
                if i:
                    act.wait_ge(summed, i)
                act.activation(squares[0:m, :], rows, ACT.Square,
                               accum_out=stat[0:m, 0, i:i + 1]).then_inc(summed, 1)
            act.wait_ge(meaned, 1)
            act.activation(stat[:, 2, 0:n], stat[:, 1, 0:n], ACT.Sqrt).then_inc(rooted, 1)
            for i, (rows, m, col, src) in enumerate(tiles):
                for g in range(groups):
                    k = i * groups + g
                    act.wait_ge(emptied, k + 1)
                    act.copy(hi[:, 4 * g:4 * g + 4, col:col + m], whole[:, k % 4, :, 0:m])\
                        .then_inc(high, 1)

        @block.gpsimd
        def _(pool):
            for i, (rows, m, col, src) in enumerate(tiles):
                for g in range(groups):
                    k = i * groups + g
                    pool.wait_ge(high, k + 1)
                    pool.tensor_tensor(lo[:, 4 * g:4 * g + 4, col:col + m], whole[:, k % 4, :, 0:m],
                                       hi[:, 4 * g:4 * g + 4, col:col + m].bitcast(F32),
                                       ALU.subtract).then_inc(low, 1)

        def empty(dve, i):
            rows, m, col, src = tiles[i]
            for g in range(groups):
                k = i * groups + g
                dve.wait_ge(turned, k + 1)
                if k >= 4:
                    dve.wait_ge(low, k - 3)
                dve.tensor_tensor(whole[:, k % 4, :, 0:m], banks[k % 4][:, :, 0:m],
                                  gain[:, 4 * g:4 * g + 4].unsqueeze(2).to_broadcast([P, 4, m]),
                                  ALU.mult).then_inc(emptied, 1)

        @block.vector
        def _(dve):
            link = Count(dve, chain).link
            link(dve.memset(stat[:, 0, :], 1.0))
            if consts:
                dve.wait_ge(*consts)
            dve.wait_ge(summed, n)
            dve.tensor_scalar(stat[:, 1, 0:n], stat[:, 0, 0:n], 1.0 / D, EPS,
                              ALU.mult, ALU.add).then_inc(meaned, 1)
            dve.wait_ge(rooted, 1)
            inverse_root(dve, link, stat[:, 3, 0:n], stat[:, 1, 0:n], stat[:, 2, 0:n], stat[:, 0, 0:n])
            for i, (rows, m, col, src) in enumerate(tiles):
                if i >= 2:
                    dve.wait_ge(turned, groups * (i - 1))
                dve.tensor_scalar(scaled_rows[0:m, i % 2, :], rows, stat[0:m, 3, i:i + 1], None,
                                  ALU.mult).then_inc(scaled, 1)
                if i == 0:
                    continue
                empty(dve, i - 1)
            empty(dve, n - 1)
            if at_end:
                at_end(dve)

        @block.tensor
        def _(pe):
            if consts:
                pe.wait_ge(*consts)
            for i, (rows, m, col, src) in enumerate(tiles):
                pe.wait_ge(scaled, i + 1)
                for g in range(groups):
                    k = i * groups + g
                    if k >= 4:
                        pe.wait_ge(emptied, k - 3)
                    for j in range(4):
                        c = 4 * g + j
                        last = pe.transpose(banks[k % 4][:, j, 0:m],
                                            scaled_rows[0:m, i % 2, c * P:(c + 1) * P],
                                            ident[0:m, 0:m])
                    last.then_inc(turned, 1)



SPAN = 2
STEPS = DC // SPAN
RAW = 4


class Stream:

    def __init__(self, nc, tag, place, kb, src):
        self.src = src
        self.raw = place(f"{tag}_raw", [P, RAW, SPAN, PC], F32, kb)
        self.hi = place(f"{tag}_hi", [P, 2, SPAN, PC], F32R, kb + 16)
        self.lo = place(f"{tag}_lo", [P, 2, SPAN, PC], F32R, kb + 24)
        self.loaded = [nc.alloc_semaphore(f"{tag}_loaded{i}") for i in range(RAW)]
        self.high, self.low, self.used = (nc.alloc_semaphore(f"{tag}_{name}")
                                          for name in ("high", "low", "used"))

    def load(self, sp, p, g, ahead=False):
        if not ahead:
            sp.wait_ge(self.low, p * STEPS + (g - RAW + 1))
        sp.dma_start(self.raw[:, g % RAW], self.src[p, :, g * SPAN:(g + 1) * SPAN, :])\
            .then_inc(self.loaded[g % RAW], 16)

    def load_start(self, sp):
        for g in range(RAW):
            self.load(sp, 0, g, ahead=True)

    def load_rest(self, sp, pieces):
        for g in range(RAW, STEPS):
            self.load(sp, 0, g)
        with sp.Fori(1, pieces) as p:
            for g in range(STEPS):
                self.load(sp, p, g)

    def split_high(self, act, p, g):
        act.wait_ge(self.loaded[g % RAW], p * (16 * STEPS // RAW) + 16 * (g // RAW + 1))
        act.wait_ge(self.used, p * STEPS + (g + 1))
        act.copy(self.hi[:, g % 2], self.raw[:, g % RAW]).then_inc(self.high, 1)

    def split_low(self, eng, p, g):
        eng.wait_ge(self.high, p * STEPS + (g + 1))
        eng.tensor_tensor(self.lo[:, g % 2], self.raw[:, g % RAW], self.hi[:, g % 2].bitcast(F32),
                          ALU.subtract).then_inc(self.low, 1)

    def split_low_all(self, eng, pieces):
        with eng.Fori(0, pieces) as p:
            for g in range(STEPS):
                self.split_low(eng, p, g)

    def start_free(self, pe):
        pe.sem_inc(self.used, 2)

    def await_step(self, pe, p, g):
        pe.wait_ge(self.low, p * STEPS + (g + 1))

    def release(self, ins):
        ins.then_inc(self.used, 1)

    def await_piece(self, eng, p):
        eng.wait_ge(self.used, p * STEPS + (STEPS + 2))

    def parts(self, g, c):
        return self.hi[:, g % 2, c], self.lo[:, g % 2, c]


def product(pe, out, left, right, first, last):
    pe.matmul(out, left[0], right[0], start=first, stop=False)
    pe.matmul(out, left[1], right[0], start=False, stop=False)
    return pe.matmul(out, left[0], right[1], start=False, stop=last)



META_PIECES, PLAIN_PIECES, TURNED_PIECES = 3, 4, 4
NAT_PIECES = META_PIECES + PLAIN_PIECES
PIECES = NAT_PIECES + TURNED_PIECES
ORDER = [2, 7, 8, 0, 1, 9, 10, 3, 4, 5, 6]
KV_PIECE, HI_PIECE, Q_PIECE, HG_PIECE = 0, 1, 3, 5


def project(nc, stream, hn, nat, nat_meta, turned):
    with ExitStack() as ctx:
        def sem(name):
            return ctx.enter_context(nc.semaphore(f"proj_{name}"))

        unit_done = sem("unit_done")
        even_free, odd_free, meta_free = sem("even_free"), sem("odd_free"), sem("meta_free")
        banks = [ctx.enter_context(nc.psum_tensor(f"proj_bank{b}", [P, PC], F32)) for b in range(4)]
        meta_bank = [ctx.enter_context(nc.psum_tensor(f"proj_meta{b}", [P, PC], F32))
                     for b in range(4)]
        block = ctx.enter_context(nc.Block())

        def halves(tokens, c):
            return [part[:, c, tokens] for part in hn]

        def tile(tb):
            return slice(M + tb * P, M + (tb + 1) * P)

        @block.sync
        def _(sp):
            stream.load_rest(sp, PIECES)

        @block.gpsimd
        def _(pool):
            stream.split_low_all(pool, PIECES)

        @block.tensor
        def _(pe):
            stream.start_free(pe)

            def bank_wait(p, b):
                pe.wait_ge((even_free, odd_free)[b % 2], p * 2 + (b // 2 + 1))

            def natural(p, with_meta):
                for g in range(STEPS):
                    stream.await_step(pe, p, g)
                    for s in range(SPAN):
                        c = g * SPAN + s
                        w = stream.parts(g, s)
                        for tb in range(TB):
                            if c == 0:
                                bank_wait(p, tb)
                            last = product(pe, banks[tb][:, :], halves(tile(tb), c), w,
                                           c == 0, c == DC - 1)
                            if c == DC - 1 and tb < TB - 1:
                                last.then_inc(unit_done, 1)
                        if with_meta:
                            if c == 0:
                                pe.wait_ge(meta_free, p + 1)
                            last = product(pe, meta_bank[0][0:M, :], halves(slice(0, M), c), w,
                                           c == 0, c == DC - 1)
                    stream.release(last)

            with pe.Fori(0, META_PIECES) as p:
                natural(p, True)
            with pe.Fori(META_PIECES, NAT_PIECES) as p:
                natural(p, False)
            with pe.Fori(NAT_PIECES, PIECES) as p:
                for g in range(STEPS):
                    stream.await_step(pe, p, g)
                    for s in range(SPAN):
                        c = g * SPAN + s
                        for cb in range(4):
                            w = [part[:, cb * P:(cb + 1) * P] for part in stream.parts(g, s)]
                            if c == 0:
                                bank_wait(p, cb)
                            if c == 0 and cb == 0:
                                pe.wait_ge(meta_free, p - (NAT_PIECES - META_PIECES - 1))
                            last = product(pe, banks[cb][:, :], w, halves(slice(M, L), c),
                                           c == 0, c == DC - 1)
                            if c == DC - 1 and cb < 3:
                                last.then_inc(unit_done, 1)
                            last = product(pe, meta_bank[cb][:, 0:M], w, halves(slice(0, M), c),
                                           c == 0, c == DC - 1)
                    stream.release(last)

        @block.vector
        def _(dve):
            dve.sem_inc(even_free, 2)
            with dve.Fori(0, NAT_PIECES) as p:
                for tb in (0, 2):
                    dve.wait_ge(unit_done, p * 3 + (tb + 1))
                    dve.tensor_copy(nat[:, p, tb, :], banks[tb][:, :]).then_inc(even_free, 1)
            with dve.Fori(NAT_PIECES, PIECES) as p:
                for cb in (0, 2):
                    dve.wait_ge(unit_done, p * 3 + (cb + 1))
                    dve.tensor_copy(turned[:, p * 4 + (cb - 4 * NAT_PIECES), M:L], banks[cb][:, :])\
                        .then_inc(even_free, 1)

        @block.scalar
        def _(act):
            act.sem_inc(odd_free, 2)
            act.sem_inc(meta_free, 1)

            def await_bank(p, b):
                if b == 1:
                    act.wait_ge(unit_done, p * 3 + 2)
                else:
                    stream.await_piece(act, p)

            def empty_natural(p, with_meta):
                for tb in (1, 3):
                    await_bank(p, tb)
                    act.copy(nat[:, p, tb, :], banks[tb][:, :]).then_inc(odd_free, 1)
                if with_meta:
                    act.copy(nat_meta[:, p, :], meta_bank[0][0:M, :]).then_inc(meta_free, 1)

            def empty_turned(p):
                for cb in (1, 3):
                    await_bank(p, cb)
                    act.copy(turned[:, p * 4 + (cb - 4 * NAT_PIECES), M:L], banks[cb][:, :])\
                        .then_inc(odd_free, 1)
                for cb in range(4):
                    last = act.copy(turned[:, p * 4 + (cb - 4 * NAT_PIECES), 0:M],
                                    meta_bank[cb][:, 0:M])
                last.then_inc(meta_free, 1)

            def run(first, end, empty):
                with act.Fori(first, end) as p:
                    for g in range(1, STEPS):
                        stream.split_high(act, p, g)
                    stream.split_high(act, p + 1, 0)
                    empty(p)

            stream.split_high(act, 0, 0)
            run(0, META_PIECES, lambda p: empty_natural(p, True))
            run(META_PIECES, NAT_PIECES, lambda p: empty_natural(p, False))
            run(NAT_PIECES, PIECES - 1, empty_turned)
            for g in range(1, STEPS):
                stream.split_high(act, PIECES - 1, g)
            empty_turned(PIECES - 1)


def pl(start, count):
    return bass.ds(start, count)




def attend(nc, place, kb, nat, nat_meta, mix, cst):
    units = GROUP * TB
    qk = GROUP + 1
    with ExitStack() as ctx:
        def sem(name):
            return ctx.enter_context(nc.semaphore(f"att_{name}"))

        def bank(name, shape):
            return ctx.enter_context(nc.psum_tensor(f"att_{name}", shape, F32))

        rows = place("att_rows", [P, TB, qk, HD], F32, kb)
        squares = place("att_squares", [P, TB, qk, HD], F32, kb + 10)
        qT = place("att_qT", [P, GROUP, T], F32, kb + 20)
        kT = place("att_kT", [P, L], F32, kb + 28)
        logits = place("att_logits", [P, 2, KEYS], F32, kb + 31)
        probs = place("att_probs", [P, 2, KEYS], F32, kb + 34)
        probsT = place("att_probsT", [P, 2, 2, P], F32, kb + 37)
        probsT_meta = place("att_probsT_meta", [M, 2, P], F32, kb + 39)
        rows_meta = place("att_rows_meta", [M, 2, HD], F32, kb + 40)
        rot = place("att_rot", [P, 2, TB, qk, HALF], F32, kb + 41)
        stat = place("att_stat", [P, 4, TB * qk + 1], F32, kb + 44)
        soft = place("att_soft", [P, 6, units], F32, kb + 44.5)
        sink = place("att_sink", [P, GROUP], F32, kb + 45)
        top, neg_top, den, sink_exp, inv = (soft[:, k, :] for k in range(5))

        squared, meaned, rooted, rows_ready = (sem("squared"), sem("meaned"), sem("rooted"),
                                               sem("rows_ready"))
        chain, turned, turned_out, key_out = sem("chain"), sem("turned"), sem("turned_out"), sem("key_out")
        scores_done, scores_free, soft_ready = sem("scores_done"), sem("scores_free"), sem("soft_ready")
        exp_done, probs_turned, probs_out = sem("exp_done"), sem("probs_turned"), sem("probs_out")
        out_done, out_free = sem("out_done"), sem("out_free")
        prep_bank = [bank(f"prep{b}", [P, TB, P]) for b in range(2)]
        s_bank = [bank(f"s{b}", [P, PC]) for b in range(2)]
        t_bank = [bank(f"t{b}", [P, 3, P]) for b in range(2)]
        o_bank = [bank(f"o{b}", [P, HD]) for b in range(2)]
        block = ctx.enter_context(nc.Block())

        def heads(u):
            return u // TB, u % TB

        @block.scalar
        def _(act):
            with act.Fori(0, KVH) as g:
                act.wait_ge(rows_ready, g)
                act.activation(squares[:, :, 0:GROUP, :],
                               nat[:, Q_PIECE + g, :, :].rearrange("p t (h d) -> p t h d", d=HD),
                               ACT.Square).then_inc(squared, 1)
                act.activation(squares[:, :, GROUP, :], nat[:, KV_PIECE, :, pl(g * HD, HD)],
                               ACT.Square).then_inc(squared, 1)
                act.activation(rows_meta[:, 1, :], nat_meta[:, KV_PIECE, pl(g * HD, HD)],
                               ACT.Square).then_inc(squared, 1)
                act.wait_ge(meaned, g + 1)
                act.activation(stat[:, 2, :], stat[:, 1, :], ACT.Sqrt).then_inc(rooted, 1)
                for k in range(qk):
                    act.wait_ge(turned, g * qk + k + 1)
                    if k == 0:
                        act.wait_ge(out_done, g * units)
                    if k < GROUP:
                        act.copy(qT[:, k, :], prep_bank[k % 2][:, :, :].rearrange("p t d -> p (t d)"))\
                            .then_inc(turned_out, 1)
                    else:
                        act.copy(kT[:, M:L], prep_bank[k % 2][:, :, :].rearrange("p t d -> p (t d)"))\
                            .then_inc(turned_out, 1)
                for s in range(units + 1):
                    if s < units:
                        act.wait_ge(soft_ready, g * units + s + 1)
                        if s >= 2:
                            act.wait_ge(probs_turned, g * units + s - 1)
                        h, n = heads(s)
                        keys = KEYS if n else M + P
                        act.activation(probs[:, s % 2, 0:keys], logits[:, s % 2, 0:keys], ACT.Exp,
                                       bias=neg_top[:, s:s + 1], accum_out=den[:, s:s + 1])\
                            .then_inc(exp_done, 1)
                        act.activation(sink_exp[:, s:s + 1], sink[:, h:h + 1], ACT.Exp,
                                       bias=neg_top[:, s:s + 1]).then_inc(exp_done, 1)
                    if s:
                        u = s - 1
                        act.wait_ge(probs_turned, g * units + u + 1)
                        if u >= 2:
                            act.wait_ge(out_done, g * units + u - 1)
                        act.copy(probsT_meta[:, u % 2, :], t_bank[u % 2][0:M, 2, :])
                        lo = 0 if u % TB else 1
                        act.copy(probsT[:, u % 2, lo:2, :], t_bank[u % 2][:, lo:2, :])\
                            .then_inc(probs_out, 1)

        @block.vector
        def _(dve):
            count = Count(dve, chain)
            link = count.link
            dve.sem_inc(scores_free, 2)
            dve.sem_inc(out_free, 2)
            link(dve.memset(stat[:, 0, :], 1.0))
            with dve.Fori(0, KVH) as g:
                count.enter(g, PREP_LINKS + 3 * units)
                dve.wait_ge(squared, 3 * g + 3)
                link(dve.tensor_reduce(stat[:, 0, 0:TB * qk],
                                       squares[:, :, :, :].rearrange("p t h d -> p (t h) d"),
                                       AX.X, ALU.add))
                link(dve.tensor_reduce(stat[0:M, 0, TB * qk:], rows_meta[:, 1, :], AX.X, ALU.add))
                dve.tensor_scalar(stat[:, 1, :], stat[:, 0, :], 1.0 / HD, EPS,
                                  ALU.mult, ALU.add).then_inc(meaned, 1)
                dve.wait_ge(rooted, g + 1)
                inverse_root(dve, link, stat[:, 3, :], stat[:, 1, :], stat[:, 2, :], stat[:, 0, :])
                link(dve.tensor_copy(sink[:, :], cst["sinks"][:, pl(g * GROUP, GROUP)]))
                rstd = stat[:, 3, 0:TB * qk].rearrange("p (t h) -> p t h", h=qk)
                for tb in range(TB):
                    dve.tensor_tensor(
                        rows[:, tb, 0:GROUP, :],
                        nat[:, Q_PIECE + g, tb, :].rearrange("p (h d) -> p h d", d=HD),
                        rstd[:, tb, 0:GROUP].unsqueeze(2).to_broadcast([P, GROUP, HD]), ALU.mult)
                link(dve.tensor_tensor(
                    rows[:, :, GROUP, :], nat[:, KV_PIECE, :, pl(g * HD, HD)],
                    rstd[:, :, GROUP:qk].to_broadcast([P, TB, HD]), ALU.mult))
                link(dve.tensor_tensor(
                    rows[:, :, :, :], rows[:, :, :, :],
                    cst["qk_gain"][:, :, :].unsqueeze(1).to_broadcast([P, TB, qk, HD]), ALU.mult))
                link(dve.scalar_tensor_tensor(
                    rows_meta[:, 0, :], nat_meta[:, KV_PIECE, pl(g * HD, HD)],
                    stat[0:M, 3, TB * qk:], cst["qk_gain"][0:M, GROUP, :], ALU.mult, ALU.mult))
                rotate(dve, link, rows[:, :, :, 0:HALF], rows[:, :, :, HALF:ROPE],
                       rot[:, 0], rot[:, 1],
                       cst["cos"][:, :, :].unsqueeze(2).to_broadcast([P, TB, qk, HALF]),
                       cst["sin"][:, :, :].unsqueeze(2).to_broadcast([P, TB, qk, HALF]))
                rotate(dve, link, rows_meta[:, 0, 0:HALF], rows_meta[:, 0, HALF:ROPE],
                       rot[0:M, 0, 0, 0, :], rot[0:M, 1, 0, 0, :],
                       cst["meta_cos"][:, :], cst["meta_sin"][:, :])
                dve.sem_inc(rows_ready, 1)
                dve.wait_ge(turned, g * qk + qk)
                dve.wait_ge(out_done, g * units)
                dve.tensor_copy(kT[:, 0:M], t_bank[0][:, 0, 0:M]).then_inc(key_out, 1)
                for s in range(units + 2):
                    if s < units:
                        h, n = heads(s)
                        keys = KEYS if n else M + P
                        mask = cst["mask"][:, 0:KEYS] if n else cst["mask_first"][:, :]
                        dve.wait_ge(scores_done, g * units + s + 1)
                        if s >= 2:
                            dve.wait_ge(exp_done, 2 * units * g + 2 * (s - 1))
                        dve.scalar_tensor_tensor(logits[:, s % 2, 0:keys], s_bank[s % 2][:, 0:keys],
                                                 SCALE, mask, ALU.mult, ALU.add)\
                            .then_inc(scores_free, 1)
                        dve.wait_ge(scores_free, g * units + s + 3)
                        link(dve.tensor_reduce(top[:, s:s + 1], logits[:, s % 2, 0:keys],
                                               AX.X, ALU.max))
                        dve.tensor_scalar(neg_top[:, s:s + 1], top[:, s:s + 1], sink[:, h:h + 1],
                                          -1.0, ALU.max, ALU.mult).then_inc(soft_ready, 1)
                    if 1 <= s <= units:
                        u = s - 1
                        dve.wait_ge(exp_done, 2 * units * g + 2 * (u + 1))
                        link(dve.tensor_tensor(inv[:, u:u + 1], den[:, u:u + 1],
                                               sink_exp[:, u:u + 1], ALU.add))
                        link(dve.reciprocal(inv[:, u:u + 1], inv[:, u:u + 1]))
                    if s >= 2:
                        u = s - 2
                        h, n = heads(u)
                        dve.wait_ge(out_done, g * units + u + 1)
                        dve.tensor_scalar(mix[:, n, pl(g * (GROUP * HD) + h * HD, HD)],
                                          o_bank[u % 2][:, :], inv[:, u:u + 1], None, ALU.mult)\
                            .then_inc(out_free, 1)
                count.leave(KVH)

        @block.tensor
        def _(pe):
            ident = cst["ident"]
            with pe.Fori(0, KVH) as g:
                pe.wait_ge(rows_ready, g + 1)
                for k in range(qk):
                    if k >= 2:
                        pe.wait_ge(turned_out, g * qk + k - 1)
                    for tb in range(TB):
                        last = pe.transpose(prep_bank[k % 2][:, tb, :], rows[:, tb, k, :],
                                            ident[:, :])
                    if k == GROUP:
                        last = pe.transpose(t_bank[0][:, 0, 0:M], rows_meta[:, 0, :],
                                            ident[0:M, 0:M])
                    last.then_inc(turned, 1)
                pe.wait_ge(turned_out, (g + 1) * qk)
                pe.wait_ge(key_out, g + 1)
                for s in range(units + 2):
                    if s < units:
                        h, n = heads(s)
                        pe.wait_ge(scores_free, g * units + s + 1)
                        q = qT[:, h, n * P:(n + 1) * P]
                        if n < 2:
                            keys = M + (n + 1) * P
                            last = pe.matmul(s_bank[s % 2][:, 0:keys], q, kT[:, 0:keys],
                                             start=True, stop=True)
                        else:
                            pe.matmul(s_bank[s % 2][:, 0:M], q, kT[:, 0:M], start=True, stop=True)
                            last = pe.matmul(s_bank[s % 2][:, M:KEYS], q,
                                             kT[:, M + (n - 1) * P:M + (n + 1) * P],
                                             start=True, stop=True)
                        last.then_inc(scores_done, 1)
                    if 1 <= s <= units:
                        u = s - 1
                        pe.wait_ge(exp_done, 2 * units * g + 2 * u + 1)
                        if u >= 2:
                            pe.wait_ge(probs_out, g * units + u - 1)
                        pe.transpose(t_bank[u % 2][0:M, 2, :], probs[:, u % 2, 0:M], ident[:, :])
                        if u % TB:
                            pe.transpose(t_bank[u % 2][:, 0, :], probs[:, u % 2, M:M + P], ident[:, :])
                            own = probs[:, u % 2, M + P:KEYS]
                        else:
                            own = probs[:, u % 2, M:M + P]
                        pe.transpose(t_bank[u % 2][:, 1, :], own, ident[:, :])\
                            .then_inc(probs_turned, 1)
                    if s >= 2:
                        u = s - 2
                        h, n = heads(u)
                        b = u % 2
                        pe.wait_ge(probs_out, g * units + u + 1)
                        pe.wait_ge(out_free, g * units + u + 1)
                        value = pl(g * HD + KVH * HD, HD)
                        pe.matmul(o_bank[b][:, :], probsT[:, b, 1, :],
                                  nat[:, KV_PIECE, n, value], start=True, stop=False)
                        if n:
                            pe.matmul(o_bank[b][:, :], probsT[:, b, 0, :],
                                      nat[:, KV_PIECE, n - 1, value], start=False, stop=False)
                        pe.matmul(o_bank[b][:, :], probsT_meta[:, b, :],
                                  nat_meta[:, KV_PIECE, value], start=False, stop=True)\
                            .then_inc(out_done, 1)


PREP_LINKS = 2 + 5 + 1 + 3 + 2 * 3


def rotate(dve, link, x1, x2, a, b, cos, sin):
    dve.tensor_tensor(a, x1, sin, ALU.mult)
    link(dve.tensor_tensor(b, x2, sin, ALU.mult))
    dve.tensor_tensor(x1, x1, cos, ALU.mult)
    link(dve.tensor_tensor(x2, x2, cos, ALU.mult))
    dve.tensor_tensor(x1, x1, b, ALU.subtract)
    link(dve.tensor_tensor(x2, x2, a, ALU.add))




def recur(nc, place, kb, nat, nat_meta, turned, mix, cst, stream):
    grams = LEVELS + 1
    with ExitStack() as ctx:
        def sem(name):
            return ctx.enter_context(nc.semaphore(f"rec_{name}"))

        def bank(name, shape):
            return ctx.enter_context(nc.psum_tensor(f"rec_{name}", shape, F32))

        keys = place("rec_keys", [P, RH, L], F32, kb)
        logs = place("rec_logs", [P, RH, L], F32, kb + 16.5)
        gaps = place("rec_gaps", [P, 2, T], F32, kb + 33)
        decays = place("rec_decays", [P, 2, T], F32, kb + 37)
        halves = place("rec_halves", [P, 2, T], F32, kb + 41)
        scores = place("rec_scores", [P, TB, P], F32, kb + 45)
        q_in = place("rec_q_in", [P, T], F32, kb + 47)
        k_out = place("rec_k_out", [P, L], F32, kb + 49)
        gap_out = place("rec_gap_out", [P, L], F32, kb + 51.5)
        k_now = place("rec_k_now", [P, T], F32, kb + 54)
        grown = place("rec_grown", [P, T], F32, kb + 56)
        k_outT = place("rec_k_outT", [P, TB, HD], F32, kb + 58)
        state = place("rec_state", [P, TB, HD], F32, kb + 60)
        lb = place("rec_lb", [P, 2, RH], F32, kb + 62)
        diff = place("rec_diff", [P, RH], F32, kb + 62.25)
        stat = place("rec_stat", [P, 4, TB * RH], F32, kb + 62.5)
        query, gate = turned[:, 0:RH, :], turned[:, RH:2 * RH, :]

        apart, bounded = sem("apart"), sem("bounded")
        opened, logged, bounds, summed = sem("opened"), sem("logged"), sem("bounds"), sem("summed")
        gap_ready, decay_ready, half_ready = sem("gap_ready"), sem("decay_ready"), sem("half_ready")
        gram_done, gram_out, copied = sem("gram_done"), sem("gram_out"), sem("k_now_copied")
        out_gap, edge_ready = sem("out_gap"), sem("edge_ready")
        in_out_ready, k_turned, k_turned_out = sem("in_out"), sem("k_turned"), sem("k_turned_out")
        update_done, state_ready = sem("update_done"), sem("state_ready")
        out_done, out_copied, mix_ready = sem("out_done"), sem("out_copied"), sem("mix_ready")
        squared, meaned, rooted, silu = sem("squared"), sem("meaned"), sem("rooted"), sem("silu")
        waited, pool_waited = sem("waited"), sem("pool_waited")
        g_bank = [bank(f"g{b}", [P, TB, P]) for b in range(2)]
        k_bank, u_bank = bank("k", [P, TB, P]), bank("u", [P, TB, HD])
        o_bank = bank("o", [P, TB, HD])
        block = ctx.enter_context(nc.Block())

        def value(h, c):
            return nat[:, h // 4 + HI_PIECE, c, pl((h % 4) * HD, HD)]

        def split(ap, l):
            return ap.rearrange("p (n s m) -> p n s m", s=2, m=P >> (l + 1))

        @block.sync
        def _(sp):
            sp.wait_ge(squared, 1)
            stream.load_start(sp)

        @block.gpsimd
        def _(pool):
            pool.wait_ge(logged, 1)
            pool.wait_ge(summed, 1)
            with pool.Fori(0, RH) as h:
                b_real = logs[:, h, M:L]

                def gap(l):
                    m = P >> (l + 1)
                    b, d = split(b_real, l), split(gaps[:, l % 2, :], l)
                    edge = b[:, :, 0, m - 1:m].to_broadcast([P, T // (2 * m), m])
                    if l >= 2:
                        pool.wait_ge(decay_ready, LEVELS * h + l - 1)
                    elif l == 0:
                        pool.wait_ge(decay_ready, LEVELS * h)
                    if l != 1:
                        pool.sem_inc(pool_waited, 1)
                    pool.tensor_tensor(d[:, :, 0, :], edge, b[:, :, 0, :], ALU.subtract)
                    pool.tensor_tensor(d[:, :, 1, :], b[:, :, 1, :], edge, ALU.subtract)\
                        .then_inc(gap_ready, 1)

                gap(0)
                gap(1)
                pool.wait_ge(gram_done, grams * h)
                pool.tensor_copy(k_now[:, :], keys[:, h, M:L]).then_inc(copied, 1)
                for l in range(2, LEVELS):
                    gap(l)

        @block.scalar
        def _(act):
            act.wait_ge(apart, 1)
            act.activation(lb[:, 0, :], diff[:, :], ACT.Sigmoid)
            act.activation(lb[:, 1, :], diff[:, :], ACT.Sigmoid, scale=-1.0).then_inc(bounded, 1)
            act.activation(logs[:, :, :], query, ACT.Sigmoid).then_inc(opened, 1)
            act.activation(keys[:, :, :], gate, ACT.Sigmoid, scale=-1.0).then_inc(opened, 1)
            act.wait_ge(opened, 2)
            act.activation(gate, gate, ACT.Sigmoid).then_inc(opened, 1)
            act.wait_ge(bounds, 1)
            act.activation(gate, gate, ACT.Ln).then_inc(logged, 1)
            act.wait_ge(summed, 1)

            def copy_out(h):
                act.wait_ge(out_done, h)
                act.copy(mix[:, :, pl(h * HD + (QH - 1) * HD, HD)], o_bank[:, :, :])\
                    .then_inc(out_copied, 1)

            def head(h, first):
                if not first:
                    act.wait_ge(state_ready, TB * h)
                act.activation(grown[:, :], logs[:, h, M:L], ACT.Exp).then_inc(edge_ready, 1)
                act.wait_ge(out_gap, h + 1)
                act.wait_ge(edge_ready, 2 * h + 1)
                if not first:
                    act.wait_ge(k_turned, h)
                act.activation(k_out[:, :], gap_out[:, :], ACT.Exp).then_inc(edge_ready, 1)
                for l in range(LEVELS):
                    b = l % 2
                    act.wait_ge(gap_ready, LEVELS * h + l + 1)
                    if l >= 2:
                        act.wait_ge(half_ready, LEVELS * h + l - 1)
                    act.activation(decays[:, b, :], gaps[:, b, :], ACT.Exp)\
                        .then_inc(decay_ready, 1)
                    if l == 1:
                        if not first:
                            copy_out(h)
                        act.wait_ge(k_turned, h + 1)
                        act.copy(k_outT[:, 0:TB - 1, :], k_bank[:, 0:TB - 1, :])
                        act.copy(k_outT[0:M, TB - 1, :], k_bank[0:M, TB - 1, :])\
                            .then_inc(k_turned_out, 1)

            head(0, True)
            with act.Fori(1, RH) as h:
                head(h, False)
            copy_out(RH)
            act.wait_ge(out_copied, RH)
            act.activation(logs_as_squares(logs), mix[:, :, QH * HD:], ACT.Square).then_inc(squared, 1)
            act.activation(keys_as_gates(keys), hg_view(nat), ACT.Sigmoid).then_inc(silu, 1)
            act.wait_ge(meaned, 1)
            act.activation(stat[:, 2, :], stat[:, 1, :], ACT.Sqrt).then_inc(rooted, 1)

        @block.tensor
        def _(pe):
            ident = cst["ident"]
            with pe.Fori(0, RH) as h:
                pe.wait_ge(copied, h + 1)
                pe.wait_ge(gram_out, grams * h)
                for c in range(TB):
                    last = pe.matmul(g_bank[0][:, c, :], k_now[:, c * P:(c + 1) * P],
                                     query[:, h, pl(M + c * P, P)], start=True, stop=True)
                last.then_inc(gram_done, 1)
                for l in range(LEVELS):
                    b = (l + 1) % 2
                    pe.wait_ge(half_ready, LEVELS * h + l + 1)
                    if l:
                        pe.wait_ge(gram_out, grams * h + l)
                    tile = halves[:, l % 2, :]
                    for c in range(TB):
                        part = tile[:, c * P:(c + 1) * P]
                        last = pe.matmul(g_bank[b][:, c, :], part, part, start=True, stop=True)
                    last.then_inc(gram_done, 1)
                    if l == 0:
                        pe.wait_ge(in_out_ready, 2 * h + 2)
                        for c in range(TB - 1):
                            pe.transpose(k_bank[:, c, :], k_out[:, M + c * P:M + (c + 1) * P], ident[:, :])
                        pe.transpose(k_bank[0:M, TB - 1, :], k_out[:, 0:M], ident[:, :])\
                            .then_inc(k_turned, 1)
                    if l == 2:
                        pe.wait_ge(k_turned_out, h + 1)
                        for c in range(TB - 1):
                            pe.matmul(u_bank[:, c, :], k_outT[:, c, :], value(h, c),
                                      start=True, stop=True)
                        pe.matmul(u_bank[:, TB - 1, :], k_outT[0:M, TB - 1, :],
                                  nat_meta[:, h // 4 + HI_PIECE, pl((h % 4) * HD, HD)],
                                  start=True, stop=True).then_inc(update_done, 1)
                pe.wait_ge(gram_out, grams * (h + 1))
                pe.wait_ge(state_ready, TB * (h + 1))
                pe.wait_ge(out_copied, h)
                for c in range(TB):
                    pe.matmul(o_bank[:, c, :], scores[:, c, :], value(h, c), start=True, stop=False)
                    last = pe.matmul(o_bank[:, c, :], q_in[:, c * P:(c + 1) * P], state[:, c, :],
                                     start=False, stop=True)
                last.then_inc(out_done, 1)

        @block.vector
        def _(dve):
            dve.tensor_tensor(diff[:, :], cst["lb_logits"][:, 0, :], cst["lb_logits"][:, 1, :],
                              ALU.subtract).then_inc(apart, 1)
            dve.wait_ge(opened, 1)
            dve.tensor_tensor(query, query, logs[:, :, :], ALU.mult)
            dve.wait_ge(bounded, 1)
            dve.wait_ge(opened, 3)
            for h in range(RH):
                dve.tensor_scalar(keys[:, h, :], keys[:, h, :], lb[:, 1, h:h + 1], None, ALU.mult)
                last = dve.tensor_scalar(gate[:, h, :], gate[:, h, :], lb[:, 1, h:h + 1],
                                         lb[:, 0, h:h + 1], ALU.mult, ALU.add)
            last.then_inc(bounds, 1)
            dve.wait_ge(logged, 1)
            for h in range(RH):
                last = dve.tensor_tensor_scan(logs[:, h, :], cst["keep"][:, :], gate[:, h, :], 0.0,
                                              ALU.mult, ALU.add)
            last.then_inc(summed, 1)
            dve.wait_ge(summed, 1)
            with dve.Fori(0, RH) as h:
                b_real = logs[:, h, M:L]
                by_chunk = b_real.rearrange("p (c t) -> p c t", t=P)
                dve.wait_ge(edge_ready, 2 * h)
                dve.tensor_tensor(gap_out[:, M:L].rearrange("p (c t) -> p c t", t=P),
                                  by_chunk[:, :, P - 1:P].to_broadcast([P, TB, P]), by_chunk,
                                  ALU.subtract)
                dve.tensor_tensor(gap_out[:, 0:M], logs[:, h, M - 1:M].to_broadcast([P, M]),
                                  logs[:, h, 0:M], ALU.subtract).then_inc(out_gap, 1)

                def half(l):
                    w, e = split(halves[:, l % 2, :], l), split(decays[:, l % 2, :], l)
                    dve.wait_ge(decay_ready, LEVELS * h + l + 1)
                    if l >= 2:
                        dve.wait_ge(gram_done, grams * h + l)
                    dve.tensor_tensor(w[:, :, 0, :], e[:, :, 0, :],
                                      split(keys[:, h, M:L], l)[:, :, 0, :], ALU.mult)
                    dve.tensor_tensor(w[:, :, 1, :], e[:, :, 1, :],
                                      split(query[:, h, M:L], l)[:, :, 1, :], ALU.mult)\
                        .then_inc(half_ready, 1)

                def pick(l):
                    dve.wait_ge(gram_done, grams * h + l + 2)
                    dve.wait_ge(gram_out, grams * h + l + 1)
                    dve.sem_inc(waited, 1)
                    dve.copy_predicated(
                        scores[:, :, :],
                        cst["level_mask"][:, l, :].unsqueeze(1).to_broadcast([P, TB, P]),
                        g_bank[(l + 1) % 2][:, :, :]).then_inc(gram_out, 1)

                half(0)
                dve.wait_ge(edge_ready, 2 * h + 1)
                dve.wait_ge(out_done, h)
                dve.tensor_tensor(q_in[:, :], grown[:, :], query[:, h, M:L], ALU.mult)\
                    .then_inc(in_out_ready, 1)
                dve.wait_ge(edge_ready, 2 * h + 2)
                dve.tensor_tensor(k_out[:, :], k_out[:, :], keys[:, h, :], ALU.mult)\
                    .then_inc(in_out_ready, 1)
                dve.wait_ge(gram_done, grams * h + 1)
                dve.tensor_tensor(scores[:, :, :], g_bank[0][:, :, :],
                                  cst["ident"][:, :].unsqueeze(1).to_broadcast([P, TB, P]),
                                  ALU.mult).then_inc(gram_out, 1)
                for l in range(LEVELS):
                    if l:
                        half(l)
                        pick(l - 1)
                    if l == 4:
                        dve.wait_ge(update_done, h + 1)
                        dve.tensor_copy(state[:, 0, :], u_bank[:, TB - 1, :])\
                            .then_inc(state_ready, 1)
                        for c in range(TB - 1):
                            dve.wait_ge(state_ready, TB * h + c + 1)
                            dve.scalar_tensor_tensor(state[:, c + 1, :], state[:, c, :],
                                                     grown[:, (c + 1) * P - 1:(c + 1) * P],
                                                     u_bank[:, c, :], ALU.mult, ALU.add)\
                                .then_inc(state_ready, 1)
                pick(LEVELS - 1)
            outs = mix[:, :, QH * HD:].rearrange("p t (h d) -> p t h d", d=HD)
            gates = hg_view(nat)
            squares = logs_as_squares(logs)
            dve.wait_ge(squared, 1)
            dve.tensor_reduce(stat[:, 0, :], squares.rearrange("p t (h d) -> p (t h) d", d=HD),
                              AX.X, ALU.add).then_inc(squared, 1)
            dve.wait_ge(squared, 2)
            dve.tensor_scalar(stat[:, 1, :], stat[:, 0, :], 1.0 / HD, EPS, ALU.mult, ALU.add)\
                .then_inc(meaned, 1)
            dve.wait_ge(rooted, 1)
            tail = Count(dve, mix_ready)
            inverse_root(dve, tail.link, stat[:, 3, :], stat[:, 1, :], stat[:, 2, :], stat[:, 0, :])
            dve.wait_ge(silu, 1)
            dve.tensor_tensor(gates, gates, keys_as_gates(keys), ALU.mult)
            tail.link(dve.tensor_tensor(outs, outs, stat[:, 3, :].rearrange("p (t h) -> p t h", h=RH)
                                        .unsqueeze(3).to_broadcast([P, TB, RH, HD]), ALU.mult))
            rows = mix[:, :, QH * HD:]
            tail.link(dve.tensor_tensor(rows, rows, cst["hgrn_gain"][:, :].unsqueeze(1)
                                        .to_broadcast([P, TB, RH * HD]), ALU.mult))
            dve.tensor_tensor(rows.rearrange("p t (j c) -> p j t c", c=PC),
                              rows.rearrange("p t (j c) -> p j t c", c=PC), gates, ALU.mult)


def logs_as_squares(logs):
    return logs[:, :, :].rearrange("p h t -> p (h t)")[:, 0:TB * RH * HD]\
        .rearrange("p (t c) -> p t c", t=TB)


def hg_view(nat):
    return nat[:, HG_PIECE:HG_PIECE + 2, :, :]


def keys_as_gates(keys):
    return keys[:, :, :].rearrange("p h t -> p (h t)")[:, 0:TB * RH * HD]\
        .rearrange("p (j t c) -> p j t c", j=2, t=TB)



OUT_PIECES = D // PC


def mix_out(nc, stream, mix, mixT, h, x, cst):
    hi, lo = mixT
    with ExitStack() as ctx:
        def sem(name):
            return ctx.enter_context(nc.semaphore(f"out_{name}"))

        turned, high, low = sem("turned"), sem("high"), sem("low")
        x_loaded, unit_done, added = sem("x_loaded"), sem("unit_done"), sem("added")
        t_bank = [ctx.enter_context(nc.psum_tensor(f"out_t{b}", [P, TB, P], F32)) for b in range(4)]
        banks = [ctx.enter_context(nc.psum_tensor(f"out_bank{b}", [P, PC], F32)) for b in range(4)]
        block = ctx.enter_context(nc.Block())

        @block.sync
        def _(sp):
            sp.wait_ge(turned, DC)
            sp.dma_start(h[:, :, :], x.rearrange("(b p) d -> p b d", p=P)).then_inc(x_loaded, 16)
            stream.load_rest(sp, OUT_PIECES)

        @block.gpsimd
        def _(pool):
            stream.split_low_all(pool, OUT_PIECES)

        @block.tensor
        def _(pe):
            stream.start_free(pe)
            for c in range(DC):
                if c >= 4:
                    pe.wait_ge(low, c - 3)
                for tb in range(TB):
                    last = pe.transpose(t_bank[c % 4][:, tb, :], mix[:, tb, c * P:(c + 1) * P],
                                        cst["ident"][:, :])
                last.then_inc(turned, 1)
            pe.wait_ge(low, DC)
            with pe.Fori(0, OUT_PIECES) as p:
                for g in range(STEPS):
                    stream.await_step(pe, p, g)
                    for s in range(SPAN):
                        c = g * SPAN + s
                        for tb in range(TB):
                            if c == 0:
                                pe.wait_ge(added, p * TB + (tb + 1))
                            tokens = slice(tb * P, (tb + 1) * P)
                            last = product(pe, banks[tb][:, :], (hi[:, c, tokens], lo[:, c, tokens]),
                                           stream.parts(g, s), c == 0, c == DC - 1)
                            if c == DC - 1 and tb < TB - 1:
                                last.then_inc(unit_done, 1)
                    stream.release(last)

        @block.scalar
        def _(act):
            stream.split_high(act, 0, 0)
            stream.split_high(act, 0, 1)
            for c in range(DC):
                act.wait_ge(turned, c + 1)
                act.copy(hi[:, c, :], t_bank[c % 4][:, :, :].rearrange("p b t -> p (b t)"))\
                    .then_inc(high, 1)
            for g in range(2, STEPS):
                stream.split_high(act, 0, g)
            with act.Fori(1, OUT_PIECES) as p:
                for g in range(STEPS):
                    stream.split_high(act, p, g)

        @block.vector
        def _(dve):
            dve.sem_inc(added, TB)
            for c in range(DC):
                dve.wait_ge(high, c + 1)
                dve.tensor_tensor(lo[:, c, :], t_bank[c % 4][:, :, :].rearrange("p b t -> p (b t)"),
                                  hi[:, c, :].bitcast(F32), ALU.subtract).then_inc(low, 1)
            dve.wait_ge(x_loaded, 16)
            with dve.Fori(0, OUT_PIECES) as p:
                for tb in range(TB):
                    if tb < TB - 1:
                        dve.wait_ge(unit_done, p * (TB - 1) + (tb + 1))
                    else:
                        stream.await_piece(dve, p)
                    cols = h[:, tb, pl(p * PC, PC)]
                    dve.tensor_tensor(cols, cols, banks[tb][:, :], ALU.add).then_inc(added, 1)



HC = 2 * PH


def route(nc, place, kb, stream, xT, picks, cst):
    with ExitStack() as ctx:
        def sem(name):
            return ctx.enter_context(nc.semaphore(f"route_{name}"))

        qT = place("route_qT", [P, 4, T], F32, kb)
        sc = place("route_scores", [P, 4, TB, NK], F32, kb + 8)
        rest = place("route_rest", [P, 2, TB, NK], F32, kb + 16)
        cand = place("route_cand", [P, TB, TOPK * TOPK], F32, kb + 20)
        cand_rest = place("route_cand_rest", [P, TB, TOPK * TOPK], F32, kb + 24)
        hot = place("route_hot", [P, 2, TB, TOPK, TOPK], F32, kb + 28)
        val = place("route_val", [P, 2, TB, TOPK], F32, kb + 36)
        idx = place("route_idx", [P, 2, TB, TOPK], U32, kb + 36.5)
        idx_f = place("route_idx_f", [P, 2, TB, TOPK], F32, kb + 37)
        best = place("route_best", [P, TB, TOPK], F32, kb + 37.5)
        pos = place("route_pos", [P, 3, TB, TOPK], U32, kb + 38)
        pos_f = place("route_pos_f", [P, 2, TB, TOPK], F32, kb + 39)
        gate = place("route_gate", [P, 2, TB, TOPK], F32, kb + 39.5)
        total = place("route_total", [P, 2, TB, PH], F32, kb + 40)

        q_done, q_out, s_done, s_out = sem("q_done"), sem("q_out"), sem("s_done"), sem("s_out")
        chain, scores_used, shifted, exp_done = (sem("chain"), sem("scores_used"), sem("shifted"),
                                                 sem("exp_done"))
        waited = sem("waited")
        q_bank = [ctx.enter_context(nc.psum_tensor(f"route_q{k}", [P, T], F32)) for k in range(4)]
        s_bank = [ctx.enter_context(nc.psum_tensor(f"route_s{k}", [P, TB, NK], F32)) for k in range(4)]
        block = ctx.enter_context(nc.Block())
        pieces = PH // 2

        @block.sync
        def _(sp):
            stream.load_rest(sp, pieces)

        @block.gpsimd
        def _(pool):
            stream.split_low_all(pool, pieces)

        @block.tensor
        def _(pe):
            stream.start_free(pe)

            def queries(p, steps, peeled=False):
                for g in steps:
                    stream.await_step(pe, p, g)
                    for s in range(SPAN):
                        c = g * SPAN + s
                        for k in range(4):
                            if c == 0 and not peeled:
                                pe.wait_ge(q_out, p * 4 + (k - 3))
                            w = [part[:, k * P:(k + 1) * P] for part in stream.parts(g, s)]
                            last = product(pe, q_bank[k][:, :], w, [x[:, c, :] for x in xT],
                                           c == 0, c == DC - 1)
                            if c == DC - 1 and k < 3:
                                last.then_inc(q_done, 1)
                    stream.release(last)

            def scores(p, peeled):
                for k in range(4):
                    pe.wait_ge(q_out, p * 4 + (k - 3))
                    if not peeled:
                        pe.wait_ge(s_out, p * 4 + (k - 7))
                    for tb in range(TB):
                        last = pe.matmul(s_bank[k][:, tb, :], qT[:, k, tb * P:(tb + 1) * P],
                                         cst["sub_keys"][:, p * 4 + (k - 4), :],
                                         start=True, stop=True)
                    last.then_inc(s_done, 1)

            queries(0, range(STEPS), True)
            queries(1, range(2))
            scores(1, True)
            queries(1, range(2, STEPS))
            with pe.Fori(2, pieces) as p:
                queries(p, range(2))
                scores(p, False)
                queries(p, range(2, STEPS))
            scores(pieces, False)

        @block.scalar
        def _(act):
            def empty_queries(p):
                for k in range(4):
                    if k < 3:
                        act.wait_ge(q_done, p * 3 + (k + 1))
                    else:
                        stream.await_piece(act, p)
                    act.copy(qT[:, k, :], q_bank[k][:, :]).then_inc(q_out, 1)

            def empty_scores(p, used=True):
                for k in range(4):
                    act.wait_ge(s_done, p * 4 + (k - 3))
                    if used and k % 2 == 0:
                        act.wait_ge(scores_used, p * 2 + (k // 2 - 3))
                    act.copy(sc[:, k], s_bank[k][:, :, :]).then_inc(s_out, 1)

            stream.split_high(act, 0, 0)
            for g in range(1, STEPS):
                stream.split_high(act, 0, g)
            stream.split_high(act, 1, 0)
            empty_queries(0)
            for p in range(1, pieces):
                stream.split_high(act, p, 1)
                stream.split_high(act, p, 2)
                empty_scores(p, p > 1)
                for g in range(3, STEPS):
                    stream.split_high(act, p, g)
                if p < pieces - 1:
                    stream.split_high(act, p + 1, 0)
                empty_queries(p)
            empty_scores(pieces)
            act.wait_ge(shifted, 1)
            act.activation(picks[2][:, :, :], picks[2][:, :, :], ACT.Exp).then_inc(exp_done, 1)

        @block.vector
        def _(dve):
            count = Count(dve, chain)
            link = count.link

            def take_wait():
                dve.sem_inc(waited, 1)

            def top16(rows, rests, values, places):
                take_wait()
                for part in range(2):
                    cols = slice(8 * part, 8 * part + 8)
                    src = rows if part == 0 else rests
                    for r, v in zip(src, values):
                        last = dve.max(out=v[:, cols], in_=r)
                    link(last)
                    take_wait()
                    for r, v, p in zip(src, values, places):
                        last = dve.max_index(out=p[:, cols], in_max=v[:, cols], in_values=r)
                    if part == 0:
                        for r, t, v in zip(rows, rests, values):
                            last = dve.match_replace(out=t, in_to_replace=v[:, cols],
                                                     in_values=r, imm_value=-3.0e38)
                    link(last)
                    take_wait()

            def head(i, j):
                k, at = 2 * j, i * (2 * TOPK) + j * TOPK
                dve.wait_ge(s_out, i * 4 + (2 * j + 2))
                both = [(c, tb) for c in range(2) for tb in range(TB)]
                top16([sc[:, k + c, tb, :] for c, tb in both], [rest[:, c, tb, :] for c, tb in both],
                      [val[:, c, tb, :] for c, tb in both], [idx[:, c, tb, :] for c, tb in both])
                dve.sem_inc(scores_used, 1)
                dve.tensor_copy(idx_f[:, :, :, :], idx[:, :, :, :])
                link(dve.tensor_tensor(
                    cand[:, :, :].rearrange("p b (i j) -> p b i j", j=TOPK),
                    val[:, 0].unsqueeze(3).to_broadcast([P, TB, TOPK, TOPK]),
                    val[:, 1].unsqueeze(2).to_broadcast([P, TB, TOPK, TOPK]), ALU.add))
                tiles = range(TB)
                top16([cand[:, b, :] for b in tiles], [cand_rest[:, b, :] for b in tiles],
                      [best[:, b, :] for b in tiles], [pos[:, 0, b, :] for b in tiles])
                dve.tensor_copy(picks[2][:, :, pl(at, TOPK)], best[:, :, :])
                dve.tensor_scalar(pos[:, 1], pos[:, 0], 4, None, ALU.logical_shift_right)
                link(dve.tensor_scalar(pos[:, 2], pos[:, 0], TOPK - 1, None, ALU.bitwise_and))
                link(dve.tensor_copy(pos_f[:, :, :, :], pos[:, 1:3]))
                for c in range(2):
                    last = dve.tensor_tensor(
                        hot[:, c].rearrange("p b n r -> p (b n) r"),
                        pos_f[:, c].rearrange("p b n -> p (b n)").unsqueeze(2)
                        .to_broadcast([P, TB * TOPK, TOPK]),
                        cst["iota"][:, 0:TOPK].unsqueeze(1).to_broadcast([P, TB * TOPK, TOPK]),
                        ALU.is_equal)
                link(last)
                for c in range(2):
                    last = dve.tensor_tensor(
                        hot[:, c], hot[:, c],
                        idx_f[:, c].unsqueeze(2).to_broadcast([P, TB, TOPK, TOPK]), ALU.mult)
                link(last)
                for c in range(2):
                    last = dve.tensor_reduce(picks[c][:, :, pl(at, TOPK)], hot[:, c], AX.X, ALU.add)
                link(last)

            with dve.Fori(0, pieces) as i:
                count.enter(i, 2 * (4 + 1 + 4 + 2 + 3))
                head(i, 0)
                head(i, 1)
                count.leave(pieces)

            gates = picks[2][:, :, :].rearrange("p b (h n) -> p b h n", n=TOPK)
            tops = total[:, 0]
            link(dve.tensor_copy(tops, gates[:, :, :, 0]))
            dve.tensor_tensor(gates, gates, tops.unsqueeze(3).to_broadcast([P, TB, PH, TOPK]),
                              ALU.subtract).then_inc(shifted, 1)
            dve.wait_ge(exp_done, 1)
            link(dve.tensor_reduce(total[:, 1], gates, AX.X, ALU.add))
            link(dve.reciprocal(total[:, 1], total[:, 1]))
            dve.tensor_tensor(gates, gates, total[:, 1].unsqueeze(3)
                              .to_broadcast([P, TB, PH, TOPK]), ALU.mult)



SLOTS, SLOT_TOKENS = 4, 4
TABLE_TOKENS = 64
PARTS = T // TABLE_TOKENS


def gate_table(nc, stages, hot, picks, picksT, table, cst, at_turned):
    run = SLOTS * SLOT_TOKENS
    slots_of_part = TABLE_TOKENS // SLOT_TOKENS
    with ExitStack() as ctx:
        def sem(name):
            return ctx.enter_context(nc.semaphore(f"table_{name}"))

        turned, turned_out = sem("turned"), sem("turned_out")
        hot_ready, gated = sem("hot_ready"), sem("gated")
        banks_done, banks_out, waited = sem("banks_done"), sem("banks_out"), sem("waited")
        stored = [sem("stored0"), sem("stored1")]
        t_bank = [ctx.enter_context(nc.psum_tensor(f"table_t{b}", [P, TB, P], F32)) for b in range(3)]
        banks = [ctx.enter_context(nc.psum_tensor(f"table_b{b}", [P, SLOT_TOKENS, NK], F32))
                 for b in range(SLOTS)]
        block = ctx.enter_context(nc.Block())

        def gates(t):
            return picksT[:, 2, pl(t, SLOT_TOKENS)].unsqueeze(2).to_broadcast([P, SLOT_TOKENS, NK])

        @block.sync
        def _(sp):
            sp.wait_ge(turned, 3)
            at_turned(sp)
            with sp.Fori(0, PARTS // 2) as q:
                for s in range(2):
                    sp.wait_ge(banks_out, q * (2 * slots_of_part) + (slots_of_part * (s + 1) + SLOTS))
                    sp.dma_start(table[q * 2 + s], stages[s][:]).then_inc(stored[s], 16)
            for s in stored:
                sp.wait_ge(s, 16 * PARTS // 2)

        @block.tensor
        def _(pe):
            pe.sem_inc(banks_done, SLOTS)
            for k in range(3):
                for tb in range(TB):
                    last = pe.transpose(t_bank[k][:, tb, :], picks[k][:, tb, :], cst["ident"][:, :])
                last.then_inc(turned, 1)
            with pe.Fori(0, T // run) as i:
                for s in range(SLOTS):
                    pe.wait_ge(gated, i * SLOTS + (s + 1))
                    pe.wait_ge(banks_out, i * SLOTS + (s + 1))
                    for j in range(SLOT_TOKENS):
                        last = pe.matmul(banks[s][:, j, :], hot[:, s, 1, j, :], hot[:, s, 0, j, :],
                                         start=True, stop=True)
                    last.then_inc(banks_done, 1)

        @block.gpsimd
        def _(pool):
            pool.wait_ge(turned_out, 3)
            with pool.Fori(0, T // run) as i:
                for s in range(SLOTS):
                    pool.wait_ge(hot_ready, i * SLOTS + (s + 1))
                    pool.sem_inc(waited, 1)
                    pool.tensor_tensor(hot[:, s, 1], hot[:, s, 1], gates(i * run + s * SLOT_TOKENS),
                                       ALU.mult).then_inc(gated, 1)

        @block.vector
        def _(dve):
            for k in range(3):
                dve.wait_ge(turned, k + 1)
                dve.tensor_copy(picksT[:, k, :], t_bank[k][:, :, :].rearrange("p b t -> p (b t)"))\
                    .then_inc(turned_out, 1)
            dve.wait_ge(turned_out, 3)
            with dve.Fori(0, T // run) as i:
                for s in range(SLOTS):
                    dve.wait_ge(banks_done, i * SLOTS + (s + 1))
                    dve.tensor_tensor(hot[:, s],
                                      cst["iota"][:, :].unsqueeze(1).unsqueeze(1)
                                      .to_broadcast([P, 2, SLOT_TOKENS, NK]),
                                      picksT[:, 0:2, pl(i * run + s * SLOT_TOKENS, SLOT_TOKENS)]
                                      .unsqueeze(3).to_broadcast([P, 2, SLOT_TOKENS, NK]),
                                      ALU.is_equal).then_inc(hot_ready, 1)

        @block.scalar
        def _(act):
            act.sem_inc(banks_out, SLOTS)
            for q in range(PARTS):
                if q >= 2:
                    act.wait_ge(stored[q % 2], 16 * (q // 2))
                with act.Fori(0, TABLE_TOKENS // run) as i:
                    for s in range(SLOTS):
                        act.wait_ge(banks_done, i * SLOTS + (slots_of_part * q + s + SLOTS + 1))
                        act.copy(stages[q % 2][:, :, pl(i * run + s * SLOT_TOKENS, SLOT_TOKENS)],
                                 banks[s][:, :, :].rearrange("p t i -> p i t"))\
                            .then_inc(banks_out, 1)



GROUPS = NK // 2
HALF_D = D // 2


def experts(nc, place, h, xT, u, v, raw, loaded, load_raw, table, out):
    xh, xl = xT
    with ExitStack() as ctx:
        def sem(name):
            return ctx.enter_context(nc.semaphore(f"exp_{name}"))

        uh = place("exp_uh", [P, 2, DC, P], F32R, 32)
        ul = place("exp_ul", [P, 2, DC, P], F32R, 48)
        vh = place("exp_vh", [P, 2, D], F32R, 128)
        vl = place("exp_vl", [P, 2, D], F32R, 144)
        ah = place("exp_ah", [P, 2, 2, T], F32R, 160)
        al = place("exp_al", [P, 2, 2, T], F32R, 168)
        gates = place("exp_gates", [P, 2, T], F32, 192)
        act_f = place("exp_act", [P, 2, T], F32, 196)

        gates_in = [sem(f"gates_in{b}") for b in range(2)]
        high, low = sem("high"), sem("low")
        a_done, gelu_done, weighted, a_high, a_split = (sem("a_done"), sem("gelu_done"),
                                                        sem("weighted"), sem("a_high"), sem("a_split"))
        o_done, o_out, stored = sem("o_done"), sem("o_out"), sem("stored")
        a_bank = [ctx.enter_context(nc.psum_tensor(f"exp_a{b}", [P, T], F32)) for b in range(2)]
        o_bank = [ctx.enter_context(nc.psum_tensor(f"exp_o{b}", [P, PC], F32)) for b in range(D // PC)]
        block = ctx.enter_context(nc.Block())
        units = TB * (D // PC)

        def wait(eng, s, value):
            if not isinstance(value, int) or value > 0:
                eng.wait_ge(s, value)

        def run(eng, phase):
            last = GROUPS - 1
            phase("u", 0, 0, 0, ("u", 1))
            with eng.Fori(0, GROUPS // 2 - 1) as i:
                phase("u", i * 2 + 1, 1, i * 4 + 1, ("v", i * 2))
                phase("v", i * 2, 0, i * 4 + 2, ("u", i * 2 + 2))
                phase("u", i * 2 + 2, 0, i * 4 + 3, ("v", i * 2 + 1))
                phase("v", i * 2 + 1, 1, i * 4 + 4, ("u", i * 2 + 3))
            phase("u", last, 1, 2 * last - 1, ("v", last - 1))
            phase("v", last - 1, 0, 2 * last, ("v", last))
            phase("v", last, 1, 2 * last + 1, None)

        @block.sync
        def _(sp):
            def u_phase(g, parity, k):
                if not isinstance(k, int) or k > 0:
                    for n in range(4):
                        wait(sp, low, 4 * (k - 1) + (n + 1))
                        load_raw(sp, u, g, n)
                for b in range(2):
                    wait(sp, weighted, 2 * g + (b - 1))
                    sp.dma_start(gates[:, b, :].rearrange("p (q t) -> p q t", q=PARTS),
                                 table[:, :, g * 2 + b, :].rearrange("q j t -> j q t"))\
                        .then_inc(gates_in[b], 16)

            def v_phase(g, parity, k):
                for n in range(4):
                    wait(sp, low, 4 * (k - 1) + (n + 1))
                    load_raw(sp, v, g, n)

            run(sp, lambda kind, g, parity, k, after:
                (u_phase if kind == "u" else v_phase)(g, parity, k))
            sp.wait_ge(o_out, units * GROUPS + 4)
            sp.dma_start(out.rearrange("(b p) d -> p b d", p=P), h[:, :, :]).then_inc(stored, 16)
            sp.wait_ge(stored, 16)

        @block.tensor
        def _(pe):
            def u_phase(g, parity, k):
                for b in range(2):
                    wait(pe, gelu_done, g * 2 + (b - 1))
                    for c in range(DC):
                        if c % (DC // 2) == 0:
                            pe.wait_ge(low, 4 * k + (2 * b + c // (DC // 2) + 1))
                        pe.matmul(a_bank[b][:, :], uh[:, b, c, :], xh[:, c, :],
                                  start=(c == 0), stop=False)
                        pe.matmul(a_bank[b][:, :], uh[:, b, c, :], xl[:, c, :],
                                  start=False, stop=False)
                        last = pe.matmul(a_bank[b][:, :], ul[:, b, c, :], xh[:, c, :],
                                         start=False, stop=(c == DC - 1))
                    last.then_inc(a_done, 1)

            def v_phase(g, parity, k):
                pe.wait_ge(low, 4 * k + 4)
                pe.wait_ge(a_split, g * 2 + 2)
                for n in range(units):
                    tb, dc = n // 4, n % 4
                    tokens, cols = slice(tb * P, (tb + 1) * P), slice(dc * PC, (dc + 1) * PC)
                    pe.wait_ge(o_out, g * units + (n + 1))
                    for b in range(2):
                        pe.matmul(o_bank[dc][:, :], ah[:, parity, b, tokens], vh[:, b, cols],
                                  start=(b == 0), stop=False)
                        pe.matmul(o_bank[dc][:, :], ah[:, parity, b, tokens], vl[:, b, cols],
                                  start=False, stop=False)
                        last = pe.matmul(o_bank[dc][:, :], al[:, parity, b, tokens], vh[:, b, cols],
                                         start=False, stop=(b == 1))
                    last.then_inc(o_done, 1)

            run(pe, lambda kind, g, parity, k, after:
                (u_phase if kind == "u" else v_phase)(g, parity, k))

        @block.scalar
        def _(act):
            def split_high(kind, g, k, n):
                if n == 0:
                    wait(act, a_done if kind == "u" else o_done, g * (2 if kind == "u" else units))
                act.wait_ge(loaded[n], 16 * (k + 1))
                act.copy(part(uh if kind == "u" else vh, kind, n), raw[:, n, :]).then_inc(high, 1)

            def phase(kind, g, parity, k, after):
                late = after is None or kind == after[0]
                if kind == "u":
                    for b in range(2):
                        if not late:
                            split_high(*after, k + 1, 2 * b)
                            split_high(*after, k + 1, 2 * b + 1)
                        act.wait_ge(a_done, g * 2 + (b + 1))
                        wait(act, a_split, g * 2 + (b - 1))
                        act.activation(act_f[:, b, :], a_bank[b][:, :], ACT.Gelu_apprx_tanh)\
                            .then_inc(gelu_done, 1)
                if (late or kind == "v") and after is not None:
                    for n in range(4):
                        split_high(*after, k + 1, n)

            for n in range(4):
                split_high("u", 0, 0, n)
            run(act, phase)

        @block.vector
        def _(dve):
            dve.sem_inc(o_out, 4)
            def split_low(kind, g, k, n):
                dve.wait_ge(high, 4 * k + (n + 1))
                dve.tensor_tensor(part(ul if kind == "u" else vl, kind, n), raw[:, n, :],
                                  part(uh if kind == "u" else vh, kind, n).bitcast(F32), ALU.subtract)\
                    .then_inc(low, 1)

            def phase(kind, g, parity, k, after):
                late = after is None or kind == after[0]
                if kind == "u":
                    for b in range(2):
                        if not late:
                            split_low(*after, k + 1, 2 * b)
                            split_low(*after, k + 1, 2 * b + 1)
                        dve.wait_ge(gelu_done, g * 2 + (b + 1))
                        dve.wait_ge(gates_in[b], 16 * (g + 1))
                        dve.tensor_tensor(act_f[:, b, :], act_f[:, b, :], gates[:, b, :], ALU.mult)\
                            .then_inc(weighted, 1)
                        dve.wait_ge(weighted, g * 2 + (b + 1))
                        wait(dve, o_done, (g - 1) * units)
                        dve.tensor_copy(ah[:, parity, b, :], act_f[:, b, :]).then_inc(a_high, 1)
                        dve.wait_ge(a_high, g * 2 + (b + 1))
                        dve.tensor_tensor(al[:, parity, b, :], act_f[:, b, :],
                                          ah[:, parity, b, :].bitcast(F32), ALU.subtract)\
                            .then_inc(a_split, 1)
                else:
                    for n in range(units):
                        tb, dc = n // 4, n % 4
                        dve.wait_ge(o_done, g * units + (n + 1))
                        sums = h[:, tb, dc * PC:(dc + 1) * PC]
                        dve.tensor_tensor(sums, sums, o_bank[dc][:, :], ALU.add).then_inc(o_out, 1)
                        if n % 4 == 2 and not late:
                            split_low(*after, k + 1, n // 4)
                if late and after is not None:
                    for n in range(4):
                        split_low(*after, k + 1, n)

            for n in range(4):
                split_low("u", 0, 0, n)
            run(dve, phase)


def part(tile, kind, n):
    b, half = n // 2, n % 2
    if kind == "u":
        return tile[:, b, half * (DC // 2):(half + 1) * (DC // 2), :].rearrange("p c e -> p (c e)")
    return tile[:, b, half * HALF_D:(half + 1) * HALF_D]




def shape_constants():
    pos = np.arange(L, dtype=np.float32)
    inv = (np.float32(500000.0) ** (-np.arange(0, ROPE, 2, dtype=np.float32) / np.float32(ROPE)))
    ang = pos[:, None] * inv.astype(np.float32)[None, :]
    cos, sin = np.cos(ang).astype(np.float32), np.sin(ang).astype(np.float32)
    row = np.arange(P)[:, None]
    col = np.arange(P)[None, :]
    prev = np.where(col > row, 0.0, NEG)
    own = np.where(col <= row, 0.0, NEG)
    meta = np.zeros((P, M))
    return {
        "iota": np.broadcast_to(np.arange(P, dtype=np.float32), (P, P)),
        "ident": np.eye(P, dtype=np.float32),
        "cos": cos[M:].reshape(TB, P, HALF).transpose(1, 0, 2),
        "sin": sin[M:].reshape(TB, P, HALF).transpose(1, 0, 2),
        "meta_cos": cos[:M],
        "meta_sin": sin[:M],
        "mask": np.concatenate([meta, prev, own], 1).astype(np.float32),
        "keep": np.broadcast_to(((np.arange(L) % P != M) & (np.arange(L) > 0)).astype(np.float32), (P, L)),
        "level_mask": np.stack([(row // (P >> l) == col // (P >> l)) & (row % (P >> l) < (P >> (l + 1)))
                                & (col % (P >> l) >= (P >> (l + 1))) for l in range(LEVELS)],
                               1).astype(np.float32),
        "mask_first": np.concatenate([meta, own], 1).astype(np.float32),
    }



def build(nc, a, out):
    place = Place(nc)
    h = place("h", [P, TB, D], F32, 0)
    mix = place("mix", [P, TB, D], F32, 0)
    hn = [place("hn_high", [P, DC, L], F32R, 0), place("hn_low", [P, DC, L], F32R, 33)]
    w_in = Stream(nc, "w_in", place, 66, a["w_in"])
    nat = place("nat", [P, NAT_PIECES, TB, PC], F32, 98)
    nat_meta = place("nat_meta", [M, META_PIECES, PC], F32, 154)
    turned = place("turned", [P, 2 * RH, L], F32, 160)
    mixT = [place("mixT_high", [P, DC, T], F32R, 66), place("mixT_low", [P, DC, T], F32R, 98)]
    w_out = Stream(nc, "w_out", place, 160, a["w_out"])
    x_rows = place("x_rows", [P, TB, D], F32, 98)
    meta_rows = place("meta_rows", [M, D], F32, 130)
    mask_wide = place("level_mask_wide", [P, LEVELS, P], F32, 176)
    xT = [place("x_high", [P, DC, T], F32R, 64), place("x_low", [P, DC, T], F32R, 96)]
    w_q = Stream(nc, "w_q", place, 32, a["w_q"])
    picks = [place(f"picks{k}", [P, TB, P], F32, 182 + 2 * k) for k in range(3)]
    picksT = place("picksT", [P, 3, T], F32, 200)
    stages = [place(f"table_stage{i}", [P, NK, TABLE_TOKENS], F32, kb) for i, kb in enumerate((32, 128))]
    hot = place("table_hot", [P, SLOTS, 2, SLOT_TOKENS, NK], F32, 160)
    raw = place("exp_raw", [P, 4, HALF_D], F32, 176)
    raw_in = [nc.alloc_semaphore(f"exp_raw_in{n}") for n in range(4)]
    sub_keys = place("sub_keys", [P, HC, NK], F32, 128)
    table = nc.dram_tensor("gate_table", [PARTS, NK, NK, TABLE_TOKENS], F32, kind="Internal").ap()

    cst, kb = {}, 193.0
    early, late = [], []
    for name, shape, dtype in CONSTANTS:
        cst[name] = place(f"c_{name}", shape, dtype, kb)
        kb += -(-int(np.prod(shape[1:])) * mybir.dt.size(dtype) // 4) * 4 / KB
        src = a[name].partition_broadcast(P) if name in ROWS else a[name]
        (early if name in ("ident", "ln_mix") else late).append((cst[name], src))
    late.append((mask_wide, a["level_mask"]))
    cst["level_mask"] = place("c_level_mask", [P, LEVELS, P], U8, kb)
    assert kb + LEVELS * P / KB < 207.8, kb
    cst["sub_keys"] = sub_keys
    early_in, late_in = nc.alloc_semaphore("early_consts"), nc.alloc_semaphore("late_consts")
    keys_loaded = nc.alloc_semaphore("sub_keys_loaded")

    def load_early(sp):
        for dst, src in early:
            sp.dma_start(dst[:], src).then_inc(early_in, 16)

    def load_late(sp):
        w_in.load_start(sp)
        for dst, src in late:
            sp.dma_start(dst[:], src).then_inc(late_in, 16)

    def narrow_mask(dve):
        dve.wait_ge(late_in, 16 * len(late))
        dve.tensor_copy(cst["level_mask"][:], mask_wide[:])

    def load_keys(sp):
        w_q.load_start(sp)
        sp.dma_start(sub_keys[:], a["sub_keys"]).then_inc(keys_loaded, 16)
        sp.wait_ge(keys_loaded, 16)

    rows = [(x_rows[:, tb, :], P, M + tb * P, a["x"][tb * P:(tb + 1) * P, :]) for tb in range(TB)]
    norm_rows(nc, "mixnorm", [(meta_rows[:, :], M, 0, a["meta"])] + rows, cst["ln_mix"], hn,
              cst["ident"], place, 138, load_early, load_late, (early_in, 16 * len(early)), narrow_mask)
    project(nc, w_in, hn, nat, nat_meta, turned)
    attend(nc, place, 33, nat, nat_meta, mix, cst)
    recur(nc, place, 33, nat, nat_meta, turned, mix, cst, w_out)
    mix_out(nc, w_out, mix, mixT, h, a["x"], cst)
    norm_rows(nc, "ffnnorm", [(h[:, tb, :], P, tb * P, None) for tb in range(TB)], cst["ln_ffn"],
              xT, cst["ident"], place, 144, None, load_keys)
    route(nc, place, 136, w_q, xT, picks, cst)

    def load_raw(sp, weights, g, n):
        sp.dma_start(raw[:, n, :], weights[g * 2 + n // 2, :, (n % 2) * HALF_D:(n % 2 + 1) * HALF_D])\
            .then_inc(raw_in[n], 16)

    def load_first_experts(sp):
        for n in range(4):
            load_raw(sp, a["u"], 0, n)

    gate_table(nc, stages, hot, picks, picksT, table, cst, load_first_experts)
    experts(nc, place, h, xT, a["u"], a["v"], raw, raw_in, load_raw, table, out)


CONSTANTS = [
    ("ident", [P, P], F32), ("iota", [P, P], F32), ("ln_mix", [P, DC], F32), ("ln_ffn", [P, DC], F32),
    ("cos", [P, TB, HALF], F32), ("sin", [P, TB, HALF], F32),
    ("meta_cos", [M, HALF], F32), ("meta_sin", [M, HALF], F32),
    ("mask", [P, KEYS], F32), ("mask_first", [P, M + P], F32), ("qk_gain", [P, GROUP + 1, HD], F32),
    ("sinks", [P, QH], F32), ("keep", [P, L], F32),
    ("lb_logits", [P, 2, RH], F32), ("hgrn_gain", [P, RH * HD], F32),
]
ROWS = ("iota", "qk_gain", "sinks", "keep", "hgrn_gain")


def turn_rows(w, pieces, cols):
    return w.reshape(DC, P, pieces, cols).transpose(2, 1, 0, 3)


def kernel(**inputs):
    import concourse.bacc as bacc
    from concourse.bass_utils import run_bass_kernel_spmd

    i = {name: np.asarray(value) for name, value in inputs.items()}
    shapes = shape_constants()
    q_gain, k_gain = i["q_norm_g"][0], i["k_norm_g"][0]
    arrays = {
        **shapes,
        "iota": shapes["iota"][0],
        "keep": shapes["keep"][0],
        "x": i["x"][0],
        "meta": i["meta_tokens"],
        "ln_mix": i["ln_mix_g"][0].reshape(DC, P).T,
        "ln_ffn": i["ln_ffn_g"][0].reshape(DC, P).T,
        "qk_gain": np.stack([q_gain] * GROUP + [k_gain]),
        "sinks": i["attn_sinks"][0],
        "lb_logits": i["hgrn_lb_logits"].reshape(2, RH, P).transpose(2, 0, 1),
        "hgrn_gain": i["hgrn_norm_g"][0],
        "w_in": turn_rows(i["w_in"][0], PIECES, PC)[ORDER],
        "w_out": turn_rows(i["w_out"][0], OUT_PIECES, PC),
        "w_q": turn_rows(i["peer_w_q"][0], PH // 2, PC),
        "sub_keys": i["peer_sub_keys"][0].reshape(HC, NK, P).transpose(2, 0, 1),
        "u": i["peer_u"][0].reshape(NK, NK, DC, P).transpose(0, 3, 2, 1).reshape(NK, P, D),
        "v": i["peer_v"][0].reshape(NK, NK, D),
    }
    arrays = {f"in_{name}": np.ascontiguousarray(value) for name, value in arrays.items()}
    nc = bacc.Bacc("TRN2", target_bir_lowering=False, num_devices=1)
    aps = {name[3:]: nc.dram_tensor(name, value.shape, mybir.dt.from_np(value.dtype),
                                    kind="ExternalInput").ap() for name, value in arrays.items()}
    out = nc.dram_tensor("out_dram", [T, D], F32, kind="ExternalOutput").ap()
    build(nc, aps, out)
    result = run_bass_kernel_spmd(nc, [arrays], core_ids=[0])
    return result.results[0]["out_dram"].reshape(1, T, D)
```

```python
from contextlib import ExitStack

import numpy as np

import concourse.bass as bass
from concourse import mybir

ALU = mybir.AluOpType
ACT = mybir.ActivationFunctionType
AX = mybir.AxisListType
F32 = mybir.dt.float32
F32R = mybir.dt.float32r
U32 = mybir.dt.uint32
U8 = mybir.dt.uint8

P = 128
D = 2048
DC = D // P
T = 512
TB = T // P
M = 16
L = M + T
HD = 128
QH, KVH = 8, 2
GROUP = QH // KVH
RH = 8
ROPE = 32
HALF = ROPE // 2
EPS = 1e-6
SCALE = HD ** -0.5
BAND = 2 * P
KEYS = M + BAND
NEG = -1e30
LEVELS = 7
PH, NK, TOPK = 8, 128, 16
PC = 512
KB = 1024
BASE = 16512


class Count:

    def __init__(self, eng, sem):
        self.eng, self.sem, self.n, self.reg, self.per = eng, sem, 0, None, 0

    def up(self, ins):
        ins.then_inc(self.sem, 1)
        self.n += 1

    def link(self, ins):
        self.up(ins)
        self.wait()

    def wait(self):
        self.eng.wait_ge(self.sem, self.n if self.reg is None else self.reg * self.per + self.n)

    def enter(self, reg, per):
        self.reg, self.per, self.start = reg, per, self.n

    def leave(self, trips):
        assert self.n - self.start == self.per, (self.n - self.start, self.per)
        self.n = self.start + trips * self.per
        self.reg = None


class Place:

    def __init__(self, nc):
        self.nc = nc

    def __call__(self, name, shape, dtype, kb):
        off = BASE + int(round(kb * KB))
        assert off % 4 == 0
        return self.nc.alloc_sbuf_tensor_at(name, shape, dtype, offset=off)


def inverse_root(dve, link, out, square, root, spare):
    link(dve.reciprocal(out, root))
    link(dve.tensor_tensor(spare, out, out, ALU.mult))
    link(dve.tensor_tensor(spare, spare, square, ALU.mult))
    link(dve.tensor_scalar(spare, spare, -0.5, 1.5, ALU.mult, ALU.add))
    link(dve.tensor_tensor(out, out, spare, ALU.mult))




def norm_rows(nc, tag, tiles, gain, parts, ident, place, kb, first_loads=None, more_loads=None,
              consts=None, at_end=None, stream=None):
    n = len(tiles)
    hi, lo = parts
    with ExitStack() as ctx:
        def sem(name):
            return ctx.enter_context(nc.semaphore(f"{tag}_{name}"))

        loaded, summed, meaned, rooted = ([sem(f"loaded{i}") for i in range(n)], sem("summed"),
                                          sem("meaned"), sem("rooted"))
        scaled, turned, emptied, chain = sem("scaled"), sem("turned"), sem("emptied"), sem("chain")
        high, low, odd_low = sem("high"), sem("low"), sem("odd_low")
        scaled_rows = place(f"{tag}_scaled_rows", [P, 2, D], F32, kb)
        squares = place(f"{tag}_squares", [P, D], F32, kb + 16)
        stat = place(f"{tag}_stat", [P, 4, 8], F32, kb + 24)
        whole = place(f"{tag}_whole", [P, 4, 4, P], F32, kb + 25)
        banks = [ctx.enter_context(nc.psum_tensor(f"{tag}_bank{b}", [P, 4, P], F32)) for b in range(4)]
        block = ctx.enter_context(nc.Block())
        groups = DC // 4

        @block.sync
        def _(sp):
            if first_loads:
                first_loads(sp)
            for i, (rows, m, col, src) in enumerate(tiles):
                if src is not None:
                    sp.dma_start(rows, src).then_inc(loaded[i], 16)
            if more_loads:
                more_loads(sp)

        @block.scalar
        def _(act):
            act.wait_ge(chain, 1)
            for i, (rows, m, col, src) in enumerate(tiles):
                if src is not None:
                    act.wait_ge(loaded[i], 16)
                if i:
                    act.wait_ge(summed, i)
                act.activation(squares[0:m, :], rows, ACT.Square,
                               accum_out=stat[0:m, 0, i:i + 1]).then_inc(summed, 1)
            act.wait_ge(meaned, 1)
            act.activation(stat[:, 2, 0:n], stat[:, 1, 0:n], ACT.Sqrt).then_inc(rooted, 1)
            for i, (rows, m, col, src) in enumerate(tiles):
                if i == n - 1:
                    stream.split_first_high(act)
                for g in range(groups):
                    k = i * groups + g
                    act.wait_ge(emptied, k + 1)
                    act.copy(hi[:, 4 * g:4 * g + 4, col:col + m], whole[:, k % 4, :, 0:m])\
                        .then_inc(high, 1)

        def split_low(eng, k):
            rows, m, col, src = tiles[k // groups]
            g = k % groups
            eng.wait_ge(high, k + 1)
            return eng.tensor_tensor(lo[:, 4 * g:4 * g + 4, col:col + m], whole[:, k % 4, :, 0:m],
                                     hi[:, 4 * g:4 * g + 4, col:col + m].bitcast(F32), ALU.subtract)

        @block.gpsimd
        def _(pool):
            for k in range(0, n * groups, 2):
                if k == (n - 1) * groups:
                    stream.split_first_low(pool)
                split_low(pool, k).then_inc(low, 1)

        def empty(dve, i):
            rows, m, col, src = tiles[i]
            for g in range(groups):
                k = i * groups + g
                dve.wait_ge(turned, k + 1)
                if k >= 4:
                    dve.wait_ge(*((low, k // 2 - 1) if k % 2 == 0 else (odd_low, k // 2 - 1)))
                dve.tensor_tensor(whole[:, k % 4, :, 0:m], banks[k % 4][:, :, 0:m],
                                  gain[:, 4 * g:4 * g + 4].unsqueeze(2).to_broadcast([P, 4, m]),
                                  ALU.mult).then_inc(emptied, 1)
                if k % 2 and k >= 3:
                    split_low(dve, k - 2).then_inc(odd_low, 1)

        @block.vector
        def _(dve):
            link = Count(dve, chain).link
            link(dve.memset(stat[:, 0, :], 1.0))
            if consts:
                dve.wait_ge(*consts)
            dve.wait_ge(summed, n)
            dve.tensor_scalar(stat[:, 1, 0:n], stat[:, 0, 0:n], 1.0 / D, EPS,
                              ALU.mult, ALU.add).then_inc(meaned, 1)
            dve.wait_ge(rooted, 1)
            inverse_root(dve, link, stat[:, 3, 0:n], stat[:, 1, 0:n], stat[:, 2, 0:n], stat[:, 0, 0:n])
            for i, (rows, m, col, src) in enumerate(tiles):
                if i >= 2:
                    dve.wait_ge(turned, groups * (i - 1))
                dve.tensor_scalar(scaled_rows[0:m, i % 2, :], rows, stat[0:m, 3, i:i + 1], None,
                                  ALU.mult).then_inc(scaled, 1)
                if i == 0:
                    continue
                empty(dve, i - 1)
            empty(dve, n - 1)
            split_low(dve, n * groups - 1)
            if at_end:
                at_end(dve)

        @block.tensor
        def _(pe):
            if consts:
                pe.wait_ge(*consts)
            for i, (rows, m, col, src) in enumerate(tiles):
                pe.wait_ge(scaled, i + 1)
                for g in range(groups):
                    k = i * groups + g
                    if k >= 4:
                        pe.wait_ge(emptied, k - 3)
                    for j in range(4):
                        c = 4 * g + j
                        last = pe.transpose(banks[k % 4][:, j, 0:m],
                                            scaled_rows[0:m, i % 2, c * P:(c + 1) * P],
                                            ident[0:m, 0:m])
                    last.then_inc(turned, 1)



SPAN = 2
STEPS = DC // SPAN
QSPAN, QSTEPS = 2 * SPAN, STEPS // 2
RAW = 4


class Stream:

    def __init__(self, nc, tag, place, kb, src, span=SPAN):
        self.src, self.span, self.steps = src, span, DC // span
        cols = PC * SPAN // span
        self.raw = place(f"{tag}_raw", [P, RAW, span, cols], F32, kb)
        self.hi = place(f"{tag}_hi", [P, 2, span, cols], F32R, kb + 16)
        self.lo = place(f"{tag}_lo", [P, 2, span, cols], F32R, kb + 24)
        self.loaded = [nc.alloc_semaphore(f"{tag}_loaded{i}") for i in range(RAW)]
        self.high, self.low, self.used = (nc.alloc_semaphore(f"{tag}_{name}")
                                          for name in ("high", "low", "used"))

    def load(self, sp, p, g, ahead=False):
        if not ahead:
            sp.wait_ge(self.low, p * self.steps + (g - RAW + 1))
        sp.dma_start(self.raw[:, g % RAW], self.src[p, :, g * self.span:(g + 1) * self.span, :])\
            .then_inc(self.loaded[g % RAW], 16)

    def load_start(self, sp):
        for g in range(RAW):
            self.load(sp, 0, g, ahead=True)

    def load_rest(self, sp, pieces):
        for g in range(RAW, self.steps):
            self.load(sp, 0, g)
        with sp.Fori(1, pieces) as p:
            for g in range(self.steps):
                self.load(sp, p, g)

    def split_high(self, act, p, g):
        act.wait_ge(self.loaded[g % RAW], p * (16 * self.steps // RAW) + 16 * (g // RAW + 1))
        act.wait_ge(self.used, p * self.steps + (g + 1))
        act.copy(self.hi[:, g % 2], self.raw[:, g % RAW]).then_inc(self.high, 1)

    def split_first_high(self, act):
        for g in range(2):
            act.wait_ge(self.loaded[g], 16)
            act.copy(self.hi[:, g], self.raw[:, g]).then_inc(self.high, 1)

    def split_first_low(self, eng):
        for g in range(2):
            self.split_low(eng, 0, g)

    def split_low(self, eng, p, g):
        eng.wait_ge(self.high, p * self.steps + (g + 1))
        eng.tensor_tensor(self.lo[:, g % 2], self.raw[:, g % RAW], self.hi[:, g % 2].bitcast(F32),
                          ALU.subtract).then_inc(self.low, 1)

    def split_low_rest(self, eng, pieces):
        for g in range(2, self.steps):
            self.split_low(eng, 0, g)
        with eng.Fori(1, pieces) as p:
            for g in range(self.steps):
                self.split_low(eng, p, g)

    def start_free(self, pe):
        pe.sem_inc(self.used, 2)

    def await_step(self, pe, p, g):
        pe.wait_ge(self.low, p * self.steps + (g + 1))

    def release(self, ins):
        ins.then_inc(self.used, 1)

    def await_piece(self, eng, p):
        eng.wait_ge(self.used, p * self.steps + (self.steps + 2))

    def parts(self, g, c):
        return self.hi[:, g % 2, c], self.lo[:, g % 2, c]


def product(pe, out, left, right, first, last):
    pe.matmul(out, left[0], right[0], start=first, stop=False)
    pe.matmul(out, left[1], right[0], start=False, stop=False)
    return pe.matmul(out, left[0], right[1], start=False, stop=last)



META_PIECES, PLAIN_PIECES, TURNED_PIECES = 3, 4, 4
NAT_PIECES = META_PIECES + PLAIN_PIECES
PIECES = NAT_PIECES + TURNED_PIECES
ORDER = [2, 7, 8, 0, 1, 9, 10, 3, 4, 5, 6]
GATE_PIECE = PIECES - 2
META_LAG = GATE_PIECE - META_PIECES - 1
KV_PIECE, HI_PIECE, Q_PIECE, HG_PIECE = 0, 1, 3, 5


def project(nc, stream, hn, nat, nat_meta, meta_row, turned, ident):
    with ExitStack() as ctx:
        def sem(name):
            return ctx.enter_context(nc.semaphore(f"proj_{name}"))

        unit_done = sem("unit_done")
        even_free, odd_free, meta_free = sem("even_free"), sem("odd_free"), sem("meta_free")
        meta_turned, meta_kept, waited = sem("meta_turned"), sem("meta_kept"), sem("waited")
        banks = [ctx.enter_context(nc.psum_tensor(f"proj_bank{b}", [P, PC], F32)) for b in range(4)]
        meta_bank = ctx.enter_context(nc.psum_tensor("proj_meta", [P, PC], F32))
        turn_bank = ctx.enter_context(nc.psum_tensor("proj_turn", [P, 4, M], F32))
        block = ctx.enter_context(nc.Block())

        def halves(tokens, c):
            return [part[:, c, tokens] for part in hn]

        def tile(tb):
            return slice(M + tb * P, M + (tb + 1) * P)

        @block.sync
        def _(sp):
            stream.load_rest(sp, PIECES)

        @block.gpsimd
        def _(pool):
            stream.split_low_rest(pool, PIECES)

        @block.tensor
        def _(pe):
            stream.start_free(pe)

            def bank_wait(p, b):
                pe.wait_ge((even_free, odd_free)[b % 2], p * 2 + (b // 2 + 1))

            def meta_rows(p, c, w, emptied):
                if c == 0:
                    pe.wait_ge(meta_free, emptied)
                return product(pe, meta_bank[0:M, :], halves(slice(0, M), c), w,
                               c == 0, c == DC - 1)

            def turn_meta(p):
                pe.wait_ge(meta_free, p - META_LAG)
                pe.wait_ge(meta_kept, p - GATE_PIECE)
                pe.sem_inc(waited, 1)
                for cb in range(4):
                    last = pe.transpose(turn_bank[:, cb, :], meta_row[:, cb * P:(cb + 1) * P],
                                        ident[0:M, 0:M])
                last.then_inc(meta_turned, 1)

            def natural(p, with_meta):
                for g in range(STEPS):
                    stream.await_step(pe, p, g)
                    for s in range(SPAN):
                        c = g * SPAN + s
                        w = stream.parts(g, s)
                        for tb in range(TB):
                            if c == 0:
                                bank_wait(p, tb)
                            last = product(pe, banks[tb][:, :], halves(tile(tb), c), w,
                                           c == 0, c == DC - 1)
                            if c == DC - 1 and tb < TB - 1:
                                last.then_inc(unit_done, 1)
                        if with_meta:
                            last = meta_rows(p, c, w, p + 1)
                    stream.release(last)

            with pe.Fori(0, META_PIECES) as p:
                natural(p, True)
            with pe.Fori(META_PIECES, NAT_PIECES) as p:
                natural(p, False)

            def turned_piece(p, with_meta, turn_last):
                for g in range(STEPS):
                    stream.await_step(pe, p, g)
                    for s in range(SPAN):
                        c = g * SPAN + s
                        w = stream.parts(g, s)
                        for cb in range(4):
                            if c == 0:
                                bank_wait(p, cb)
                            last = product(pe, banks[cb][:, :],
                                           [part[:, cb * P:(cb + 1) * P] for part in w],
                                           halves(slice(M, L), c), c == 0, c == DC - 1)
                            if c == DC - 1 and cb < 3:
                                last.then_inc(unit_done, 1)
                        if with_meta:
                            last = meta_rows(p, c, w, p - META_LAG)
                    stream.release(last)
                    if g == 0 and turn_last:
                        turn_meta(p)

            with pe.Fori(NAT_PIECES, GATE_PIECE) as p:
                turned_piece(p, False, False)
            turned_piece(GATE_PIECE, True, False)
            turned_piece(GATE_PIECE + 1, True, True)
            turn_meta(PIECES)

        @block.vector
        def _(dve):
            dve.sem_inc(even_free, 2)
            with dve.Fori(0, NAT_PIECES) as p:
                for tb in (0, 2):
                    dve.wait_ge(unit_done, p * 3 + (tb + 1))
                    dve.tensor_copy(nat[:, p, tb, :], banks[tb][:, :]).then_inc(even_free, 1)
            with dve.Fori(NAT_PIECES, PIECES) as p:
                for cb in (0, 2):
                    dve.wait_ge(unit_done, p * 3 + (cb + 1))
                    dve.tensor_copy(turned[:, p * 4 + (cb - 4 * NAT_PIECES), M:L], banks[cb][:, :])\
                        .then_inc(even_free, 1)

        @block.scalar
        def _(act):
            act.sem_inc(odd_free, 2)
            act.sem_inc(meta_free, 1)
            act.sem_inc(meta_kept, 1)

            def await_bank(p, b):
                if b == 1:
                    act.wait_ge(unit_done, p * 3 + 2)
                else:
                    stream.await_piece(act, p)

            def empty_natural(p, with_meta):
                for tb in (1, 3):
                    await_bank(p, tb)
                    act.copy(nat[:, p, tb, :], banks[tb][:, :]).then_inc(odd_free, 1)
                if with_meta:
                    act.copy(nat_meta[:, p, :], meta_bank[0:M, :]).then_inc(meta_free, 1)

            def empty_turned(p, with_meta):
                for cb in (1, 3):
                    await_bank(p, cb)
                    act.copy(turned[:, p * 4 + (cb - 4 * NAT_PIECES), M:L], banks[cb][:, :])\
                        .then_inc(odd_free, 1)
                if with_meta:
                    act.copy(meta_row[:, :], meta_bank[0:M, :]).then_inc(meta_free, 1)

            def keep_meta(p):
                act.wait_ge(meta_turned, p - GATE_PIECE)
                act.copy(turned[:, pl(p * 4 - 4 * (NAT_PIECES + 1), 4), 0:M], turn_bank[:, :, :])\
                    .then_inc(meta_kept, 1)

            def splits(p, steps):
                for g in steps:
                    stream.split_high(act, p, g)

            splits(0, range(2, STEPS))
            splits(1, [0])
            empty_natural(0, True)
            for first, end, with_meta in ((1, META_PIECES, True), (META_PIECES, NAT_PIECES, False)):
                with act.Fori(first, end) as p:
                    splits(p, range(1, STEPS))
                    splits(p + 1, [0])
                    empty_natural(p, with_meta)
            with act.Fori(NAT_PIECES, GATE_PIECE) as p:
                splits(p, range(1, STEPS))
                splits(p + 1, [0])
                empty_turned(p, False)
            splits(GATE_PIECE, range(1, STEPS))
            splits(GATE_PIECE + 1, [0])
            empty_turned(GATE_PIECE, True)
            splits(PIECES - 1, [1, 2])
            keep_meta(PIECES - 1)
            splits(PIECES - 1, range(3, STEPS))
            empty_turned(PIECES - 1, True)
            keep_meta(PIECES)


def pl(start, count):
    return bass.ds(start, count)




def attend(nc, place, kb, nat, nat_meta, turned_cols, mix, cst, load_keep):
    pairs = GROUP * TB // 2
    qk = GROUP + 1
    with ExitStack() as ctx:
        def sem(name):
            return ctx.enter_context(nc.semaphore(f"att_{name}"))

        rows = place("att_rows", [P, KVH, TB, qk, HD], F32, kb)
        squares = place("att_squares", [P, TB, qk, HD], F32, kb + 20)
        qT = place("att_qT", [P, GROUP, T], F32, kb + 20)
        kT = place("att_kT", [P, L], F32, kb + 30)
        logits = place("att_logits", [P, 2, 2, KEYS], F32, kb + 32.25)
        probs = place("att_probs", [P, 2, 2, KEYS], F32, kb + 36.5)
        probsT = place("att_probsT", [P, 2, 2, BAND], F32, kb + 40.75)
        probsT_meta = place("att_probsT_meta", [M, 2, 2, P], F32, kb + 44.75)
        rows_meta = place("att_rows_meta", [M, KVH, 2, HD], F32, kb + 46.75)
        rot = place("att_rot", [P, KVH, 2, TB, qk, HALF], F32, kb + 48.75)
        rot_meta = place("att_rot_meta", [M, 2, HALF], F32, kb + 53.75)
        stat = place("att_stat", [P, KVH, 4, TB * qk + 1], F32, kb + 54)
        soft = place("att_soft", [P, 5, pairs, 2], F32, kb + 54.75)
        top, neg_top, den, sink_exp, inv = (soft[:, k] for k in range(5))
        sinks = place("att_sinks", [P, GROUP], F32, kb + 55.25)

        squared, meaned, rooted = sem("squared"), sem("meaned"), sem("rooted")
        chain, pool_chain, scales_ready = sem("chain"), sem("pool_chain"), sem("scales_ready")
        pool_rows, rows_ready = sem("pool_rows"), sem("rows_ready")
        turned, turned_out, key_out = sem("turned"), sem("turned_out"), sem("key_out")
        scores_done, scores_free, soft_ready = sem("scores_done"), sem("scores_free"), sem("soft_ready")
        exp_done, probs_turned, probs_out = sem("exp_done"), sem("probs_turned"), sem("probs_out")
        out_done, out_free = sem("out_done"), sem("out_free")
        opened, side, queries_done = sem("opened"), sem("side"), sem("queries_done")
        output_gates = nat[:, HG_PIECE:HG_PIECE + 2, :, :]
        query = turned_cols[:, 0:RH, M:L].rearrange("p (a b) t -> p a b t", b=2)
        spare = mix[:, :, QH * HD:]
        as_gates = spare.rearrange("p t (j c) -> p j t c", c=PC)
        as_query = spare.rearrange("p a (b t) -> p a b t", b=2)
        s_bank = [ctx.enter_context(nc.psum_tensor(f"att_s{b}", [P, 2, PC], F32)) for b in range(2)]
        t_bank = ctx.enter_context(nc.psum_tensor("att_t", [P, 2, PC], F32))
        o_bank = [ctx.enter_context(nc.psum_tensor(f"att_o{b}", [P, 2, HD], F32)) for b in range(2)]
        block = ctx.enter_context(nc.Block())

        def where(s):
            return s // 2, s % 2

        def normed_rows(eng, link, g):
            here = rows[:, g]
            rstd = stat[:, g, 3, 0:TB * qk].rearrange("p (t h) -> p t h", h=qk)
            for tb in range(TB):
                eng.tensor_tensor(here[:, tb, 0:GROUP, :],
                                  nat[:, Q_PIECE + g, tb, :].rearrange("p (h d) -> p h d", d=HD),
                                  rstd[:, tb, 0:GROUP].unsqueeze(2).to_broadcast([P, GROUP, HD]),
                                  ALU.mult)
            link(eng.tensor_tensor(here[:, :, GROUP, :], nat[:, KV_PIECE, :, g * HD:(g + 1) * HD],
                                   rstd[:, :, GROUP:qk].to_broadcast([P, TB, HD]), ALU.mult))
            link(eng.tensor_tensor(here, here, cst["qk_gain"][:, :, :].unsqueeze(1)
                                   .to_broadcast([P, TB, qk, HD]), ALU.mult))
            rotate(eng, link, here[:, :, :, 0:HALF], here[:, :, :, HALF:ROPE],
                   rot[:, g, 0], rot[:, g, 1],
                   cst["cos"][:, :, :].unsqueeze(2).to_broadcast([P, TB, qk, HALF]),
                   cst["sin"][:, :, :].unsqueeze(2).to_broadcast([P, TB, qk, HALF]))

        @block.sync
        def _(sp):
            load_keep(sp)

        @block.gpsimd
        def _(pool):
            link = Count(pool, pool_chain).link
            for g in range(KVH):
                pool.wait_ge(scales_ready, g + 1)
                if g:
                    normed_rows(pool, link, g)
                meta = rows_meta[:, g, 0, :]
                link(pool.tensor_tensor(meta, nat_meta[:, KV_PIECE, g * HD:(g + 1) * HD],
                                        stat[0:M, g, 3, TB * qk:].to_broadcast([M, HD]), ALU.mult))
                link(pool.tensor_tensor(meta, meta, cst["qk_gain"][0:M, GROUP, :], ALU.mult))
                rotate(pool, link, meta[:, 0:HALF], meta[:, HALF:ROPE], rot_meta[:, 0, :],
                       rot_meta[:, 1, :], cst["meta_cos"][:, :], cst["meta_sin"][:, :])
                pool.sem_inc(pool_rows, 1)
            step = Count(pool, side)
            pool.wait_ge(opened, 1)
            step.link(pool.tensor_tensor(output_gates, output_gates, as_gates, ALU.mult))
            for j in range(2):
                gain = cst["hgrn_gain"][:, j * PC:(j + 1) * PC].unsqueeze(1).to_broadcast([P, TB, PC])
                pool.tensor_tensor(output_gates[:, j], output_gates[:, j], gain, ALU.mult)
            pool.wait_ge(opened, 2)
            pool.tensor_tensor(query, query, as_query, ALU.mult).then_inc(queries_done, 1)

        @block.scalar
        def _(act):
            def root(g):
                act.wait_ge(meaned, g + 1)
                act.activation(stat[:, g, 2, :], stat[:, g, 1, :], ACT.Sqrt).then_inc(rooted, 1)

            for g in range(KVH):
                act.activation(squares[:, :, 0:GROUP, :],
                               nat[:, Q_PIECE + g, :, :].rearrange("p t (h d) -> p t h d", d=HD),
                               ACT.Square)
                act.activation(squares[:, :, GROUP, :], nat[:, KV_PIECE, :, g * HD:(g + 1) * HD],
                               ACT.Square)
                act.activation(rows_meta[:, g, 1, :], nat_meta[:, KV_PIECE, g * HD:(g + 1) * HD],
                               ACT.Square).then_inc(squared, 1)
                root(g)
            act.activation(as_gates, output_gates, ACT.Sigmoid).then_inc(opened, 1)
            for g in range(KVH):
                if g:
                    act.wait_ge(side, 1)
                    act.activation(as_query, query, ACT.Sigmoid).then_inc(opened, 1)
                for k in range(qk):
                    act.wait_ge(turned, g * qk + k + 1)
                    if k == 0:
                        act.wait_ge(out_done, g * pairs + 1)
                    if k < GROUP:
                        act.copy(qT[:, k, :], s_bank[k % 2][:, 0, :]).then_inc(turned_out, 1)
                    else:
                        act.copy(kT[:, M:L], s_bank[k % 2][:, 0, :]).then_inc(turned_out, 1)
                for s in range(pairs + 1):
                    if s < pairs:
                        act.wait_ge(soft_ready, g * pairs + s + 1)
                        if s >= 2:
                            act.wait_ge(probs_turned, g * pairs + s - 1)
                        h, a = where(s)
                        for u in range(2):
                            act.activation(probs[:, s % 2, u, :], logits[:, s % 2, u, :], ACT.Exp,
                                           bias=neg_top[:, s, u:u + 1],
                                           accum_out=den[:, s, u:u + 1])
                        act.activation(sink_exp[:, s, :], neg_top[:, s, :], ACT.Exp,
                                       bias=sinks[:, h:h + 1]).then_inc(exp_done, 1)
                    if s:
                        r = s - 1
                        act.wait_ge(probs_turned, g * pairs + r + 1)
                        if r >= 2:
                            act.wait_ge(out_done, g * pairs + r)
                        act.copy(probsT_meta[:, r % 2], t_bank[0:M, :, BAND:BAND + P])
                        act.copy(probsT[:, r % 2], t_bank[:, :, 0:BAND]).then_inc(probs_out, 1)

        @block.vector
        def _(dve):
            link = Count(dve, chain).link
            dve.sem_inc(scores_free, 2)
            dve.sem_inc(out_free, 2)
            link(dve.memset(stat[:, :, 0, :], 1.0))

            def scales(g):
                dve.wait_ge(squared, g + 1)
                link(dve.tensor_reduce(stat[:, g, 0, 0:TB * qk],
                                       squares[:, :, :, :].rearrange("p t h d -> p (t h) d"),
                                       AX.X, ALU.add))
                link(dve.tensor_reduce(stat[0:M, g, 0, TB * qk:], rows_meta[:, g, 1, :], AX.X, ALU.add))
                dve.tensor_scalar(stat[:, g, 1, :], stat[:, g, 0, :], 1.0 / HD, EPS,
                                  ALU.mult, ALU.add).then_inc(meaned, 1)
                dve.wait_ge(rooted, g + 1)
                inverse_root(dve, link, stat[:, g, 3, :], stat[:, g, 1, :], stat[:, g, 2, :],
                             stat[:, g, 0, :])
                dve.sem_inc(scales_ready, 1)

            scales(0)
            normed_rows(dve, link, 0)
            for g in range(KVH):
                dve.wait_ge(pool_rows, g + 1)
                dve.sem_inc(rows_ready, 1)
                if g == 0:
                    scales(1)
                dve.wait_ge(turned, g * qk + qk)
                dve.wait_ge(out_done, g * pairs + 1)
                link(dve.tensor_copy(sinks[:, :], cst["sinks"][:, pl(g * GROUP, GROUP)]))
                dve.tensor_copy(kT[:, 0:M], t_bank[:, 0, 0:M]).then_inc(key_out, 1)
                for s in range(pairs + 2):
                    if s < pairs:
                        h, a = where(s)
                        mask = cst["mask"][:, 1:2, :].to_broadcast([P, 2, KEYS]) if a \
                            else cst["mask"][:, :, :]
                        dve.wait_ge(scores_done, g * pairs + s + 1)
                        if s >= 2:
                            dve.wait_ge(exp_done, g * pairs + s - 1)
                        dve.scalar_tensor_tensor(logits[:, s % 2], s_bank[s % 2][:, :, 0:KEYS],
                                                 SCALE, mask, ALU.mult, ALU.add)\
                            .then_inc(scores_free, 1)
                        dve.wait_ge(scores_free, g * pairs + s + 3)
                        link(dve.tensor_reduce(top[:, s, :], logits[:, s % 2], AX.X, ALU.max))
                        dve.tensor_scalar(neg_top[:, s, :], top[:, s, :], sinks[:, h:h + 1],
                                          -1.0, ALU.max, ALU.mult).then_inc(soft_ready, 1)
                    if 1 <= s <= pairs:
                        r = s - 1
                        dve.wait_ge(exp_done, g * pairs + r + 1)
                        link(dve.tensor_tensor(inv[:, r, :], den[:, r, :], sink_exp[:, r, :],
                                               ALU.add))
                        link(dve.reciprocal(inv[:, r, :], inv[:, r, :]))
                    if s >= 2:
                        r = s - 2
                        h, a = where(r)
                        dve.wait_ge(out_done, g * pairs + r + 2)
                        dve.tensor_tensor(mix[:, 2 * a:2 * a + 2, pl(g * (GROUP * HD) + h * HD, HD)],
                                          o_bank[r % 2][:, :, :],
                                          inv[:, r, :].unsqueeze(2).to_broadcast([P, 2, HD]),
                                          ALU.mult).then_inc(out_free, 1)

        @block.tensor
        def _(pe):
            ident = cst["ident"]
            pe.sem_inc(out_done, 1)
            for g in range(KVH):
                pe.wait_ge(rows_ready, g + 1)
                for k in range(qk):
                    if k >= 2:
                        pe.wait_ge(turned_out, g * qk + k - 1)
                    for tb in range(TB):
                        last = pe.transpose(s_bank[k % 2][:, 0, tb * P:(tb + 1) * P],
                                            rows[:, g, tb, k, :], ident[:, :])
                    if k == GROUP:
                        last = pe.transpose(t_bank[:, 0, 0:M], rows_meta[:, g, 0, :],
                                            ident[0:M, 0:M])
                    last.then_inc(turned, 1)
                pe.wait_ge(turned_out, (g + 1) * qk)
                pe.wait_ge(key_out, g + 1)
                for s in range(pairs + 2):
                    if s < pairs:
                        h, a = where(s)
                        pe.wait_ge(scores_free, g * pairs + s + 1)
                        for u in range(2):
                            n = 2 * a + u
                            q = qT[:, h, n * P:(n + 1) * P]
                            prev = M + max(n - 1, 0) * P
                            if n == 1:
                                spans = [(0, 0, KEYS)]
                            elif n == 0:
                                spans = [(0, 0, M + P), (M + P, M, P)]
                            else:
                                spans = [(0, 0, M), (M, prev, BAND)]
                            for to, start, size in spans:
                                last = pe.matmul(s_bank[s % 2][:, u, to:to + size], q,
                                                 kT[:, start:start + size], start=True, stop=True)
                        last.then_inc(scores_done, 1)
                    if 1 <= s <= pairs:
                        r = s - 1
                        pe.wait_ge(exp_done, g * pairs + r + 1)
                        if r:
                            pe.wait_ge(probs_out, g * pairs + r)
                        for part in range(2):
                            for u in range(2):
                                at = M + part * P
                                pe.transpose(t_bank[:, u, part * P:(part + 1) * P],
                                             probs[:, r % 2, u, at:at + P], ident[:, :])
                        for u in range(2):
                            last = pe.transpose(t_bank[0:M, u, BAND:BAND + P],
                                                probs[:, r % 2, u, 0:M], ident[:, :])
                        last.then_inc(probs_turned, 1)
                    if s >= 2:
                        r = s - 2
                        h, a = where(r)
                        b = r % 2
                        pe.wait_ge(probs_out, g * pairs + r + 1)
                        pe.wait_ge(out_free, g * pairs + r + 1)
                        value = pl(g * HD + KVH * HD, HD)
                        for u in range(2):
                            n = 2 * a + u
                            pe.matmul(o_bank[b][:, u, :], probsT[:, b, u, P:BAND],
                                      nat[:, KV_PIECE, n, value], start=True, stop=False)
                            if n:
                                pe.matmul(o_bank[b][:, u, :], probsT[:, b, u, 0:P],
                                          nat[:, KV_PIECE, n - 1, value], start=False, stop=False)
                            last = pe.matmul(o_bank[b][:, u, :], probsT_meta[:, b, u, :],
                                             nat_meta[:, KV_PIECE, value], start=False, stop=True)
                        last.then_inc(out_done, 1)


def rotate(dve, link, x1, x2, a, b, cos, sin):
    dve.tensor_tensor(a, x1, sin, ALU.mult)
    link(dve.tensor_tensor(b, x2, sin, ALU.mult))
    dve.tensor_tensor(x1, x1, cos, ALU.mult)
    link(dve.tensor_tensor(x2, x2, cos, ALU.mult))
    dve.tensor_tensor(x1, x1, b, ALU.subtract)
    link(dve.tensor_tensor(x2, x2, a, ALU.add))




GRAM_BANKS = 3
HEAD_HALVES = slice(0, RH // 2), slice(RH // 2, RH)


def recur(nc, place, kb, nat, nat_meta, turned, mix, cst, stream):
    grams = LEVELS + 1
    with ExitStack() as ctx:
        def sem(name):
            return ctx.enter_context(nc.semaphore(f"rec_{name}"))

        def bank(name, shape):
            return ctx.enter_context(nc.psum_tensor(f"rec_{name}", shape, F32))

        keys = place("rec_keys", [P, RH, L], F32, kb)
        logs = place("rec_logs", [P, RH, L], F32, kb + 16.5)
        gaps = place("rec_gaps", [P, 2, T], F32, kb + 33)
        decays = place("rec_decays", [P, 2, T], F32, kb + 37)
        halves = place("rec_halves", [P, 2, T], F32, kb + 41)
        scores = place("rec_scores", [P, TB, P], F32, kb + 45)
        q_in = place("rec_q_in", [P, T], F32, kb + 47)
        k_out = place("rec_k_out", [P, L], F32, kb + 49)
        gap_out = place("rec_gap_out", [P, L], F32, kb + 51.5)
        k_now = place("rec_k_now", [P, T], F32, kb + 54)
        grown = place("rec_grown", [P, T], F32, kb + 56)
        k_outT = place("rec_k_outT", [P, TB, HD], F32, kb + 58)
        state = place("rec_state", [P, TB, HD], F32, kb + 60)
        lb = place("rec_lb", [P, 2, RH], F32, kb + 62)
        diff = place("rec_diff", [P, RH], F32, kb + 62.25)
        stat = place("rec_stat", [P, 4, TB, RH], F32, kb + 62.5)
        squares = place("rec_squares", [P, HD], F32, kb + 63)
        query, gate = turned[:, 0:RH, :], turned[:, RH:2 * RH, :]

        apart, bounded = sem("apart"), sem("bounded")
        opened, logged, bounds, summed = sem("opened"), sem("logged"), sem("bounds"), sem("summed")
        gap_ready, decay_ready, half_ready = sem("gap_ready"), sem("decay_ready"), sem("half_ready")
        gram_done, gram_out, copied = sem("gram_done"), sem("gram_out"), sem("k_now_copied")
        out_gap, edge_ready = sem("out_gap"), sem("edge_ready")
        in_out_ready, k_turned, k_turned_out = sem("in_out"), sem("k_turned"), sem("k_turned_out")
        update_done, state_ready = sem("update_done"), sem("state_ready")
        out_done, out_copied, mix_ready = sem("out_done"), sem("out_copied"), sem("mix_ready")
        squared, meaned, rooted = sem("squared"), sem("meaned"), sem("rooted")
        waited, pool_waited, keys_ready = sem("waited"), sem("pool_waited"), sem("keys_ready")
        g_bank = [bank(f"g{b}", [P, TB, P]) for b in range(GRAM_BANKS)]
        k_bank, u_bank = bank("k", [P, TB, P]), bank("u", [P, TB, HD])
        o_bank = bank("o", [P, TB, HD])
        block = ctx.enter_context(nc.Block())

        def value(h, c):
            return nat[:, h // 4 + HI_PIECE, c, pl((h % 4) * HD, HD)]

        def split(ap, l):
            return ap.rearrange("p (n s m) -> p n s m", s=2, m=P >> (l + 1))

        @block.sync
        def _(sp):
            sp.wait_ge(squared, TB * RH)
            stream.load_start(sp)


        @block.gpsimd
        def _(pool):
            pool.wait_ge(keys_ready, 1)
            pool.wait_ge(summed, 1)
            with pool.Fori(0, RH) as h:
                b_real = logs[:, h, M:L]

                def gap(l):
                    m = P >> (l + 1)
                    b, d = split(b_real, l), split(gaps[:, l % 2, :], l)
                    edge = b[:, :, 0, m - 1:m].to_broadcast([P, T // (2 * m), m])
                    if l >= 2:
                        pool.wait_ge(decay_ready, LEVELS * h + l)
                    elif l == 0:
                        pool.wait_ge(decay_ready, LEVELS * h + 1)
                    if l != 1:
                        pool.sem_inc(pool_waited, 1)
                    pool.tensor_tensor(d[:, :, 0, :], edge, b[:, :, 0, :], ALU.subtract)
                    pool.tensor_tensor(d[:, :, 1, :], b[:, :, 1, :], edge, ALU.subtract)\
                        .then_inc(gap_ready, 1)

                gap(0)
                gap(1)
                pool.wait_ge(gram_done, grams * h + 1)
                pool.tensor_copy(k_now[:, :], keys[:, h, M:L]).then_inc(copied, 1)
                for l in range(2, LEVELS):
                    gap(l)

        @block.scalar
        def _(act):
            for counter in (decay_ready, edge_ready, out_copied):
                act.sem_inc(counter, 1)
            act.wait_ge(apart, 1)
            act.activation(lb[:, 0, :], diff[:, :], ACT.Sigmoid)
            act.activation(lb[:, 1, :], diff[:, :], ACT.Sigmoid, scale=-1.0).then_inc(bounded, 1)
            for part in HEAD_HALVES:
                act.activation(logs[:, part], gate[:, part], ACT.Sigmoid).then_inc(opened, 1)
            for part in HEAD_HALVES:
                act.activation(keys[:, part], gate[:, part], ACT.Sigmoid, scale=-1.0)\
                    .then_inc(opened, 1)
            act.wait_ge(opened, 4)
            for i, part in enumerate(HEAD_HALVES):
                act.wait_ge(bounds, i + 1)
                act.activation(gate[:, part], logs[:, part], ACT.Ln).then_inc(logged, 1)
            act.wait_ge(summed, 1)

            def copy_out(h):
                act.wait_ge(out_done, h + 1)
                for tb in range(TB):
                    act.activation(squares[:, :], o_bank[:, tb, :], ACT.Square,
                                   accum_out=stat[:, 0, tb, pl(h - 1, 1)]).then_inc(squared, 1)
                    act.wait_ge(squared, (h - 1) * TB + (tb + 1))
                act.copy(mix[:, :, pl(h * HD + (QH - 1) * HD, HD)], o_bank[:, :, :])\
                    .then_inc(out_copied, 1)

            def head(h, first):
                if not first:
                    act.wait_ge(state_ready, TB * h)
                act.activation(grown[:, :], logs[:, h, M:L], ACT.Exp).then_inc(edge_ready, 1)
                act.wait_ge(out_gap, h + 1)
                act.wait_ge(edge_ready, 2 * h + 2)
                if not first:
                    act.wait_ge(k_turned, h)
                act.activation(k_out[:, :], gap_out[:, :], ACT.Exp).then_inc(edge_ready, 1)
                for l in range(LEVELS):
                    b = l % 2
                    act.wait_ge(gap_ready, LEVELS * h + l + 1)
                    if l >= 2:
                        act.wait_ge(half_ready, LEVELS * h + l - 1)
                    act.activation(decays[:, b, :], gaps[:, b, :], ACT.Exp)\
                        .then_inc(decay_ready, 1)
                    if l == 1:
                        if not first:
                            copy_out(h)
                        act.wait_ge(k_turned, h + 1)
                        act.copy(k_outT[:, 0:TB - 1, :], k_bank[:, 0:TB - 1, :])
                        act.copy(k_outT[0:M, TB - 1, :], k_bank[0:M, TB - 1, :])\
                            .then_inc(k_turned_out, 1)

            head(0, True)
            with act.Fori(1, RH) as h:
                head(h, False)
            copy_out(RH)
            act.wait_ge(meaned, 1)
            act.activation(stat[:, 2], stat[:, 1], ACT.Sqrt).then_inc(rooted, 1)

        @block.tensor
        def _(pe):
            ident = cst["ident"]
            pe.sem_inc(gram_done, 1)
            pe.sem_inc(out_done, 1)
            with pe.Fori(0, RH) as h:
                pe.wait_ge(copied, h + 1)
                pe.wait_ge(gram_out, grams * h + 1)
                for c in range(TB):
                    last = pe.matmul(g_bank[0][:, c, :], k_now[:, c * P:(c + 1) * P],
                                     query[:, h, pl(M + c * P, P)], start=True, stop=True)
                last.then_inc(gram_done, 1)
                for l in range(LEVELS):
                    b = (l + 1) % GRAM_BANKS
                    pe.wait_ge(half_ready, LEVELS * h + l + 1)
                    if l + 1 >= GRAM_BANKS:
                        pe.wait_ge(gram_out, grams * h + (l + 3 - GRAM_BANKS))
                    tile = halves[:, l % 2, :]
                    for c in range(TB):
                        part = tile[:, c * P:(c + 1) * P]
                        last = pe.matmul(g_bank[b][:, c, :], part, part, start=True, stop=True)
                    last.then_inc(gram_done, 1)
                    if l == 0:
                        pe.wait_ge(in_out_ready, 2 * h + 2)
                        for c in range(TB - 1):
                            pe.transpose(k_bank[:, c, :], k_out[:, M + c * P:M + (c + 1) * P], ident[:, :])
                        pe.transpose(k_bank[0:M, TB - 1, :], k_out[:, 0:M], ident[:, :])\
                            .then_inc(k_turned, 1)
                    if l == 2:
                        pe.wait_ge(k_turned_out, h + 1)
                        for c in range(TB - 1):
                            pe.matmul(u_bank[:, c, :], k_outT[:, c, :], value(h, c),
                                      start=True, stop=True)
                        pe.matmul(u_bank[:, TB - 1, :], k_outT[0:M, TB - 1, :],
                                  nat_meta[:, h // 4 + HI_PIECE, pl((h % 4) * HD, HD)],
                                  start=True, stop=True).then_inc(update_done, 1)
                pe.wait_ge(gram_out, grams * (h + 1) + 1)
                pe.wait_ge(state_ready, TB * (h + 1))
                pe.wait_ge(out_copied, h + 1)
                for c in range(TB):
                    pe.matmul(o_bank[:, c, :], scores[:, c, :], value(h, c), start=True, stop=False)
                    last = pe.matmul(o_bank[:, c, :], q_in[:, c * P:(c + 1) * P], state[:, c, :],
                                     start=False, stop=True)
                last.then_inc(out_done, 1)

        @block.vector
        def _(dve):
            dve.sem_inc(gram_out, 1)
            dve.tensor_tensor(diff[:, :], cst["lb_logits"][:, 0, :], cst["lb_logits"][:, 1, :],
                              ALU.subtract).then_inc(apart, 1)
            dve.wait_ge(bounded, 1)
            for i, part in enumerate(HEAD_HALVES):
                dve.wait_ge(opened, i + 1)
                for h in range(part.start, part.stop):
                    last = dve.tensor_scalar(logs[:, h, :], logs[:, h, :], lb[:, 1, h:h + 1],
                                             lb[:, 0, h:h + 1], ALU.mult, ALU.add)
                last.then_inc(bounds, 1)
            dve.wait_ge(opened, 4)
            for h in range(RH):
                last = dve.tensor_scalar(keys[:, h, :], keys[:, h, :], lb[:, 1, h:h + 1], None,
                                         ALU.mult)
            last.then_inc(keys_ready, 1)
            for i, part in enumerate(HEAD_HALVES):
                dve.wait_ge(logged, i + 1)
                for h in range(part.start, part.stop):
                    last = dve.tensor_tensor_scan(logs[:, h, :], cst["keep"][:, :], gate[:, h, :],
                                                  0.0, ALU.mult, ALU.add)
            last.then_inc(summed, 1)
            dve.wait_ge(summed, 1)
            with dve.Fori(0, RH) as h:
                b_real = logs[:, h, M:L]
                by_chunk = b_real.rearrange("p (c t) -> p c t", t=P)
                dve.wait_ge(edge_ready, 2 * h + 1)
                dve.tensor_tensor(gap_out[:, M:L].rearrange("p (c t) -> p c t", t=P),
                                  by_chunk[:, :, P - 1:P].to_broadcast([P, TB, P]), by_chunk,
                                  ALU.subtract)
                dve.tensor_tensor(gap_out[:, 0:M], logs[:, h, M - 1:M].to_broadcast([P, M]),
                                  logs[:, h, 0:M], ALU.subtract).then_inc(out_gap, 1)

                def half(l):
                    w, e = split(halves[:, l % 2, :], l), split(decays[:, l % 2, :], l)
                    dve.wait_ge(decay_ready, LEVELS * h + l + 2)
                    if l >= 2:
                        dve.wait_ge(gram_done, grams * h + l + 1)
                    dve.tensor_tensor(w[:, :, 0, :], e[:, :, 0, :],
                                      split(keys[:, h, M:L], l)[:, :, 0, :], ALU.mult)
                    dve.tensor_tensor(w[:, :, 1, :], e[:, :, 1, :],
                                      split(query[:, h, M:L], l)[:, :, 1, :], ALU.mult)\
                        .then_inc(half_ready, 1)

                def pick(l):
                    dve.wait_ge(gram_done, grams * h + l + 3)
                    dve.wait_ge(gram_out, grams * h + l + 2)
                    dve.sem_inc(waited, 1)
                    dve.copy_predicated(
                        scores[:, :, :],
                        cst["level_mask"][:, l, :].unsqueeze(1).to_broadcast([P, TB, P]),
                        g_bank[(l + 1) % GRAM_BANKS][:, :, :]).then_inc(gram_out, 1)

                half(0)
                dve.wait_ge(edge_ready, 2 * h + 2)
                dve.wait_ge(out_done, h + 1)
                dve.tensor_tensor(q_in[:, :], grown[:, :], query[:, h, M:L], ALU.mult)\
                    .then_inc(in_out_ready, 1)
                dve.wait_ge(edge_ready, 2 * h + 3)
                dve.tensor_tensor(k_out[:, :], k_out[:, :], keys[:, h, :], ALU.mult)\
                    .then_inc(in_out_ready, 1)
                half(1)
                dve.wait_ge(gram_done, grams * h + 2)
                dve.tensor_tensor(scores[:, :, :], g_bank[0][:, :, :],
                                  cst["ident"][:, :].unsqueeze(1).to_broadcast([P, TB, P]),
                                  ALU.mult).then_inc(gram_out, 1)
                for l in range(2, LEVELS):
                    half(l)
                    pick(l - 2)
                    if l == 4:
                        dve.wait_ge(update_done, h + 1)
                        dve.tensor_copy(state[:, 0, :], u_bank[:, TB - 1, :])\
                            .then_inc(state_ready, 1)
                        for c in range(TB - 1):
                            dve.wait_ge(state_ready, TB * h + c + 1)
                            dve.scalar_tensor_tensor(state[:, c + 1, :], state[:, c, :],
                                                     grown[:, (c + 1) * P - 1:(c + 1) * P],
                                                     u_bank[:, c, :], ALU.mult, ALU.add)\
                                .then_inc(state_ready, 1)
                pick(LEVELS - 2)
                pick(LEVELS - 1)
            outs = mix[:, :, QH * HD:].rearrange("p t (j h d) -> p t j h d", j=2, d=HD)
            gates = nat[:, HG_PIECE:HG_PIECE + 2, :, :].rearrange("p j t (h d) -> p j t h d", d=HD)
            dve.wait_ge(squared, TB * RH)
            dve.tensor_scalar(stat[:, 1], stat[:, 0], 1.0 / HD, EPS, ALU.mult, ALU.add)\
                .then_inc(meaned, 1)
            dve.wait_ge(rooted, 1)
            tail = Count(dve, mix_ready)
            inverse_root(dve, tail.link, stat[:, 3], stat[:, 1], stat[:, 2], stat[:, 0])
            dve.wait_ge(out_copied, RH + 1)
            for tb in range(TB):
                for h in range(RH):
                    head = outs[:, tb, h // 4, h % 4, :]
                    dve.scalar_tensor_tensor(head, head, stat[:, 3, tb, h:h + 1],
                                             gates[:, h // 4, tb, h % 4, :], ALU.mult, ALU.mult)



OUT_PIECES = D // PC


def mix_out(nc, stream, mix, mixT, h, x, cst):
    hi, lo = mixT
    with ExitStack() as ctx:
        def sem(name):
            return ctx.enter_context(nc.semaphore(f"out_{name}"))

        turned, high, low = sem("turned"), sem("high"), sem("low")
        x_loaded, unit_done, added = sem("x_loaded"), sem("unit_done"), sem("added")
        t_bank = [ctx.enter_context(nc.psum_tensor(f"out_t{b}", [P, TB, P], F32)) for b in range(4)]
        banks = [ctx.enter_context(nc.psum_tensor(f"out_bank{b}", [P, PC], F32)) for b in range(4)]
        block = ctx.enter_context(nc.Block())

        @block.sync
        def _(sp):
            sp.wait_ge(turned, DC)
            sp.dma_start(h[:, :, :], x.rearrange("(b p) d -> p b d", p=P)).then_inc(x_loaded, 16)
            stream.load_rest(sp, OUT_PIECES)

        @block.gpsimd
        def _(pool):
            stream.split_first_low(pool)
            stream.split_low_rest(pool, OUT_PIECES)

        @block.tensor
        def _(pe):
            stream.start_free(pe)
            for c in range(DC):
                if c >= 4:
                    pe.wait_ge(low, c - 3)
                for tb in range(TB):
                    last = pe.transpose(t_bank[c % 4][:, tb, :], mix[:, tb, c * P:(c + 1) * P],
                                        cst["ident"][:, :])
                last.then_inc(turned, 1)
            pe.wait_ge(low, DC)
            with pe.Fori(0, OUT_PIECES) as p:
                for g in range(STEPS):
                    stream.await_step(pe, p, g)
                    for s in range(SPAN):
                        c = g * SPAN + s
                        for tb in range(TB):
                            if c == 0:
                                pe.wait_ge(added, p * TB + (tb + 1))
                            tokens = slice(tb * P, (tb + 1) * P)
                            last = product(pe, banks[tb][:, :], (hi[:, c, tokens], lo[:, c, tokens]),
                                           stream.parts(g, s), c == 0, c == DC - 1)
                            if c == DC - 1 and tb < TB - 1:
                                last.then_inc(unit_done, 1)
                    stream.release(last)

        @block.scalar
        def _(act):
            stream.split_first_high(act)
            for c in range(DC):
                act.wait_ge(turned, c + 1)
                act.copy(hi[:, c, :], t_bank[c % 4][:, :, :].rearrange("p b t -> p (b t)"))\
                    .then_inc(high, 1)
            for g in range(2, STEPS):
                stream.split_high(act, 0, g)
            with act.Fori(1, OUT_PIECES) as p:
                for g in range(STEPS):
                    stream.split_high(act, p, g)

        @block.vector
        def _(dve):
            dve.sem_inc(added, TB)
            for c in range(DC):
                dve.wait_ge(high, c + 1)
                dve.tensor_tensor(lo[:, c, :], t_bank[c % 4][:, :, :].rearrange("p b t -> p (b t)"),
                                  hi[:, c, :].bitcast(F32), ALU.subtract).then_inc(low, 1)
            dve.wait_ge(x_loaded, 16)
            with dve.Fori(0, OUT_PIECES) as p:
                for tb in range(TB):
                    if tb < TB - 1:
                        dve.wait_ge(unit_done, p * (TB - 1) + (tb + 1))
                    else:
                        stream.await_piece(dve, p)
                    cols = h[:, tb, pl(p * PC, PC)]
                    dve.tensor_tensor(cols, cols, banks[tb][:, :], ALU.add).then_inc(added, 1)



HC = 2 * PH
WIDE, NARROW = 4, 4
CANDS = WIDE * TOPK + (TOPK - WIDE) * NARROW
HEAD_LINKS = 4 + 1 + 4 + 5 + 1


def route(nc, place, kb, stream, xT, picks, cst):
    with ExitStack() as ctx:
        def sem(name):
            return ctx.enter_context(nc.semaphore(f"route_{name}"))

        qT = place("route_qT", [P, 2, T], F32, kb)
        sc = place("route_scores", [P, 4, TB, NK], F32, kb + 4)
        rest = place("route_rest", [P, 2, TB, NK], F32, kb + 12)
        cand = place("route_cand", [P, TB, CANDS], F32, kb + 16)
        cand_rest = place("route_cand_rest", [P, TB, CANDS], F32, kb + 18)
        hot = place("route_hot", [P, 2, 2, TB, TOPK, TOPK], F32, kb + 20)
        val = place("route_val", [P, 2, TB, TOPK], F32, kb + 36)
        idx = place("route_idx", [P, 2, TB, TOPK], U32, kb + 36.5)
        idx_f = place("route_idx_f", [P, 2, 2, TB, TOPK], F32, kb + 37)
        best = place("route_best", [P, TB, TOPK], F32, kb + 38)
        pos = place("route_pos", [P, 4, TB, TOPK], U32, kb + 38.25)
        place_f = place("route_place_f", [P, 4, TB, TOPK], F32, kb + 39.25)
        pos_f = place("route_pos_f", [P, 2, TB, TOPK], F32, kb + 40.25)
        total = place("route_total", [P, 2, TB, PH], F32, kb + 40.75)

        q_done, q_out, s_done, s_out = sem("q_done"), sem("q_out"), sem("s_done"), sem("s_out")
        chain, scores_used, shifted, exp_done = (sem("chain"), sem("scores_used"), sem("shifted"),
                                                 sem("exp_done"))
        places_met, hot_done, waited = sem("places_met"), sem("hot_done"), sem("waited")
        q_bank = [[ctx.enter_context(nc.psum_tensor(f"route_q{s}{k}", [P, T], F32))
                   for k in range(2)] for s in range(2)]
        s_bank = [[ctx.enter_context(nc.psum_tensor(f"route_s{s}{k}", [P, TB, NK], F32))
                   for k in range(2)] for s in range(2)]
        block = ctx.enter_context(nc.Block())

        def each_head(eng, head, peeled):
            for m in range(peeled):
                head(m, m % 2, True)
            with eng.Fori(peeled // 2, PH // 2) as i:
                for s in range(2):
                    head(i * 2 + s, s, False)

        @block.sync
        def _(sp):
            stream.load_rest(sp, PH)

        @block.gpsimd
        def _(pool):
            def weigh(m, s):
                pool.wait_ge(places_met, m - 1)
                for c in range(2):
                    last = pool.tensor_tensor(
                        hot[:, s, c], hot[:, s, c],
                        idx_f[:, s, c].unsqueeze(2).to_broadcast([P, TB, TOPK, TOPK]), ALU.mult)
                last.then_inc(hot_done, 1)

            def head(m, s, first):
                for g in range(QSTEPS):
                    if not (first and m == 0 and g < 2):
                        stream.split_low(pool, m, g)
                    if g == 1 and not first:
                        weigh(m, s)

            each_head(pool, head, 2)
            weigh(PH, 0)
            weigh(PH + 1, 1)

        @block.tensor
        def _(pe):
            stream.start_free(pe)

            def scores(m, s, wait_bank=True):
                for k in range(2):
                    pe.wait_ge(q_out, m * 2 + (k - 1))
                    if wait_bank:
                        pe.wait_ge(s_out, m * 2 + (k - 5))
                    for tb in range(TB):
                        last = pe.matmul(s_bank[s][k][:, tb, :], qT[:, k, tb * P:(tb + 1) * P],
                                         cst["sub_keys"][:, m * 2 + (k - 2), :],
                                         start=True, stop=True)
                    last.then_inc(s_done, 1)

            def head(m, s, first):
                for g in range(QSTEPS):
                    stream.await_step(pe, m, g)
                    for at in range(QSPAN):
                        c = g * QSPAN + at
                        for k in range(2):
                            if c == 0 and not (first and m < 2):
                                pe.wait_ge(q_out, m * 2 + (k - 3))
                            w = [part[:, k * P:(k + 1) * P] for part in stream.parts(g, at)]
                            last = product(pe, q_bank[s][k][:, :], w, [x[:, c, :] for x in xT],
                                           c == 0, c == DC - 1)
                            if c == DC - 1 and k == 0:
                                last.then_inc(q_done, 1)
                    stream.release(last)
                    if g == 0 and not (first and m == 0):
                        scores(m, 1 - s, not (first and m < 3))

            each_head(pe, head, 4)
            scores(PH, 1)

        @block.scalar
        def _(act):
            def empty_scores(m, s, wait_place=True):
                for k in range(2):
                    act.wait_ge(s_done, m * 2 + (k - 1))
                    if wait_place and k == 0:
                        act.wait_ge(scores_used, m - 2)
                    act.copy(sc[:, 2 * s + k], s_bank[s][k][:, :, :]).then_inc(s_out, 1)

            def head(m, s, first, last=False):
                if not (first and m == 0):
                    stream.split_high(act, m, 1)
                stream.split_high(act, m, 2)
                if not (first and m == 0):
                    empty_scores(m, 1 - s, not (first and m < 3))
                stream.split_high(act, m, 3)
                if not last:
                    stream.split_high(act, m + 1, 0)
                act.wait_ge(q_done, m + 1)
                if not (first and m == 0):
                    act.wait_ge(s_done, m * 2)
                act.copy(qT[:, 0, :], q_bank[s][0][:, :]).then_inc(q_out, 1)
                stream.await_piece(act, m)
                act.copy(qT[:, 1, :], q_bank[s][1][:, :]).then_inc(q_out, 1)

            for m in range(4):
                head(m, m % 2, True)
            with act.Fori(2, PH // 2 - 1) as i:
                for s in range(2):
                    head(i * 2 + s, s, False)
            head(PH - 2, 0, False)
            head(PH - 1, 1, False, True)
            empty_scores(PH, 1)
            act.wait_ge(shifted, 1)
            act.activation(picks[2][:, :, :], picks[2][:, :, :], ACT.Exp).then_inc(exp_done, 1)

        @block.vector
        def _(dve):
            count = Count(dve, chain)
            link = count.link

            def take_wait():
                dve.sem_inc(waited, 1)

            def top16(rows, rests, values, places):
                take_wait()
                for part in range(2):
                    cols = slice(8 * part, 8 * part + 8)
                    src = rows if part == 0 else rests
                    for r, v in zip(src, values):
                        last = dve.max(out=v[:, cols], in_=r)
                    link(last)
                    take_wait()
                    for r, v, p in zip(src, values, places):
                        last = dve.max_index(out=p[:, cols], in_max=v[:, cols], in_values=r)
                    if part == 0:
                        for r, t, v in zip(rows, rests, values):
                            last = dve.match_replace(out=t, in_to_replace=v[:, cols],
                                                     in_values=r, imm_value=-3.0e38)
                    link(last)
                    take_wait()

            def keep(m, s):
                dve.wait_ge(hot_done, m)
                for c in range(2):
                    last = dve.tensor_reduce(picks[c][:, :, pl(m * TOPK - TOPK, TOPK)], hot[:, s, c],
                                             AX.X, ALU.add)
                link(last)

            def head(m, s, first):
                dve.wait_ge(s_out, m * 2 + 2)
                both = [(c, tb) for c in range(2) for tb in range(TB)]
                top16([sc[:, 2 * s + c, tb, :] for c, tb in both],
                      [rest[:, c, tb, :] for c, tb in both],
                      [val[:, c, tb, :] for c, tb in both], [idx[:, c, tb, :] for c, tb in both])
                dve.sem_inc(scores_used, 1)
                dve.tensor_copy(idx_f[:, s], idx[:, :, :, :])
                for ranks, width, at in ((slice(0, WIDE), TOPK, 0),
                                         (slice(WIDE, TOPK), NARROW, WIDE * TOPK)):
                    rows = ranks.stop - ranks.start
                    last = dve.tensor_tensor(
                        cand[:, :, at:at + rows * width].rearrange("p b (i j) -> p b i j", j=width),
                        val[:, 0, :, ranks].unsqueeze(3).to_broadcast([P, TB, rows, width]),
                        val[:, 1, :, 0:width].unsqueeze(2).to_broadcast([P, TB, rows, width]),
                        ALU.add)
                link(last)
                tiles = range(TB)
                top16([cand[:, b, :] for b in tiles], [cand_rest[:, b, :] for b in tiles],
                      [best[:, b, :] for b in tiles], [pos[:, 0, b, :] for b in tiles])
                dve.tensor_copy(picks[2][:, :, pl(m * TOPK, TOPK)], best[:, :, :])
                dve.tensor_scalar(pos[:, 1], pos[:, 0], 4, None, ALU.logical_shift_right)
                dve.tensor_scalar(pos[:, 2], pos[:, 0], 2, None, ALU.logical_shift_right)
                dve.tensor_scalar(pos[:, 3], pos[:, 0], NARROW - 1, None, ALU.bitwise_and)
                link(dve.tensor_scalar(pos[:, 0], pos[:, 0], TOPK - NARROW, None, ALU.bitwise_and))
                link(dve.tensor_copy(place_f[:, :, :, :], pos[:, :, :, :]))
                link(dve.scalar_tensor_tensor(pos_f[:, 0], place_f[:, 2], -(WIDE * TOPK // NARROW - WIDE),
                                              place_f[:, 1], ALU.add, ALU.max))
                link(dve.scalar_tensor_tensor(pos_f[:, 1], pos_f[:, 0], WIDE - 0.5, place_f[:, 0],
                                              ALU.is_lt, ALU.mult))
                link(dve.tensor_tensor(pos_f[:, 1], pos_f[:, 1], place_f[:, 3], ALU.add))
                if not (first and m == 0):
                    keep(m, 1 - s)
                for c in range(2):
                    last = dve.tensor_tensor(
                        hot[:, s, c].rearrange("p b n r -> p (b n) r"),
                        pos_f[:, c].rearrange("p b n -> p (b n)").unsqueeze(2)
                        .to_broadcast([P, TB * TOPK, TOPK]),
                        cst["iota"][:, 0:TOPK].unsqueeze(1).to_broadcast([P, TB * TOPK, TOPK]),
                        ALU.is_equal)
                last.then_inc(places_met, 1)

            head(0, 0, True)
            head(1, 1, True)
            with dve.Fori(1, PH // 2) as i:
                count.enter(i - 1, 2 * HEAD_LINKS)
                for s in range(2):
                    head(i * 2 + s, s, False)
                count.leave(PH // 2 - 1)

            gates = picks[2][:, :, :].rearrange("p b (h n) -> p b h n", n=TOPK)
            tops = total[:, 0]
            link(dve.tensor_copy(tops, gates[:, :, :, 0]))
            dve.tensor_tensor(gates, gates, tops.unsqueeze(3).to_broadcast([P, TB, PH, TOPK]),
                              ALU.subtract).then_inc(shifted, 1)
            keep(PH, 1)
            dve.wait_ge(exp_done, 1)
            link(dve.tensor_reduce(total[:, 1], gates, AX.X, ALU.add))
            link(dve.reciprocal(total[:, 1], total[:, 1]))
            dve.tensor_tensor(gates, gates, total[:, 1].unsqueeze(3)
                              .to_broadcast([P, TB, PH, TOPK]), ALU.mult)



SLOTS, SLOT_TOKENS = 4, 4
TABLE_TOKENS = 64
PARTS = T // TABLE_TOKENS


def gate_table(nc, stages, stored, hot, picks, picksT, table, cst, at_turned):
    run = SLOTS * SLOT_TOKENS
    slots_of_part = TABLE_TOKENS // SLOT_TOKENS
    with ExitStack() as ctx:
        def sem(name):
            return ctx.enter_context(nc.semaphore(f"table_{name}"))

        turned, turned_out = sem("turned"), sem("turned_out")
        hot_ready, gated = sem("hot_ready"), sem("gated")
        banks_done, banks_out, waited = sem("banks_done"), sem("banks_out"), sem("waited")
        t_bank = [ctx.enter_context(nc.psum_tensor(f"table_t{b}", [P, TB, P], F32)) for b in range(3)]
        banks = [ctx.enter_context(nc.psum_tensor(f"table_b{b}", [P, SLOT_TOKENS, NK], F32))
                 for b in range(SLOTS)]
        block = ctx.enter_context(nc.Block())

        def gates(t):
            return picksT[:, 2, pl(t, SLOT_TOKENS)].unsqueeze(2).to_broadcast([P, SLOT_TOKENS, NK])

        @block.sync
        def _(sp):
            sp.wait_ge(turned, 3)
            at_turned(sp)
            with sp.Fori(0, PARTS // 2) as q:
                for s in range(2):
                    sp.wait_ge(banks_out, q * (2 * slots_of_part) + (slots_of_part * (s + 1) + SLOTS))
                    sp.dma_start(table[q * 2 + s], stages[s][:]).then_inc(stored[s], 16)

        @block.tensor
        def _(pe):
            pe.sem_inc(banks_done, SLOTS)
            for k in range(3):
                for tb in range(TB):
                    last = pe.transpose(t_bank[k][:, tb, :], picks[k][:, tb, :], cst["ident"][:, :])
                last.then_inc(turned, 1)
            with pe.Fori(0, T // run) as i:
                for s in range(SLOTS):
                    pe.wait_ge(gated, i * SLOTS + (s + 1))
                    pe.wait_ge(banks_out, i * SLOTS + (s + 1))
                    for j in range(SLOT_TOKENS):
                        last = pe.matmul(banks[s][:, j, :], hot[:, s, 1, j, :], hot[:, s, 0, j, :],
                                         start=True, stop=True)
                    last.then_inc(banks_done, 1)

        @block.gpsimd
        def _(pool):
            pool.wait_ge(turned_out, 3)
            with pool.Fori(0, T // run) as i:
                for s in range(SLOTS):
                    pool.wait_ge(hot_ready, i * SLOTS + (s + 1))
                    pool.sem_inc(waited, 1)
                    pool.tensor_tensor(hot[:, s, 1], hot[:, s, 1], gates(i * run + s * SLOT_TOKENS),
                                       ALU.mult).then_inc(gated, 1)

        @block.vector
        def _(dve):
            for k in range(3):
                dve.wait_ge(turned, k + 1)
                dve.tensor_copy(picksT[:, k, :], t_bank[k][:, :, :].rearrange("p b t -> p (b t)"))\
                    .then_inc(turned_out, 1)
            dve.wait_ge(turned_out, 3)
            with dve.Fori(0, T // run) as i:
                for s in range(SLOTS):
                    dve.wait_ge(banks_done, i * SLOTS + (s + 1))
                    dve.tensor_tensor(hot[:, s],
                                      cst["iota"][:, :].unsqueeze(1).unsqueeze(1)
                                      .to_broadcast([P, 2, SLOT_TOKENS, NK]),
                                      picksT[:, 0:2, pl(i * run + s * SLOT_TOKENS, SLOT_TOKENS)]
                                      .unsqueeze(3).to_broadcast([P, 2, SLOT_TOKENS, NK]),
                                      ALU.is_equal).then_inc(hot_ready, 1)

        @block.scalar
        def _(act):
            act.sem_inc(banks_out, SLOTS)
            for q in range(PARTS):
                if q >= 2:
                    act.wait_ge(stored[q % 2], 16 * (q // 2))
                with act.Fori(0, TABLE_TOKENS // run) as i:
                    for s in range(SLOTS):
                        act.wait_ge(banks_done, i * SLOTS + (slots_of_part * q + s + SLOTS + 1))
                        act.copy(stages[q % 2][:, :, pl(i * run + s * SLOT_TOKENS, SLOT_TOKENS)],
                                 banks[s][:, :, :].rearrange("p t i -> p i t"))\
                            .then_inc(banks_out, 1)



GROUPS = NK // 2
HALF_D = D // 2


def experts(nc, place, h, xT, u, v, raw, loaded, load_raw, table, table_stored, out):
    xh, xl = xT
    with ExitStack() as ctx:
        def sem(name):
            return ctx.enter_context(nc.semaphore(f"exp_{name}"))

        uh = place("exp_uh", [P, 2, DC, P], F32R, 32)
        ul = place("exp_ul", [P, 2, DC, P], F32R, 48)
        vh = place("exp_vh", [P, 2, D], F32R, 128)
        vl = place("exp_vl", [P, 2, D], F32R, 144)
        ah = place("exp_ah", [P, 2, 2, T], F32R, 160)
        al = place("exp_al", [P, 2, 2, T], F32R, 168)
        gates = place("exp_gates", [P, 2, T], F32, 192)
        act_f = place("exp_act", [P, 2, T], F32, 196)

        gates_in = [sem(f"gates_in{b}") for b in range(2)]
        high, low = sem("high"), sem("low")
        a_done, gelu_done, weighted, a_high, a_split = (sem("a_done"), sem("gelu_done"),
                                                        sem("weighted"), sem("a_high"), sem("a_split"))
        o_done, o_out, stored = sem("o_done"), sem("o_out"), sem("stored")
        a_bank = [ctx.enter_context(nc.psum_tensor(f"exp_a{b}", [P, T], F32)) for b in range(2)]
        o_bank = [ctx.enter_context(nc.psum_tensor(f"exp_o{b}", [P, PC], F32)) for b in range(D // PC)]
        block = ctx.enter_context(nc.Block())
        units = TB * (D // PC)

        def wait(eng, s, value):
            if not isinstance(value, int) or value > 0:
                eng.wait_ge(s, value)

        def run(eng, phase):
            last = GROUPS - 1
            phase("u", 0, 0, 0, ("u", 1))
            with eng.Fori(0, GROUPS // 2 - 1) as i:
                phase("u", i * 2 + 1, 1, i * 4 + 1, ("v", i * 2))
                phase("v", i * 2, 0, i * 4 + 2, ("u", i * 2 + 2))
                phase("u", i * 2 + 2, 0, i * 4 + 3, ("v", i * 2 + 1))
                phase("v", i * 2 + 1, 1, i * 4 + 4, ("u", i * 2 + 3))
            phase("u", last, 1, 2 * last - 1, ("v", last - 1))
            phase("v", last - 1, 0, 2 * last, ("v", last))
            phase("v", last, 1, 2 * last + 1, None)

        @block.sync
        def _(sp):
            def u_phase(g, parity, k):
                if not isinstance(k, int) or k > 0:
                    for n in range(4):
                        wait(sp, low, 4 * (k - 1) + (n + 1))
                        load_raw(sp, u, g, n)
                for b in range(2):
                    wait(sp, weighted, 2 * g + (b - 1))
                    sp.dma_start(gates[:, b, :].rearrange("p (q t) -> p q t", q=PARTS),
                                 table[:, :, g * 2 + b, :].rearrange("q j t -> j q t"))\
                        .then_inc(gates_in[b], 16)

            def v_phase(g, parity, k):
                for n in range(4):
                    wait(sp, low, 4 * (k - 1) + (n + 1))
                    load_raw(sp, v, g, n)

            for s in table_stored:
                sp.wait_ge(s, 16 * PARTS // 2)
            run(sp, lambda kind, g, parity, k, after:
                (u_phase if kind == "u" else v_phase)(g, parity, k))
            sp.wait_ge(o_out, units * GROUPS + 4)
            sp.dma_start(out.rearrange("(b p) d -> p b d", p=P), h[:, :, :]).then_inc(stored, 16)
            sp.wait_ge(stored, 16)

        @block.tensor
        def _(pe):
            def u_phase(g, parity, k):
                for b in range(2):
                    wait(pe, gelu_done, g * 2 + (b - 1))
                    for c in range(DC):
                        if c % (DC // 2) == 0:
                            pe.wait_ge(low, 4 * k + (2 * b + c // (DC // 2) + 1))
                        pe.matmul(a_bank[b][:, :], uh[:, b, c, :], xh[:, c, :],
                                  start=(c == 0), stop=False)
                        pe.matmul(a_bank[b][:, :], uh[:, b, c, :], xl[:, c, :],
                                  start=False, stop=False)
                        last = pe.matmul(a_bank[b][:, :], ul[:, b, c, :], xh[:, c, :],
                                         start=False, stop=(c == DC - 1))
                    last.then_inc(a_done, 1)

            def v_phase(g, parity, k):
                pe.wait_ge(low, 4 * k + 4)
                pe.wait_ge(a_split, g * 2 + 2)
                for n in range(units):
                    tb, dc = n // 4, n % 4
                    tokens, cols = slice(tb * P, (tb + 1) * P), slice(dc * PC, (dc + 1) * PC)
                    pe.wait_ge(o_out, g * units + (n + 1))
                    for b in range(2):
                        pe.matmul(o_bank[dc][:, :], ah[:, parity, b, tokens], vh[:, b, cols],
                                  start=(b == 0), stop=False)
                        pe.matmul(o_bank[dc][:, :], ah[:, parity, b, tokens], vl[:, b, cols],
                                  start=False, stop=False)
                        last = pe.matmul(o_bank[dc][:, :], al[:, parity, b, tokens], vh[:, b, cols],
                                         start=False, stop=(b == 1))
                    last.then_inc(o_done, 1)

            pe.sem_inc(o_done, 1)
            run(pe, lambda kind, g, parity, k, after:
                (u_phase if kind == "u" else v_phase)(g, parity, k))

        @block.scalar
        def _(act):
            def split_high(kind, g, k, n):
                if n == 0:
                    if kind == "u":
                        wait(act, a_done, g * 2)
                    else:
                        act.wait_ge(o_done, g * units + 1)
                act.wait_ge(loaded[n], 16 * (k + 1))
                act.copy(part(uh if kind == "u" else vh, kind, n), raw[:, n, :]).then_inc(high, 1)

            def phase(kind, g, parity, k, after):
                late = after is None or kind == after[0]
                if kind == "u":
                    for b in range(2):
                        if not late:
                            split_high(*after, k + 1, 2 * b)
                            split_high(*after, k + 1, 2 * b + 1)
                        act.wait_ge(a_done, g * 2 + (b + 1))
                        wait(act, a_split, g * 2 + (b - 1))
                        act.activation(act_f[:, b, :], a_bank[b][:, :], ACT.Gelu_apprx_tanh)\
                            .then_inc(gelu_done, 1)
                if (late or kind == "v") and after is not None:
                    for n in range(4):
                        split_high(*after, k + 1, n)

            act.wait_ge(table_stored[0], 16 * PARTS // 2)
            for n in range(4):
                split_high("u", 0, 0, n)
            act.wait_ge(table_stored[1], 16 * PARTS // 2)
            run(act, phase)

        @block.vector
        def _(dve):
            dve.sem_inc(o_out, 4)
            def split_low(kind, g, k, n):
                dve.wait_ge(high, 4 * k + (n + 1))
                dve.tensor_tensor(part(ul if kind == "u" else vl, kind, n), raw[:, n, :],
                                  part(uh if kind == "u" else vh, kind, n).bitcast(F32), ALU.subtract)\
                    .then_inc(low, 1)

            def phase(kind, g, parity, k, after):
                late = after is None or kind == after[0]
                if kind == "u":
                    for b in range(2):
                        if not late:
                            split_low(*after, k + 1, 2 * b)
                            split_low(*after, k + 1, 2 * b + 1)
                        dve.wait_ge(gelu_done, g * 2 + (b + 1))
                        dve.wait_ge(gates_in[b], 16 * (g + 1))
                        dve.tensor_tensor(act_f[:, b, :], act_f[:, b, :], gates[:, b, :], ALU.mult)\
                            .then_inc(weighted, 1)
                        dve.wait_ge(weighted, g * 2 + (b + 1))
                        wait(dve, o_done, (g - 1) * units + 1)
                        dve.tensor_copy(ah[:, parity, b, :], act_f[:, b, :]).then_inc(a_high, 1)
                        dve.wait_ge(a_high, g * 2 + (b + 1))
                        dve.tensor_tensor(al[:, parity, b, :], act_f[:, b, :],
                                          ah[:, parity, b, :].bitcast(F32), ALU.subtract)\
                            .then_inc(a_split, 1)
                else:
                    for n in range(units):
                        tb, dc = n // 4, n % 4
                        dve.wait_ge(o_done, g * units + (n + 2))
                        sums = h[:, tb, dc * PC:(dc + 1) * PC]
                        dve.tensor_tensor(sums, sums, o_bank[dc][:, :], ALU.add).then_inc(o_out, 1)
                        if n % 4 == 2 and not late:
                            split_low(*after, k + 1, n // 4)
                if late and after is not None:
                    for n in range(4):
                        split_low(*after, k + 1, n)

            for n in range(4):
                split_low("u", 0, 0, n)
            run(dve, phase)


def part(tile, kind, n):
    b, half = n // 2, n % 2
    if kind == "u":
        return tile[:, b, half * (DC // 2):(half + 1) * (DC // 2), :].rearrange("p c e -> p (c e)")
    return tile[:, b, half * HALF_D:(half + 1) * HALF_D]




def shape_constants():
    pos = np.arange(L, dtype=np.float32)
    inv = (np.float32(500000.0) ** (-np.arange(0, ROPE, 2, dtype=np.float32) / np.float32(ROPE)))
    ang = pos[:, None] * inv.astype(np.float32)[None, :]
    cos, sin = np.cos(ang).astype(np.float32), np.sin(ang).astype(np.float32)
    row = np.arange(P)[:, None]
    col = np.arange(P)[None, :]
    prev = np.where(col > row, 0.0, NEG)
    own = np.where(col <= row, 0.0, NEG)
    meta = np.zeros((P, M))
    return {
        "iota": np.broadcast_to(np.arange(P, dtype=np.float32), (P, P)),
        "ident": np.eye(P, dtype=np.float32),
        "cos": cos[M:].reshape(TB, P, HALF).transpose(1, 0, 2),
        "sin": sin[M:].reshape(TB, P, HALF).transpose(1, 0, 2),
        "meta_cos": cos[:M],
        "meta_sin": sin[:M],
        "mask": np.stack([np.concatenate([meta, np.full((P, P), NEG), own], 1),
                          np.concatenate([meta, prev, own], 1)], 1).astype(np.float32),
        "keep": np.broadcast_to(((np.arange(L) % P != M) & (np.arange(L) > 0)).astype(np.float32), (P, L)),
        "level_mask": np.stack([(row // (P >> l) == col // (P >> l)) & (row % (P >> l) < (P >> (l + 1)))
                                & (col % (P >> l) >= (P >> (l + 1))) for l in range(LEVELS)],
                               1).astype(np.float32),
    }



def build(nc, a, out):
    place = Place(nc)
    h = place("h", [P, TB, D], F32, 0)
    mix = place("mix", [P, TB, D], F32, 0)
    hn = [place("hn_high", [P, DC, L], F32R, 0), place("hn_low", [P, DC, L], F32R, 33)]
    w_in = Stream(nc, "w_in", place, 66, a["w_in"])
    nat = place("nat", [P, NAT_PIECES, TB, PC], F32, 98)
    nat_meta = place("nat_meta", [M, META_PIECES, PC], F32, 154)
    turned = place("turned", [P, 2 * RH, L], F32, 160)
    mixT = [place("mixT_high", [P, DC, T], F32R, 66), place("mixT_low", [P, DC, T], F32R, 98)]
    w_out = Stream(nc, "w_out", place, 160, a["w_out"])
    x_rows = place("x_rows", [P, TB, D], F32, 98)
    meta_rows = place("meta_rows", [M, D], F32, 130)
    mask_wide = place("level_mask_wide", [P, LEVELS, P], F32, 176)
    xT = [place("x_high", [P, DC, T], F32R, 64), place("x_low", [P, DC, T], F32R, 96)]
    w_q = Stream(nc, "w_q", place, 32, a["w_q"], QSPAN)
    picks = [place(f"picks{k}", [P, TB, P], F32, 182 + 2 * k) for k in range(3)]
    picksT = place("picksT", [P, 3, T], F32, 200)
    stages = [place(f"table_stage{i}", [P, NK, TABLE_TOKENS], F32, kb) for i, kb in enumerate((32, 128))]
    hot = place("table_hot", [P, SLOTS, 2, SLOT_TOKENS, NK], F32, 160)
    raw = place("exp_raw", [P, 4, HALF_D], F32, 176)
    raw_in = [nc.alloc_semaphore(f"exp_raw_in{n}") for n in range(4)]
    sub_keys = place("sub_keys", [P, HC, NK], F32, 128)
    table = nc.dram_tensor("gate_table", [PARTS, NK, NK, TABLE_TOKENS], F32, kind="Internal").ap()

    cst, kb = {}, 193.0
    early, late = [], []
    for name, shape, dtype in CONSTANTS:
        cst[name] = place(f"c_{name}", shape, dtype, kb)
        kb += -(-int(np.prod(shape[1:])) * mybir.dt.size(dtype) // 4) * 4 / KB
        src = a[name].partition_broadcast(P) if name in ROWS else a[name]
        (early if name in ("ident", "ln_mix") else late).append((cst[name], src))
    late.append((mask_wide, a["level_mask"]))
    cst["level_mask"] = place("c_level_mask", [P, LEVELS, P], U8, kb)
    assert kb + LEVELS * P / KB < 207.8, kb
    meta_row = place("meta_row", [M, PC], F32, kb + 1)
    assert kb + 1 + PC / KB * 4 < 207.8, kb
    cst["sub_keys"] = sub_keys
    cst["keep"] = place("c_keep", [P, L], F32, 95.75)
    early_in, late_in = nc.alloc_semaphore("early_consts"), nc.alloc_semaphore("late_consts")
    keep_in = nc.alloc_semaphore("keep_in")
    keys_loaded = nc.alloc_semaphore("sub_keys_loaded")

    def load_early(sp):
        for dst, src in early:
            sp.dma_start(dst[:], src).then_inc(early_in, 16)

    def load_late(sp):
        w_in.load_start(sp)
        for dst, src in late:
            sp.dma_start(dst[:], src).then_inc(late_in, 16)

    def narrow_mask(dve):
        dve.wait_ge(late_in, 16 * len(late))
        dve.tensor_copy(cst["level_mask"][:], mask_wide[:])

    def load_keep(sp):
        sp.dma_start(cst["keep"][:], a["keep"].partition_broadcast(P)).then_inc(keep_in, 16)
        sp.wait_ge(keep_in, 16)

    def load_keys(sp):
        w_q.load_start(sp)
        sp.dma_start(sub_keys[:], a["sub_keys"]).then_inc(keys_loaded, 16)
        sp.wait_ge(keys_loaded, 16)

    rows = [(x_rows[:, tb, :], P, M + tb * P, a["x"][tb * P:(tb + 1) * P, :]) for tb in range(TB)]
    norm_rows(nc, "mixnorm", [(meta_rows[:, :], M, 0, a["meta"])] + rows, cst["ln_mix"], hn,
              cst["ident"], place, 138, load_early, load_late, (early_in, 16 * len(early)), narrow_mask,
              w_in)
    project(nc, w_in, hn, nat, nat_meta, meta_row, turned, cst["ident"])
    attend(nc, place, 33, nat, nat_meta, turned, mix, cst, load_keep)
    recur(nc, place, 32, nat, nat_meta, turned, mix, cst, w_out)
    mix_out(nc, w_out, mix, mixT, h, a["x"], cst)
    norm_rows(nc, "ffnnorm", [(h[:, tb, :], P, tb * P, None) for tb in range(TB)], cst["ln_ffn"],
              xT, cst["ident"], place, 144, None, load_keys, stream=w_q)
    route(nc, place, 136, w_q, xT, picks, cst)

    def load_raw(sp, weights, g, n):
        sp.dma_start(raw[:, n, :], weights[g * 2 + n // 2, :, (n % 2) * HALF_D:(n % 2 + 1) * HALF_D])\
            .then_inc(raw_in[n], 16)

    def load_first_experts(sp):
        for n in range(4):
            load_raw(sp, a["u"], 0, n)

    stored = [nc.alloc_semaphore(f"table_stored{i}") for i in range(2)]
    gate_table(nc, stages, stored, hot, picks, picksT, table, cst, load_first_experts)
    experts(nc, place, h, xT, a["u"], a["v"], raw, raw_in, load_raw, table, stored, out)


CONSTANTS = [
    ("ident", [P, P], F32), ("iota", [P, P], F32), ("ln_mix", [P, DC], F32), ("ln_ffn", [P, DC], F32),
    ("cos", [P, TB, HALF], F32), ("sin", [P, TB, HALF], F32),
    ("meta_cos", [M, HALF], F32), ("meta_sin", [M, HALF], F32),
    ("mask", [P, 2, KEYS], F32), ("qk_gain", [P, GROUP + 1, HD], F32),
    ("sinks", [P, QH], F32), 
    ("lb_logits", [P, 2, RH], F32), ("hgrn_gain", [P, RH * HD], F32),
]
ROWS = ("iota", "qk_gain", "sinks", "keep", "hgrn_gain")


def turn_rows(w, pieces, cols):
    return w.reshape(DC, P, pieces, cols).transpose(2, 1, 0, 3)


def kernel(**inputs):
    import concourse.bacc as bacc
    from concourse.bass_utils import run_bass_kernel_spmd

    i = {name: np.asarray(value) for name, value in inputs.items()}
    shapes = shape_constants()
    q_gain, k_gain = i["q_norm_g"][0], i["k_norm_g"][0]
    arrays = {
        **shapes,
        "iota": shapes["iota"][0],
        "keep": shapes["keep"][0],
        "x": i["x"][0],
        "meta": i["meta_tokens"],
        "ln_mix": i["ln_mix_g"][0].reshape(DC, P).T,
        "ln_ffn": i["ln_ffn_g"][0].reshape(DC, P).T,
        "qk_gain": np.stack([q_gain] * GROUP + [k_gain]),
        "sinks": i["attn_sinks"][0],
        "lb_logits": i["hgrn_lb_logits"].reshape(2, RH, P).transpose(2, 0, 1),
        "hgrn_gain": i["hgrn_norm_g"][0],
        "w_in": turn_rows(i["w_in"][0], PIECES, PC)[ORDER],
        "w_out": turn_rows(i["w_out"][0], OUT_PIECES, PC),
        "w_q": turn_rows(i["peer_w_q"][0], PH, 2 * P),
        "sub_keys": i["peer_sub_keys"][0].reshape(HC, NK, P).transpose(2, 0, 1),
        "u": i["peer_u"][0].reshape(NK, NK, DC, P).transpose(0, 3, 2, 1).reshape(NK, P, D),
        "v": i["peer_v"][0].reshape(NK, NK, D),
    }
    arrays = {f"in_{name}": np.ascontiguousarray(value) for name, value in arrays.items()}
    nc = bacc.Bacc("TRN2", target_bir_lowering=False, num_devices=1)
    aps = {name[3:]: nc.dram_tensor(name, value.shape, mybir.dt.from_np(value.dtype),
                                    kind="ExternalInput").ap() for name, value in arrays.items()}
    out = nc.dram_tensor("out_dram", [T, D], F32, kind="ExternalOutput").ap()
    build(nc, aps, out)
    result = run_bass_kernel_spmd(nc, [arrays], core_ids=[0])
    return result.results[0]["out_dram"].reshape(1, T, D)
```
